# Optimizing a Trainium2 kernel written in Bass

```python
import jax, jax.numpy as jnp
from jax import lax
import numpy as np
import math

D_MODEL = 1024
BATCH = 1
SEQ = 256
DEPTH = 2

D_MIX = D_MODEL
D_RG = D_MIX // 2
RG_BLOCKS = 8
RG_BLOCK_W = D_RG // RG_BLOCKS
CONV_W = 4
RG_C = 8.0
GLA_HEADS = 4
GLA_VD = D_MIX - D_RG
GLA_KD = GLA_VD // 2
GLA_DK = GLA_KD // GLA_HEADS
GLA_DV = GLA_VD // GLA_HEADS
GLA_RANK = 16
GLA_TAU = 16.0
GLA_CHUNK = 64
D_IN = 2 * D_RG + 2 * GLA_KD + 2 * GLA_VD + GLA_RANK
D_FF = 2816
N_EXPERTS = 8
TOP_K = 2
N_DENSE = (DEPTH + 1) // 2
N_MOE = DEPTH // 2
EPS = 1e-6


def rms_norm(x, g):
    x32 = x.astype(jnp.float32)
    y = x32 * lax.rsqrt(jnp.mean(jnp.square(x32), axis=-1, keepdims=True) + EPS)
    return (y * g.astype(jnp.float32)).astype(x.dtype)

def modulate(h, shift, scale):
    return h * (1.0 + scale) + shift

def causal_depthwise_conv(u, w, b):
    s = u.shape[1]
    up = jnp.pad(u, ((0, 0), (CONV_W - 1, 0), (0, 0)))
    out = b
    for tap in range(CONV_W):
        out = out + up[:, tap:tap + s] * w[tap]
    return out

def _linear_combine(c1, c2):
    a1, b1 = c1
    a2, b2 = c2
    return a1 * a2, a2 * b1 + b2

def rg_lru(u, wa, ba, wx, bx, lam):
    bsz, s, d = u.shape
    ub = u.reshape(bsz, s, RG_BLOCKS, RG_BLOCK_W)
    r = jax.nn.sigmoid((jnp.einsum('bsnd,nde->bsne', ub, wa).reshape(bsz, s, d) + ba).astype(jnp.float32))
    i = jax.nn.sigmoid((jnp.einsum('bsnd,nde->bsne', ub, wx).reshape(bsz, s, d) + bx).astype(jnp.float32))
    log_a = -RG_C * r * jax.nn.softplus(-lam.astype(jnp.float32))
    a = jnp.exp(log_a)
    mult = jnp.sqrt(-jnp.expm1(2.0 * log_a))
    first = (jnp.arange(s) == 0)[None, :, None]
    mult = jnp.where(first, 1.0, mult)
    b_term = mult * i * u.astype(jnp.float32)
    _, h = lax.associative_scan(_linear_combine, (a, b_term), axis=1)
    return h.astype(u.dtype)

def gla_chunked(q, k, v, log_f):
    out_dtype = v.dtype
    bsz, s, nh, dk = q.shape
    dv = v.shape[-1]
    n = s // GLA_CHUNK
    q = q.astype(jnp.float32) * (dk ** -0.5)
    k = k.astype(jnp.float32)
    v = v.astype(jnp.float32)
    q = q.reshape(bsz, n, GLA_CHUNK, nh, dk)
    k = k.reshape(bsz, n, GLA_CHUNK, nh, dk)
    v = v.reshape(bsz, n, GLA_CHUNK, nh, dv)
    b = jnp.cumsum(log_f.astype(jnp.float32).reshape(bsz, n, GLA_CHUNK, nh, dk), axis=2)
    b_last = b[:, :, -1]
    b_ref = b[:, :, GLA_CHUNK // 2 - 1:GLA_CHUNK // 2]
    q_loc = q * jnp.exp(b - b_ref)
    k_loc = k * jnp.exp(b_ref - b)
    scores = jnp.einsum('bnihd,bnjhd->bnhij', q_loc, k_loc)
    causal = jnp.tril(jnp.ones((GLA_CHUNK, GLA_CHUNK), dtype=bool))
    scores = jnp.where(causal, scores, 0.0)
    o_intra = jnp.einsum('bnhij,bnjhv->bnihv', scores, v)
    k_end = k * jnp.exp(b_last[:, :, None] - b)
    u_chunk = jnp.einsum('bnjhd,bnjhv->bnhdv', k_end, v)
    decay = jnp.exp(b_last)

    def step(state, inp):
        dec, upd = inp
        return dec[..., None] * state + upd, state

    init = jnp.zeros((bsz, nh, dk, dv), jnp.float32)
    _, states = lax.scan(step, init, (jnp.moveaxis(decay, 1, 0), jnp.moveaxis(u_chunk, 1, 0)))
    states = jnp.moveaxis(states, 0, 1)
    o_inter = jnp.einsum('bnihd,bnhdv->bnihv', q * jnp.exp(b), states)
    o = (o_intra + o_inter).reshape(bsz, s, nh, dv)
    return o.astype(out_dtype)

def gla_branch(q, k, v, g, f_low, wg2, bg, norm_g):
    bsz, s, _ = q.shape
    log_f = jax.nn.log_sigmoid((f_low @ wg2 + bg).astype(jnp.float32)) / GLA_TAU
    o = gla_chunked(q.reshape(bsz, s, GLA_HEADS, GLA_DK),
                    k.reshape(bsz, s, GLA_HEADS, GLA_DK),
                    v.reshape(bsz, s, GLA_HEADS, GLA_DV),
                    log_f.reshape(bsz, s, GLA_HEADS, GLA_DK))
    o = rms_norm(o, norm_g)
    return o.reshape(bsz, s, GLA_VD) * jax.nn.silu(g)

def hybrid_mixer(h, w_in, conv_w, conv_b, wa, ba, wx, bx, lam, wg2, bg, gla_g, w_out):
    z = h @ w_in
    splits = np.cumsum([D_RG, D_RG, GLA_KD, GLA_KD, GLA_VD, GLA_VD]).tolist()
    rg_x, rg_gate, q, k, v, g, f_low = jnp.split(z, splits, axis=-1)
    u = causal_depthwise_conv(rg_x, conv_w, conv_b)
    rg_out = rg_lru(u, wa, ba, wx, bx, lam) * jax.nn.gelu(rg_gate)
    gla_out = gla_branch(q, k, v, g, f_low, wg2, bg, gla_g)
    return jnp.concatenate([rg_out, gla_out], axis=-1) @ w_out

def swiglu(h, w1, w3, w2):
    return (jax.nn.silu(h @ w1) * (h @ w3)) @ w2

def moe_swiglu(h, router_w, w1, w3, w2):
    logits = (h @ router_w).astype(jnp.float32)
    top_v, top_i = lax.top_k(logits, TOP_K)
    probs = jax.nn.softmax(top_v, axis=-1)
    gates = jnp.sum(jax.nn.one_hot(top_i, N_EXPERTS, dtype=jnp.float32) * probs[..., None], axis=-2)
    gates = gates.astype(h.dtype)
    y = jnp.zeros_like(h)
    for e in range(N_EXPERTS):
        y = y + gates[..., e:e + 1] * swiglu(h, w1[e], w3[e], w2[e])
    return y

def first_inputs(seed: int = 0) -> dict:
    key = jax.random.key(seed)
    ks = jax.random.split(key, 32)

    def nrm(k, shape, scale):
        return scale * jax.random.normal(k, shape, jnp.float32)

    a0 = jax.random.uniform(ks[13], (DEPTH, D_RG), jnp.float32, 0.9, 0.999)
    a_root = a0 ** (1.0 / RG_C)
    rg_lambda = jnp.log(a_root) - jnp.log1p(-a_root)
    return {
        "x": nrm(ks[0], (BATCH, SEQ, D_MODEL), 1.0),
        "c": nrm(ks[1], (BATCH, D_MODEL), 1.0),
        "ada_w": nrm(ks[2], (DEPTH, D_MODEL, 6 * D_MODEL), 0.5 * D_MODEL ** -0.5),
        "ada_b": nrm(ks[3], (DEPTH, 6 * D_MODEL), 0.01),
        "norm_mix_g": 1.0 + nrm(ks[4], (DEPTH, D_MODEL), 0.05),
        "norm_ffn_g": 1.0 + nrm(ks[5], (DEPTH, D_MODEL), 0.05),
        "w_in": nrm(ks[6], (DEPTH, D_MODEL, D_IN), D_MODEL ** -0.5),
        "rg_conv_w": nrm(ks[7], (DEPTH, CONV_W, D_RG), CONV_W ** -0.5),
        "rg_conv_b": nrm(ks[8], (DEPTH, D_RG), 0.01),
        "rg_wa": nrm(ks[9], (DEPTH, RG_BLOCKS, RG_BLOCK_W, RG_BLOCK_W), RG_BLOCK_W ** -0.5),
        "rg_ba": nrm(ks[10], (DEPTH, D_RG), 0.01),
        "rg_wx": nrm(ks[11], (DEPTH, RG_BLOCKS, RG_BLOCK_W, RG_BLOCK_W), RG_BLOCK_W ** -0.5),
        "rg_bx": nrm(ks[12], (DEPTH, D_RG), 0.01),
        "rg_lambda": rg_lambda,
        "gla_wg2": nrm(ks[14], (DEPTH, GLA_RANK, GLA_KD), GLA_RANK ** -0.5),
        "gla_bg": nrm(ks[15], (DEPTH, GLA_KD), 0.1),
        "gla_norm_g": 1.0 + nrm(ks[16], (DEPTH, GLA_DV), 0.05),
        "w_out": nrm(ks[17], (DEPTH, D_MIX, D_MODEL), D_MIX ** -0.5),
        "ffn_w1": nrm(ks[18], (N_DENSE, D_MODEL, D_FF), D_MODEL ** -0.5),
        "ffn_w3": nrm(ks[19], (N_DENSE, D_MODEL, D_FF), D_MODEL ** -0.5),
        "ffn_w2": nrm(ks[20], (N_DENSE, D_FF, D_MODEL), D_FF ** -0.5),
        "router_w": nrm(ks[21], (N_MOE, D_MODEL, N_EXPERTS), D_MODEL ** -0.5),
        "moe_w1": nrm(ks[22], (N_MOE, N_EXPERTS, D_MODEL, D_FF), D_MODEL ** -0.5),
        "moe_w3": nrm(ks[23], (N_MOE, N_EXPERTS, D_MODEL, D_FF), D_MODEL ** -0.5),
        "moe_w2": nrm(ks[24], (N_MOE, N_EXPERTS, D_FF, D_MODEL), D_FF ** -0.5),
        "final_g": 1.0 + nrm(ks[25], (D_MODEL,), 0.05),
    }

def first_block(x, c, ada_w, ada_b, norm_mix_g, norm_ffn_g, w_in, rg_conv_w, rg_conv_b,
              rg_wa, rg_ba, rg_wx, rg_bx, rg_lambda, gla_wg2, gla_bg, gla_norm_g, w_out,
              ffn_w1, ffn_w3, ffn_w2, router_w, moe_w1, moe_w3, moe_w2, final_g):
    c_act = jax.nn.silu(c)
    for layer in range(DEPTH):
        mod = c_act @ ada_w[layer] + ada_b[layer]
        sh_m, sc_m, gt_m, sh_f, sc_f, gt_f = [m[:, None, :] for m in jnp.split(mod, 6, axis=-1)]
        h = modulate(rms_norm(x, norm_mix_g[layer]), sh_m, sc_m)
        mix = hybrid_mixer(h, w_in[layer], rg_conv_w[layer], rg_conv_b[layer],
                           rg_wa[layer], rg_ba[layer], rg_wx[layer], rg_bx[layer], rg_lambda[layer],
                           gla_wg2[layer], gla_bg[layer], gla_norm_g[layer], w_out[layer])
        x = x + gt_m * mix
        h = modulate(rms_norm(x, norm_ffn_g[layer]), sh_f, sc_f)
        j = layer // 2
        if layer % 2 == 0:
            f = swiglu(h, ffn_w1[j], ffn_w3[j], ffn_w2[j])
        else:
            f = moe_swiglu(h, router_w[j], moe_w1[j], moe_w3[j], moe_w2[j])
        x = x + gt_f * f
    return rms_norm(x, final_g)


DEPTH_2 = 1

GRID_W = 64
CTX_LEN = 256
HEAD_DIM = 64
A_HEADS = 4
R_HEADS = 4
R_DK = 64
R_DV = 128
A_QK = A_HEADS * 2 * HEAD_DIM
A_V = A_HEADS * 2 * HEAD_DIM
R_QK = R_HEADS * R_DK
R_V = R_HEADS * R_DV
D_IN_2 = 2 * A_QK + A_V + 2 * R_QK + 2 * R_V
D_MIX_2 = A_V + R_V
Q_BLOCK = 128
RET_CHUNK = 128
ROPE_BASE = 10000.0
N_EXPERTS_2 = 64
N_GROUPS = 8
TOPK_GROUPS = 4
TOP_K_2 = 8
D_EXPERT = D_MODEL // 4
D_SHARED = D_MODEL // 4
ROUTED_SCALE = 2.5
MOE_BLOCK = 128
NORM_EPS = 1e-6


def rmsnorm(x, g):
    xf = x.astype(jnp.float32)
    y = xf * lax.rsqrt(jnp.mean(xf * xf, axis=-1, keepdims=True) + NORM_EPS)
    return (y * g.astype(jnp.float32)).astype(x.dtype)

def modulate_2(h, shift, scale):
    return h * (1 + scale[:, None]) + shift[:, None]

def axial_rope_tables(n_tokens):
    n_rows = n_tokens // GRID_W
    rows = jnp.broadcast_to(jnp.arange(n_rows, dtype=jnp.float32)[:, None], (n_rows, GRID_W)).reshape(-1)
    cols = jnp.broadcast_to(jnp.arange(GRID_W, dtype=jnp.float32)[None, :], (n_rows, GRID_W)).reshape(-1)
    n_freq = HEAD_DIM // 4
    inv_freq = ROPE_BASE ** (-jnp.arange(n_freq, dtype=jnp.float32) / n_freq)
    ang = jnp.stack([rows[:, None] * inv_freq, cols[:, None] * inv_freq], axis=1)
    return jnp.cos(ang), jnp.sin(ang)

def apply_axial_rope(x, cos, sin):
    n_freq = HEAD_DIM // 4
    xr = x.reshape(x.shape[:-1] + (2, 2, n_freq)).astype(jnp.float32)
    shp = (cos.shape[0],) + (1,) * (x.ndim - 3) + (2, n_freq)
    c = cos.reshape(shp)
    s = sin.reshape(shp)
    x1, x2 = xr[..., 0, :], xr[..., 1, :]
    out = jnp.stack([x1 * c - x2 * s, x1 * s + x2 * c], axis=-2)
    return out.reshape(x.shape).astype(x.dtype)

def project_heads(h, w_in):
    bn, t, _ = h.shape
    p = h @ w_in
    sizes = (A_QK, A_QK, A_V, R_QK, R_QK, R_V, R_V)
    cuts = [sum(sizes[:i + 1]) for i in range(len(sizes) - 1)]
    dq, dk, dv, rq, rk, rv, rg = jnp.split(p, cuts, axis=-1)
    return (dq.reshape(bn, t, A_HEADS, 2, HEAD_DIM),
            dk.reshape(bn, t, A_HEADS, 2, HEAD_DIM),
            dv.reshape(bn, t, A_HEADS, 2 * HEAD_DIM),
            rq.reshape(bn, t, R_HEADS, R_DK),
            rk.reshape(bn, t, R_HEADS, R_DK),
            rv.reshape(bn, t, R_HEADS, R_DV),
            rg)

def diff_attend(q, k, v, lam):
    s = jnp.einsum('bqhmd,bkhmd->bhmqk', q, k).astype(jnp.float32)
    p = jax.nn.softmax(s, axis=-1)
    a = p[:, :, 0] - lam * p[:, :, 1]
    return jnp.einsum('bhqk,bkhe->bqhe', a.astype(v.dtype), v)

def retention_chunked(q, k, v, log_gamma, state0):
    b, t, h, dk = q.shape
    dv = v.shape[-1]
    n = t // RET_CHUNK
    f32 = jnp.float32
    qc = q.astype(f32).reshape(b, n, RET_CHUNK, h, dk)
    kc = k.astype(f32).reshape(b, n, RET_CHUNK, h, dk)
    vc = v.astype(f32).reshape(b, n, RET_CHUNK, h, dv)
    lg = log_gamma.astype(f32)
    pos = jnp.arange(RET_CHUNK, dtype=f32)
    rel = pos[:, None] - pos[None, :]
    decay = jnp.where(rel[None] >= 0, jnp.exp(jnp.maximum(rel, 0.0)[None] * lg[:, None, None]), 0.0)
    scores = jnp.einsum('bnihd,bnjhd->bnhij', qc, kc) * decay
    intra = jnp.einsum('bnhij,bnjhe->bnihe', scores, vc)
    k_dec = kc * jnp.exp((RET_CHUNK - 1 - pos)[:, None] * lg)[:, :, None]
    chunk_kv = jnp.einsum('bnjhd,bnjhe->nbhde', k_dec, vc)
    g_chunk = jnp.exp(RET_CHUNK * lg)[None, :, None, None]

    def step(s, kv_i):
        return g_chunk * s + kv_i, s

    state_final, state_prev = lax.scan(step, state0.astype(f32), chunk_kv)
    q_dec = qc * jnp.exp((pos + 1)[:, None] * lg)[:, :, None]
    cross = jnp.einsum('bnihd,nbhde->bnihe', q_dec, state_prev)
    out = (intra + cross).reshape(b, t, h, dv)
    return out.astype(v.dtype), state_final

def bidir_retention(q_c, k_c, v_c, q_x, k_x, v_x, logg_f, logg_b):
    b = q_x.shape[0]
    s0 = jnp.zeros((b, R_HEADS, R_DK, R_DV), jnp.float32)
    flip = lambda a: jnp.flip(a, axis=1)
    o_cf, s_cf = retention_chunked(q_c, k_c, v_c, logg_f, s0)
    o_xf, _ = retention_chunked(q_x, k_x, v_x, logg_f, s_cf)
    o_cb, s_cb = retention_chunked(flip(q_c), flip(k_c), flip(v_c), logg_b, s0)
    o_xb, _ = retention_chunked(flip(q_x), flip(k_x), flip(v_x), logg_b, s_cb)
    return o_cf + flip(o_cb), o_xf + flip(o_xb)

def mixer_merge(att, ret, gate, lam_init, dattn_norm_g, ret_norm_g, w_out):
    bn, t = att.shape[:2]
    a = (rmsnorm(att, dattn_norm_g) * (1 - lam_init)).reshape(bn, t, A_V)
    r = jax.nn.silu(gate) * rmsnorm(ret, ret_norm_g).reshape(bn, t, R_V)
    return jnp.concatenate([a, r], axis=-1) @ w_out

def moe_ffn(h, router_w, router_bias, w1, w3, w2, sw1, sw3, sw2):
    t, d = h.shape
    scores = jax.nn.sigmoid((h @ router_w).astype(jnp.float32))
    sel = scores + router_bias.astype(jnp.float32)
    grp = sel.reshape(t, N_GROUPS, N_EXPERTS_2 // N_GROUPS)
    grp_score = lax.top_k(grp, 2)[0].sum(-1)
    _, top_g = lax.top_k(grp_score, TOPK_GROUPS)
    gmask = jax.nn.one_hot(top_g, N_GROUPS, dtype=jnp.float32).sum(axis=1) > 0
    emask = jnp.repeat(gmask, N_EXPERTS_2 // N_GROUPS, axis=1)
    _, top_e = lax.top_k(jnp.where(emask, sel, -jnp.inf), TOP_K_2)
    wts = jnp.take_along_axis(scores, top_e, axis=1)
    wts = wts / jnp.sum(wts, axis=-1, keepdims=True) * ROUTED_SCALE
    n_assign = t * TOP_K_2
    e_flat = top_e.reshape(n_assign)
    t_flat = jnp.repeat(jnp.arange(t, dtype=jnp.int32), TOP_K_2)
    w_flat = wts.reshape(n_assign)
    order = jnp.argsort(e_flat)
    e_s, t_s, w_s = e_flat[order], t_flat[order], w_flat[order]
    counts = jax.ops.segment_sum(jnp.ones((n_assign,), jnp.int32), e_flat, num_segments=N_EXPERTS_2)
    padded = (counts + MOE_BLOCK - 1) // MOE_BLOCK * MOE_BLOCK
    pad_end = jnp.cumsum(padded)
    pad_start = pad_end - padded
    start = jnp.cumsum(counts) - counts
    dest = pad_start[e_s] + jnp.arange(n_assign, dtype=jnp.int32) - start[e_s]
    n_pad = -(-n_assign // MOE_BLOCK) * MOE_BLOCK + N_EXPERTS_2 * MOE_BLOCK
    n_blk = n_pad // MOE_BLOCK
    tok_buf = jnp.full((n_pad,), t, jnp.int32).at[dest].set(t_s)
    w_buf = jnp.zeros((n_pad,), jnp.float32).at[dest].set(w_s)
    blk_exp = jnp.clip(jnp.searchsorted(pad_end, jnp.arange(n_blk, dtype=jnp.int32) * MOE_BLOCK, side='right'),
                       0, N_EXPERTS_2 - 1).astype(jnp.int32)
    h_pad = jnp.concatenate([h, jnp.zeros((1, d), h.dtype)], axis=0)

    def body(acc, inp):
        tok, wt, e = inp
        xb = h_pad[tok]
        yb = (jax.nn.silu(xb @ w1[e]) * (xb @ w3[e])) @ w2[e]
        return acc.at[tok].add((yb * wt[:, None].astype(yb.dtype)).astype(acc.dtype)), None

    acc0 = jnp.zeros((t + 1, d), h.dtype)
    acc, _ = lax.scan(body, acc0, (tok_buf.reshape(n_blk, MOE_BLOCK), w_buf.reshape(n_blk, MOE_BLOCK), blk_exp))
    shared = (jax.nn.silu(h @ sw1) * (h @ sw3)) @ sw2
    return acc[:t] + shared

def hybrid_layer(x, xc, mod_x, mod_c, cos, sin, lam_init, update_ctx,
                 norm1_g, w_in, lambda_q1, lambda_k1, lambda_q2, lambda_k2, dattn_norm_g,
                 ret_decay_fwd, ret_decay_bwd, ret_norm_g, w_out,
                 norm2_g, router_w, router_bias, exp_w1, exp_w3, exp_w2,
                 shared_w1, shared_w3, shared_w2):
    b, s, d = x.shape
    sh1, sc1, g1, sh2, sc2, g2 = jnp.split(mod_x, 6, axis=-1)
    csh1, csc1, cg1, csh2, csc2, cg2 = jnp.split(mod_c, 6, axis=-1)

    hx = modulate_2(rmsnorm(x, norm1_g), sh1, sc1)
    hc = modulate_2(rmsnorm(xc, norm1_g), csh1, csc1)
    dq_x, dk_x, dv_x, rq_x, rk_x, rv_x, rg_x = project_heads(hx, w_in)
    dq_c, dk_c, dv_c, rq_c, rk_c, rv_c, rg_c = project_heads(hc, w_in)

    dq_x = apply_axial_rope(dq_x, cos, sin) * HEAD_DIM ** -0.5
    dk_x = apply_axial_rope(dk_x, cos, sin)
    rq_x = apply_axial_rope(rq_x, cos, sin)
    rk_x = apply_axial_rope(rk_x, cos, sin) * R_DK ** -0.5
    dq_c = dq_c * HEAD_DIM ** -0.5
    rk_c = rk_c * R_DK ** -0.5

    lam = (jnp.exp(jnp.sum(lambda_q1 * lambda_k1)) - jnp.exp(jnp.sum(lambda_q2 * lambda_k2))).astype(jnp.float32) + lam_init

    k_all = jnp.concatenate([dk_c, dk_x], axis=1)
    v_all = jnp.concatenate([dv_c, dv_x], axis=1)
    n_qblk = s // Q_BLOCK
    q_blocks = dq_x.reshape(b, n_qblk, Q_BLOCK, A_HEADS, 2, HEAD_DIM).swapaxes(0, 1)
    att_x = lax.map(lambda qb: diff_attend(qb, k_all, v_all, lam), q_blocks)
    att_x = att_x.swapaxes(0, 1).reshape(b, s, A_HEADS, 2 * HEAD_DIM)

    logg_f = jax.nn.log_sigmoid(ret_decay_fwd.astype(jnp.float32))
    logg_b = jax.nn.log_sigmoid(ret_decay_bwd.astype(jnp.float32))
    ret_c, ret_x = bidir_retention(rq_c, rk_c, rv_c, rq_x, rk_x, rv_x, logg_f, logg_b)

    y_x = mixer_merge(att_x, ret_x, rg_x, lam_init, dattn_norm_g, ret_norm_g, w_out)
    x = x + g1[:, None] * y_x
    h2 = modulate_2(rmsnorm(x, norm2_g), sh2, sc2)
    ffn_x = moe_ffn(h2.reshape(b * s, d), router_w, router_bias, exp_w1, exp_w3, exp_w2,
                    shared_w1, shared_w3, shared_w2).reshape(b, s, d)
    x = x + g2[:, None] * ffn_x

    if update_ctx:
        att_c = diff_attend(dq_c, dk_c, dv_c, lam)
        y_c = mixer_merge(att_c, ret_c, rg_c, lam_init, dattn_norm_g, ret_norm_g, w_out)
        xc = xc + cg1[:, None] * y_c
        bc, lc, _ = xc.shape
        h2c = modulate_2(rmsnorm(xc, norm2_g), csh2, csc2)
        ffn_c = moe_ffn(h2c.reshape(bc * lc, d), router_w, router_bias, exp_w1, exp_w3, exp_w2,
                        shared_w1, shared_w3, shared_w2).reshape(bc, lc, d)
        xc = xc + cg2[:, None] * ffn_c
    else:
        xc = None
    return x, xc

def second_inputs(seed: int = 0) -> dict:
    key = jax.random.key(seed)
    ks = jax.random.split(key, 32)
    f32 = jnp.float32

    def nrm(k, shape, scale):
        return jax.random.normal(k, shape, f32) * scale

    gamma0 = 1.0 - 2.0 ** (-5.0 - jnp.arange(R_HEADS, dtype=f32))
    logit0 = jnp.log(gamma0) - jnp.log1p(-gamma0)
    return {
        "x": nrm(ks[0], (BATCH, SEQ, D_MODEL), 1.0),
        "c": nrm(ks[1], (BATCH, D_MODEL), 1.0),
        "ctx": nrm(ks[2], (BATCH, CTX_LEN, D_MODEL), 1.0),
        "c_ctx": nrm(ks[3], (D_MODEL,), 1.0),
        "ada_w": nrm(ks[4], (DEPTH_2, D_MODEL, 6 * D_MODEL), 0.5 * D_MODEL ** -0.5),
        "ada_b": nrm(ks[5], (DEPTH_2, 6 * D_MODEL), 0.02),
        "norm1_g": 1.0 + nrm(ks[6], (DEPTH_2, D_MODEL), 0.05),
        "w_in": nrm(ks[7], (DEPTH_2, D_MODEL, D_IN_2), D_MODEL ** -0.5),
        "lambda_q1": nrm(ks[8], (DEPTH_2, HEAD_DIM), 0.1),
        "lambda_k1": nrm(ks[9], (DEPTH_2, HEAD_DIM), 0.1),
        "lambda_q2": nrm(ks[10], (DEPTH_2, HEAD_DIM), 0.1),
        "lambda_k2": nrm(ks[11], (DEPTH_2, HEAD_DIM), 0.1),
        "dattn_norm_g": 1.0 + nrm(ks[12], (DEPTH_2, 2 * HEAD_DIM), 0.05),
        "ret_decay_fwd": logit0[None] + nrm(ks[13], (DEPTH_2, R_HEADS), 0.1),
        "ret_decay_bwd": logit0[None] + nrm(ks[14], (DEPTH_2, R_HEADS), 0.1),
        "ret_norm_g": 1.0 + nrm(ks[15], (DEPTH_2, R_DV), 0.05),
        "w_out": nrm(ks[16], (DEPTH_2, D_MIX_2, D_MODEL), D_MIX_2 ** -0.5),
        "norm2_g": 1.0 + nrm(ks[17], (DEPTH_2, D_MODEL), 0.05),
        "router_w": nrm(ks[18], (DEPTH_2, D_MODEL, N_EXPERTS_2), D_MODEL ** -0.5),
        "router_bias": nrm(ks[19], (DEPTH_2, N_EXPERTS_2), 0.01),
        "exp_w1": nrm(ks[20], (DEPTH_2, N_EXPERTS_2, D_MODEL, D_EXPERT), D_MODEL ** -0.5),
        "exp_w3": nrm(ks[21], (DEPTH_2, N_EXPERTS_2, D_MODEL, D_EXPERT), D_MODEL ** -0.5),
        "exp_w2": nrm(ks[22], (DEPTH_2, N_EXPERTS_2, D_EXPERT, D_MODEL), D_EXPERT ** -0.5),
        "shared_w1": nrm(ks[23], (DEPTH_2, D_MODEL, D_SHARED), D_MODEL ** -0.5),
        "shared_w3": nrm(ks[24], (DEPTH_2, D_MODEL, D_SHARED), D_MODEL ** -0.5),
        "shared_w2": nrm(ks[25], (DEPTH_2, D_SHARED, D_MODEL), D_SHARED ** -0.5),
        "final_norm_g": 1.0 + nrm(ks[26], (D_MODEL,), 0.05),
    }

def second_block(x, c, ctx, c_ctx, ada_w, ada_b, norm1_g, w_in, lambda_q1, lambda_k1, lambda_q2, lambda_k2,
              dattn_norm_g, ret_decay_fwd, ret_decay_bwd, ret_norm_g, w_out, norm2_g, router_w, router_bias,
              exp_w1, exp_w3, exp_w2, shared_w1, shared_w3, shared_w2, final_norm_g):
    s = x.shape[1]
    cos, sin = axial_rope_tables(s)
    xc = ctx
    for l in range(DEPTH_2):
        lam_init = 0.8 - 0.6 * math.exp(-0.3 * l)
        mod_x = jax.nn.silu(c) @ ada_w[l] + ada_b[l]
        mod_c = (jax.nn.silu(c_ctx) @ ada_w[l] + ada_b[l])[None]
        x, xc = hybrid_layer(x, xc, mod_x, mod_c, cos, sin, lam_init, l < DEPTH_2 - 1,
                             norm1_g[l], w_in[l], lambda_q1[l], lambda_k1[l], lambda_q2[l], lambda_k2[l],
                             dattn_norm_g[l], ret_decay_fwd[l], ret_decay_bwd[l], ret_norm_g[l], w_out[l],
                             norm2_g[l], router_w[l], router_bias[l], exp_w1[l], exp_w3[l], exp_w2[l],
                             shared_w1[l], shared_w3[l], shared_w2[l])
    return rmsnorm(x, final_norm_g)


def setup_inputs(seed=0):
    out = dict(first_inputs(seed))
    for name, value in second_inputs(seed + 1).items():
        if name != "x":
            out[name + "_2"] = value
    return out


def reference(
    x, c, ada_w, ada_b, norm_mix_g, norm_ffn_g, w_in, rg_conv_w, rg_conv_b, rg_wa, rg_ba, rg_wx,
    rg_bx, rg_lambda, gla_wg2, gla_bg, gla_norm_g, w_out, ffn_w1, ffn_w3, ffn_w2, router_w,
    moe_w1, moe_w3, moe_w2, final_g, c_2, ctx_2, c_ctx_2, ada_w_2, ada_b_2, norm1_g_2, w_in_2,
    lambda_q1_2, lambda_k1_2, lambda_q2_2, lambda_k2_2, dattn_norm_g_2, ret_decay_fwd_2,
    ret_decay_bwd_2, ret_norm_g_2, w_out_2, norm2_g_2, router_w_2, router_bias_2, exp_w1_2,
    exp_w3_2, exp_w2_2, shared_w1_2, shared_w3_2, shared_w2_2, final_norm_g_2,
):
    x = first_block(
        x, c, ada_w, ada_b, norm_mix_g, norm_ffn_g, w_in, rg_conv_w, rg_conv_b, rg_wa, rg_ba,
        rg_wx, rg_bx, rg_lambda, gla_wg2, gla_bg, gla_norm_g, w_out, ffn_w1, ffn_w3, ffn_w2,
        router_w, moe_w1, moe_w3, moe_w2, final_g,
    )
    return second_block(
        x, c_2, ctx_2, c_ctx_2, ada_w_2, ada_b_2, norm1_g_2, w_in_2, lambda_q1_2, lambda_k1_2,
        lambda_q2_2, lambda_k2_2, dattn_norm_g_2, ret_decay_fwd_2, ret_decay_bwd_2,
        ret_norm_g_2, w_out_2, norm2_g_2, router_w_2, router_bias_2, exp_w1_2, exp_w3_2,
        exp_w2_2, shared_w1_2, shared_w3_2, shared_w2_2, final_norm_g_2,
    )


_drawn_inputs = setup_inputs


def setup_inputs(seed=0):
    import zlib

    import numpy as np

    out = dict(_drawn_inputs(seed))
    spreads = {}
    factors = {'rg_ba': 31.975,
     'rg_bx': 6.36,
     'lambda_q2_2': 3.128,
     'lambda_k2_2': 8.0,
     'dattn_norm_g_2': 3.303,
     'ret_norm_g_2': 3.69}
    for name, (base, spread) in spreads.items():
        noise = np.random.default_rng([zlib.crc32(name.encode()), seed]).standard_normal(out[name].shape)
        drawn = base * np.exp(spread * noise) if base else spread * noise
        out[name] = __import__('jax').numpy.asarray(drawn.astype(out[name].dtype))
    for name, factor in factors.items():
        out[name] = (out[name] * factor).astype(out[name].dtype)
    return out
```

```python
from contextlib import ExitStack

import concourse.bass as bass
from concourse import mybir

F32 = mybir.dt.float32
U32 = mybir.dt.uint32
ALU = mybir.AluOpType
ACT = mybir.ActivationFunctionType
AX = mybir.AxisListType.X

P = 128
T = 256
TT = T // P
D = 1024
KD = D // P
CW = 256
RING = 9
U = RING // 3
LAYERS = 2
RG = 512
CH = 64
NCH = T // CH
FF = 2816
EPS = 1e-6
LAM_INIT = 0.2
HEADS = 4

C_ID, C_ROT, C_COS, C_SIN, C_SCAN, C_CAUS, C_UP, C_DOWN, C_TOK, C_IOTA = (
    0, 128, 256, 512, 768, 1024, 1152, 1408, 1664, 1668)
C_N = C_IOTA + 64
V_ADAB, V_G1, V_G2 = 0, 48, 56
V_CONVW, V_CONVB, V_BA, V_BX, V_LAM, V_BG, V_GLAG, V_EXTRA = 64, 80, 84, 88, 92, 96, 98, 99
V_ROWS = 107
W_DG, W_RG, W_FG, W_C, W_CC = 64, 65, 66, 74, 82
W_ROWS = 90


def constants():
    import numpy as np
    c = np.zeros((P, C_N), np.float32)
    c[:, C_ID:C_ID + P] = np.eye(P)
    for p in range(P):
        if (p // 16) % 2 == 0:
            c[p + 16, C_ROT + p] = -1.0
        else:
            c[p - 16, C_ROT + p] = 1.0
    t = np.arange(T)
    inv = (10000.0 ** (-np.arange(16, dtype=np.float32) / 16)).astype(np.float32)
    for p in range(P):
        pos = (t // 64 if (p // 32) % 2 == 0 else t % 64).astype(np.float32)
        ang = pos * inv[p % 16]
        c[p, C_COS:C_COS + T] = np.cos(ang)
        c[p, C_SIN:C_SIN + T] = np.sin(ang)
    c[:, C_SCAN:C_SCAN + T] = (t % CH != 0)
    j = np.arange(P)[:, None]
    i = np.arange(P)[None, :]
    c[:, C_CAUS:C_CAUS + P] = (i >= j) & (i // CH == j // CH)
    c[:, C_UP:C_UP + T] = t + 1
    c[:, C_DOWN:C_DOWN + T] = T - t
    for jt in range(TT):
        tok = np.arange(P) + jt * P
        c[:, C_TOK + jt] = T - 1 - tok
        c[:, C_TOK + TT + jt] = tok
    c[:, C_IOTA:C_IOTA + 64] = np.arange(64)
    r = np.zeros((P, 4, TT, T), np.float32)
    for jt in range(TT):
        rel = t[None, :] - (np.arange(P)[:, None] + jt * P)
        r[:, 0, jt], r[:, 1, jt] = np.maximum(rel, 0), np.maximum(-rel, 0)
        r[:, 2, jt], r[:, 3, jt] = rel >= 0, rel <= 0
    return c, r.reshape(P, -1)


def build(nc, A, cst, rel, gates_dram, out):
    with ExitStack() as ctx:
        def sb(name, shape, dt=F32):
            return ctx.enter_context(nc.sbuf_tensor(name, shape, dt))

        sems = {}

        def sem(name):
            if name not in sems:
                sems[name] = ctx.enter_context(nc.semaphore(name))
            return sems[name]

        ring = sb("ring", [P, RING, KD * CW])
        xT = sb("xT", [P, KD, T])
        hcat = sb("hcat", [P, KD, 2 * T])
        hT = hcat[:, :, 0:T]
        hflat = hcat[:, :, :].rearrange("p k t -> p (k t)")
        sq = sb("sq", [P, KD, T])
        sqf = sq[:, :, :].rearrange("p k t -> p (k t)")
        mixT = sb("mixT", [P, KD, T])
        C = sb("C", [P, C_N])
        Dret = sb("Dret", [P, HEADS, TT * T])
        VT = sb("VT", [P, 3, P])
        VN = sb("VN", [P, 3, P])
        rstd = sb("rstd", [P, T])
        ffn_s = sb("ffn_s", [P, 2, T])
        ffn_a = sb("ffn_a", [P, 2, T])
        ffn_g = sb("ffn_g", [P, 4, T])
        TMP = sb("TMP", [P, 11264])
        ones = sb("ones", [P, P])
        small = sb("small", [P, 640])
        modc = sb("modc", [P, 2, 48])
        router = sb("router", [P, KD, 64])
        wf = sb("wf", [P, KD, 16])
        wa_bd = sb("wa_bd", [P, 4, P])
        wx_bd = sb("wx_bd", [P, 4, P])
        wg2 = sb("wg2", [16, T])
        ident = C[:, C_ID:C_ID + P]

        B = [ctx.enter_context(nc.psum_tensor(f"B{i}", [P, 512], F32)) for i in range(8)]

        at = [0]

        def cut(n, **dims):
            v = TMP[:, at[0]:at[0] + n]
            at[0] += n
            return v

        UPW = T + 3
        upad = cut(4 * UPW).rearrange("p (c t) -> p c t", c=4)
        gate = cut(1024)
        qT = cut(512)
        kT = cut(512)
        gT = cut(1024)
        vn = cut(1024).rearrange("p (a f) -> p a f", a=TT)
        qloc, kloc, qin, kend = cut(512), cut(512), cut(512), cut(512)
        kendn = cut(512).rearrange("p (a f) -> p a f", a=TT)
        sT = cut(1024).rearrange("p (a f) -> p a f", a=TT)
        St = cut(3 * 256).rearrange("p (n a v) -> p n a v", n=3, a=2)
        uc = cut(1024)
        sc_sig = uc
        blast = cut(8)
        assert at[0] <= 11264
        rr, ri = hflat[:, 2048:3072], hflat[:, 3072:4096]
        hT1 = hflat[:, 0:2048].rearrange("p (k t) -> p k t", k=KD)
        d1, d2, lfs, tmp1 = sqf[:, 0:512], sqf[:, 512:1024], sqf[:, 1024:1536], sqf[:, 1536:2048]
        ra = ffn_g[:, :, :].rearrange("p s t -> p (s t)")
        rm = mixT[:, 4:8, :].rearrange("p k t -> p (k t)")
        flT = ffn_s[0:16, 0, :]
        at[0] = 0
        q2 = cut(1024).rearrange("p (h t) -> p h t", h=HEADS)
        k2 = cut(2048).rearrange("p (h t) -> p h t", h=HEADS)
        v2 = cut(2048).rearrange("p (a f) -> p a f", a=4)
        rq = cut(512).rearrange("p (h t) -> p h t", h=2)
        rk = cut(512).rearrange("p (h t) -> p h t", h=2)
        rkn = cut(512).rearrange("p (a f) -> p a f", a=2)
        rv = cut(2048).rearrange("p (a f) -> p a f", a=4)
        rg = cut(1024).rearrange("p (h t) -> p h t", h=HEADS)
        qdec = cut(1024).rearrange("p (r h t) -> p r h t", r=2, h=2)
        S2 = cut(512).rearrange("p (h r v) -> p h r v", h=2, r=2)
        assert at[0] <= 11264
        kdec = sqf[:, 0:1024].rearrange("p (r a f) -> p r a f", r=2, a=2)
        sD = sqf[:, 1024:2048].rearrange("p (b f) -> p b f", b=2)
        pex = hflat[:, 0:2048].rearrange("p (b m f) -> p b m f", b=2, m=2)
        paT = hflat[:, 2048:4096].rearrange("p (b c t) -> p b c t", b=2, c=4)
        rope_t = ffn_a[:, :, :].rearrange("p b t -> p (b t)")

        def cols(w, c0):
            return w.rearrange("(k p) f -> p k f", p=P)[:, :, c0:c0 + CW]

        WIN1 = [1024, 1280, 0, 256, 1536, 1792, 2048, 2304, 512, 768]
        WIN2 = [1536, 1792, 2048, 2304, 512, 768, 1024, 1280, 0, 256, 2560, 2816]
        stream = []
        n_plain = [0]

        def plain(w, c0):
            n_plain[0] += 1
            stream.append(("plain", cols(w, c0), ("plain_used", n_plain[0])))

        marks = {}

        def mark(name):
            marks[name] = (len(stream), n_plain[0])

        STEPS = {"f0": 11, "f1": 88, "f2": 65}
        base = {"f0": 0, "f1": 0, "f2": 0}
        tile0 = 0
        for l in range(LAYERS):
            mark(f"ada{l}")
            for j in range(24):
                plain(A["ada_w"][l], j * CW)
            mark(f"win{l}")
            for c0 in WIN1:
                plain(A["w_in"][l], c0)
            mark(f"wout{l}")
            for j in range(4):
                plain(A["w_out"][l], j * CW)
            ph = f"f{l}"
            mark(ph)
            base[ph] = tile0
            for s in range(STEPS[ph]):
                stream.append(("ffn", (ph, s, 0), ("h_ready", tile0 + 2 * s + 2)))
                stream.append(("ffn", (ph, s, 1), ("h_ready", tile0 + 2 * s + 2)))
                stream.append(("ffn", (ph, s, 2), ("down_done", tile0 + 2 * s + 2)))
            tile0 += 2 * STEPS[ph]
        mark("ada2")
        for j in range(24):
            plain(A["ada_w_2"][0], j * CW)
        mark("win2")
        for c0 in WIN2:
            plain(A["w_in_2"][0], c0)
        mark("wout2")
        for j in range(4):
            plain(A["w_out_2"][0], j * CW)
        mark("f2")
        base["f2"] = tile0
        for s in range(STEPS["f2"]):
            stream.append(("ffn", ("f2", s, 0), ("h_ready", tile0 + 2 * s + 2)))
            stream.append(("ffn", ("f2", s, 1), ("h_ready", tile0 + 2 * s + 2)))
            stream.append(("ffn", ("f2", s, 2), ("down_done", tile0 + 2 * s + 2)))
        tile0 += 2 * STEPS["f2"]
        piece_sem = [sem(f"piece_in_{i}") for i in range(RING)]

        def ffn_weights(ph, s):
            if ph == "f0":
                w1, w3, w2, c = A["ffn_w1"][0], A["ffn_w3"][0], A["ffn_w2"][0], s
            elif ph == "f1":
                e, c = s // 11, s % 11
                w1, w3, w2 = A["moe_w1"][0][e], A["moe_w3"][0][e], A["moe_w2"][0][e]
            elif isinstance(s, int) and s == 64:
                w1, w3, w2, c = A["shared_w1_2"][0], A["shared_w3_2"][0], A["shared_w2_2"][0], 0
            else:
                w1, w3, w2, c = A["exp_w1_2"][0][s], A["exp_w3_2"][0][s], A["exp_w2_2"][0][s], 0
            v1, v3 = (w.rearrange("(k p) f -> p k f", p=P) for w in (w1, w3))
            v2_ = w2.rearrange("(c k p) n -> c p k n", p=P, k=2)
            if isinstance(c, int):
                return v1[:, :, c * CW:(c + 1) * CW], v3[:, :, c * CW:(c + 1) * CW], v2_[c]
            return v1[:, :, bass.ts(c, CW)], v3[:, :, bass.ts(c, CW)], v2_[c]

        def piece(n):
            return ring[:, n % RING, :].rearrange("p (k f) -> p k f", k=KD)

        def piece_down(n):
            return ring[:, n % RING, :].rearrange("p (k f) -> p k f", k=2)

        def arrived(eng, n, i=0):
            eng.wait_ge(piece_sem[n % RING], (i + (n // RING + 1)) * 16)

        block = ctx.enter_context(nc.Block())

        gate_sem = [sem(f"gate_in_{i}") for i in range(4)]
        GATED = {"f1": 88, "f2": 64}

        @block.sync
        def _(sp):
            def load(n):
                kind, what, _ = stream[n]
                if n >= RING:
                    name, value = stream[n - RING][2]
                    sp.wait_ge(sem(name), value)
                if kind == "plain":
                    sp.dma_start(piece(n), what).then_inc(piece_sem[n % RING], 16)
                else:
                    ph, s, part = what
                    dst = piece_down(n) if part == 2 else piece(n)
                    sp.dma_start(dst, ffn_weights(ph, s)[part]).then_inc(piece_sem[n % RING], 16)

            def load_ffn(ph):
                n0 = marks[ph][0]
                loops = (STEPS[ph] - 1) // U
                for n in range(n0, n0 + RING):
                    load(n)
                with sp.Fori(1, loops) as i:
                    for j in range(RING):
                        s = i * U + j // 3
                        name, value = stream[n0 + j][2]
                        sp.wait_ge(sem(name), i * (2 * U) + (value - 2 * U))
                        n = n0 + j
                        dst = piece_down(n) if j % 3 == 2 else piece(n)
                        sp.dma_start(dst, ffn_weights(ph, s)[j % 3]).then_inc(piece_sem[n % RING], 16)
                for n in range(n0 + loops * RING, n0 + 3 * STEPS[ph]):
                    load(n)

            for l in range(LAYERS):
                for n in range(marks[f"ada{l}"][0], marks[f"f{l}"][0]):
                    load(n)
                load_ffn(f"f{l}")
            for n in range(marks["ada2"][0], marks["f2"][0]):
                load(n)
            load_ffn("f2")
            sp.wait_ge(sem("out_tile"), 2)
            sp.dma_start(out.rearrange("b (a p) d -> p (b a) d", p=P),
                         hflat[:, 0:2048].rearrange("p (a d) -> p a d", a=TT)).then_inc(sem("stored"), 16)
            sp.wait_ge(sem("stored"), 16)

        XN, CN = TMP[:, 0:2048], TMP[:, 2048:4096]

        @block.gpsimd
        def _(pool):
            nc.gpsimd.memset(ones[:], 1.0).then_inc(sem("ones_ready"), 1)
            nc.gpsimd.memset(wa_bd[:], 0.0).then_inc(sem("pool_zero"), 1)
            nc.gpsimd.memset(wx_bd[:], 0.0).then_inc(sem("pool_zero"), 1)

            def rows(l, row, ap):
                n = ap.shape[0]
                pool.dma_start(VN[row:row + n, l, :], ap).then_inc(sem("vec_in"), 16)

            for l in range(LAYERS):
                rows(l, V_ADAB, A["ada_b"][l].rearrange("(a p) -> a p", p=P))
                rows(l, V_G1, A["norm_mix_g"][l].rearrange("(a p) -> a p", p=P))
                rows(l, V_G2, A["norm_ffn_g"][l].rearrange("(a p) -> a p", p=P))
                rows(l, V_CONVW, A["rg_conv_w"][l].rearrange("w (a p) -> (w a) p", p=P))
                rows(l, V_CONVB, A["rg_conv_b"][l].rearrange("(a p) -> a p", p=P))
                rows(l, V_BA, A["rg_ba"][l].rearrange("(a p) -> a p", p=P))
                rows(l, V_BX, A["rg_bx"][l].rearrange("(a p) -> a p", p=P))
                rows(l, V_LAM, A["rg_lambda"][l].rearrange("(a p) -> a p", p=P))
                rows(l, V_BG, A["gla_bg"][l].rearrange("(a p) -> a p", p=P))
                rows(l, V_GLAG, A["gla_norm_g"][l].rearrange("(a p) -> a p", p=P))
                rows(l, V_EXTRA, (A["c"][0] if l == 0 else A["final_g"]).rearrange("(a p) -> a p", p=P))
            for row, name in ((V_ADAB, "ada_b_2"), (V_G1, "norm1_g_2"), (V_G2, "norm2_g_2"),
                              (W_DG, "dattn_norm_g_2"), (W_RG, "ret_norm_g_2"), (W_C, "c_2")):
                rows(2, row, A[name][0].rearrange("(a p) -> a p", p=P))
            rows(2, W_FG, A["final_norm_g_2"].rearrange("(a p) -> a p", p=P))
            rows(2, W_CC, A["c_ctx_2"].rearrange("(a p) -> a p", p=P))
            for k, name in enumerate(("ret_decay_fwd_2", "ret_decay_bwd_2")):
                pool.dma_start(small[:, 8 + 4 * k:12 + 4 * k],
                               A[name][0:1, :].to_broadcast([P, 4])).then_inc(sem("vec_in"), 16)
            for k, name in enumerate(("lambda_q1_2", "lambda_k1_2", "lambda_q2_2", "lambda_k2_2")):
                pool.dma_start(small[:, 256 + 64 * k:320 + 64 * k],
                               A[name][0:1, :].to_broadcast([P, 64])).then_inc(sem("vec_in"), 16)

            def layer_weights(l):
                s = sem("small_w_in")
                pool.dma_start(wf[:], A["w_in"][l].rearrange("(k p) f -> p k f", p=P)[:, :, 2560:2576]).then_inc(s, 16)
                pool.dma_start(wg2[:], A["gla_wg2"][l]).then_inc(s, 16)
                for bd, name in ((wa_bd, "rg_wa"), (wx_bd, "rg_wx")):
                    for half in range(2):
                        src = A[name][l].rearrange("(c b) d e -> b d c e", b=2)[half]
                        pool.dma_start(bd[64 * half:64 * half + 64, :, 64 * half:64 * half + 64],
                                       src).then_inc(s, 16)

            pool.wait_ge(sem("pool_zero"), 2)
            layer_weights(0)
            pool.dma_start(router[:, :, 0:8], A["router_w"][0].rearrange("(k p) f -> p k f", p=P)).then_inc(sem("router_in"), 16)
            pool.wait_ge(sem("gla_u_ready"), 1)
            layer_weights(1)
            for ph, l, n, key in (("f1", 0, 88, 11), ("f2", 1, 64, 1)):
                pool.wait_ge(sem("gates_stored"), 16 * (l + 1))
                t0 = base[ph]
                if l:
                    pool.wait_ge(sem("a_ready"), base["f1"] + 2 * 88)

                def load_gate(s, j, e):
                    pool.dma_start(ffn_g[:, j, :], gates_dram[l][bass.ds(e, 1), :].to_broadcast([P, T])).then_inc(gate_sem[j], 16)

                for j in range(U):
                    load_gate(j, j, j // key)
                with pool.Fori(1, n // U) as i:
                    for j in range(U):
                        s = i * U + j
                        pool.wait_ge(sem("a_ready"), i * (2 * U) + (t0 + 2 * j + 2 - 2 * U))
                        load_gate(s, j, s // key if key > 1 else s)
                for s in range(n // U * U, n):
                    pool.wait_ge(sem("a_ready"), t0 + 2 * s + 2 - 2 * U)
                    load_gate(s, s % U, s // key)
                if l == 0:
                    pool.wait_ge(sem("logits_ready"), 1)
                    pool.dma_start(router[:], A["router_w_2"][0].rearrange("(k p) f -> p k f", p=P)).then_inc(sem("router_in"), 16)
                    pool.dma_start(small[:, 192:256], A["router_bias_2"][0:1, :].to_broadcast([P, 64])).then_inc(sem("router_in"), 16)

        NVEC = 16 * (2 * 11 + 8 + 6)

        @block.tensor
        def _(pe):
            mm = nc.tensor.matmul

            def transpose_in(src, half):
                for k in range(KD):
                    last = nc.tensor.transpose(B[2 * half + k // 4][:, (k % 4) * P:(k % 4 + 1) * P],
                                               src[:, k * P:(k + 1) * P], ident)
                last.then_inc(sem("xin_ready"), 1)

            def ada(name, nv):
                n0 = marks[name][0]
                for j in range(24):
                    arrived(pe, n0 + j)
                    w = piece(n0 + j)
                    for m in (2 * j, 2 * j + 1):
                        for k in range(KD):
                            last = mm(B[7][:, nv * m:nv * m + nv], w[:, k, (m % 2) * P:(m % 2 + 1) * P],
                                      small[:, 32 + 2 * k:32 + 2 * k + nv] if nv == 2 else small[:, 24 + k:25 + k],
                                      start=(k == 0), stop=(k == KD - 1))
                    last.then_inc(sem("plain_used"), 1)

            def norm(n, bank=6):
                pe.wait_ge(sem("sq_ready"), n + 1)
                for k in range(KD):
                    last = mm(B[bank][:, 0:T], ones[:], sq[:, k, :], start=(k == 0), stop=(k == KD - 1))
                last.then_inc(sem("ss_ready"), 1)

            def project_T(n, bank, rhs, width=T):
                arrived(pe, n)
                w = piece(n)
                for m in range(2):
                    dst = B[bank[m]][:, 0:width] if width > T else B[bank][:, m * T:(m + 1) * T]
                    for k in range(KD):
                        last = mm(dst, w[:, k, m * P:(m + 1) * P], rhs[:, k, 0:width],
                                  start=(k == 0), stop=(k == KD - 1))
                last.then_inc(sem("plain_used"), 1)

            def project_nat(n, bank, lhs):
                arrived(pe, n)
                w = piece(n)
                for a in range(len(lhs)):
                    for k in range(KD):
                        last = mm(B[bank[a // 2]][:, (a % 2) * CW:(a % 2 + 1) * CW], lhs[a](k), w[:, k, :],
                                  start=(k == 0), stop=(k == KD - 1))
                last.then_inc(sem("plain_used"), 1)

            def out_proj(name, banks, release):
                n0 = marks[name][0]
                for j in range(4):
                    if j >= len(banks):
                        pe.wait_ge(*release(j))
                    arrived(pe, n0 + j)
                    w = piece(n0 + j)
                    for m in range(2):
                        for k in range(KD):
                            last = mm(B[banks[j % len(banks)]][:, m * T:(m + 1) * T], w[:, k, m * P:(m + 1) * P],
                                      mixT[:, k, :], start=(k == 0), stop=(k == KD - 1))
                    last.then_inc(sem("plain_used"), 1)

            def mixer1(l):
                pe.wait_ge(sem("h_norm"), 2 * l + 1)
                pe.wait_ge(sem("small_w_in"), 16 * 6 * (l + 1))
                for k in range(KD):
                    last = mm(B[4][0:16, 0:T], wf[:, k, :], hT1[:, k, :], start=(k == 0), stop=(k == KD - 1))
                last.then_inc(sem("flow_ready"), 1)
                n0 = marks[f"win{l}"][0]
                for j in range(10):
                    if j >= 4:
                        pe.wait_ge(sem("z_in"), 10 * l + j - 3)
                    if j in (4, 5):
                        project_nat(n0 + j, [j % 4], [lambda k, a=a: hT1[:, k, a * P:(a + 1) * P] for a in range(TT)])
                    else:
                        project_T(n0 + j, j % 4, hT1)
                    if j == 1:
                        pe.wait_ge(sem("flT_ready"), l + 1)
                        for m in range(2):
                            last = mm(B[5][:, m * T:(m + 1) * T], wg2[:, m * P:(m + 1) * P], flT[:, :], start=True, stop=True)
                        last.then_inc(sem("lf_ready"), 1)
                    if j == 6:
                        pe.wait_ge(sem("conv_ready"), l + 1)
                        pe.wait_ge(sem("lf_done"), l + 1)
                        for g, (bank, bd, pair) in enumerate(((4, wa_bd, 0), (5, wa_bd, 1), (6, wx_bd, 0), (4, wx_bd, 1))):
                            if g == 3:
                                pe.wait_ge(sem("rgate_done"), 4 * l + 1)
                            for m in range(2):
                                c = 2 * pair + m
                                last = mm(B[bank][:, m * T:(m + 1) * T], bd[:, c, :], uc[:, c * T:(c + 1) * T], start=True, stop=True)
                            last.then_inc(sem("rgate_ready"), 1)
                pe.wait_ge(sem("gla_in"), l + 1)
                pe.wait_ge(sem("rgate_done"), 4 * l + 4)
                for a in range(TT):
                    for pr in range(2):
                        last = nc.tensor.transpose(B[4][:, a * T + pr * P:a * T + (pr + 1) * P],
                                                   kend[:, pr * T + a * P:pr * T + (a + 1) * P], ident)
                last.then_inc(sem("kendn_ready"), 1)
                pe.wait_ge(sem("z_in"), 10 * l + 10)
                for par in range(2):
                    r = slice(64 * par, 64 * par + 64)
                    for o in range(0, 512, P):
                        last = mm(B[par][:, o:o + P], kloc[r, o:o + P], qloc[r, o:o + P], start=True, stop=True)
                    last.then_inc(sem("gla_s_ready"), 1)
                pe.wait_ge(sem("kendn_done"), l + 1)
                for n in range(NCH - 1):
                    for h in range(HEADS):
                        r = slice(64 * (n % 2), 64 * (n % 2) + 64)
                        bank, o = 5 + n % 2, (n // 2) * T + (h // 2) * P
                        last = mm(B[bank][64 * (h % 2):64 * (h % 2) + 64, o:o + P],
                                  kendn[r, n // 2, h * 64:(h + 1) * 64], vn[r, n // 2, h * P:(h + 1) * P],
                                  start=True, stop=True)
                last.then_inc(sem("gla_u_ready"), 1)
                pe.wait_ge(sem("gla_sT_done"), 2 * (l + 1))
                pe.wait_ge(sem("state_ready"), 3 * (l + 1))
                for h in range(HEADS):
                    rows = slice(64 * (h % 2), 64 * (h % 2) + 64)
                    for a in range(TT):
                        o = (h // 2) * T + a * P
                        bank = B[2 + h % 2]
                        last = mm(bank[:, o:o + P], vn[:, a, h * P:(h + 1) * P], sT[:, a, h * P:(h + 1) * P],
                                  start=True, stop=False, skip_group_check=True)
                        for n in range(max(2 * a, 1), 2 * a + 2):
                            oo = (h // 2) * T + n * CH
                            last = mm(bank[:, oo:oo + CH], St[rows, n - 1, h // 2, :],
                                      qin[rows, (h // 2) * T + n * CH:(h // 2) * T + (n + 1) * CH],
                                      start=False, stop=(n == 2 * a + 1), skip_group_check=True)
                    if h >= 2:
                        last.then_inc(sem("gla_o_ready"), 1)
                for b in range(2):
                    pe.wait_ge(sem("gla_sq_ready"), 2 * l + b + 1)
                    mm(B[b][:, :], ones[:], sqf[:, b * 512:(b + 1) * 512], start=True, stop=True).then_inc(sem("gla_ss_ready"), 1)
                pe.wait_ge(sem("mix_ready"), l + 1)
                out_proj(f"wout{l}", [4, 5, 6], lambda j: (sem("x_part"), 4 * l + 1))

            def route(l, E, hh):
                pe.wait_ge(sem("router_in"), 16 if l == 0 else 48)
                for a in range(TT):
                    for k in range(KD):
                        last = mm(B[7][:, a * E:(a + 1) * E], hh(k, a), router[:, k, 0:E],
                                  start=(k == 0), stop=(k == KD - 1))
                last.then_inc(sem("logits_ready"), 1)
                pe.wait_ge(sem("gates_ready"), l + 1)
                for a in range(TT):
                    last = nc.tensor.transpose(B[7][0:E, P + a * P:P + (a + 1) * P], small[:, 512 + a * 64:512 + a * 64 + E], ident)
                last.then_inc(sem("gatesT_ready"), 1)

            def ffn(ph, hh):
                n0, t0, steps = marks[ph][0], base[ph], STEPS[ph]

                def up(j, m, i=0):
                    bank = B[4 + m]
                    for part in range(2):
                        if m == 0:
                            arrived(pe, n0 + 3 * j + part, i)
                        w = piece(n0 + 3 * j + part)
                        for k in range(KD):
                            last = mm(bank[:, part * T:(part + 1) * T], w[:, k, m * P:(m + 1) * P], hh(k),
                                      start=(k == 0), stop=(k == KD - 1))
                    last.then_inc(sem("h_ready"), 1)

                def down(j, m, i=0, first=False, last_tile=False):
                    pe.wait_ge(sem("a_ready"), i * (2 * U) + (t0 + 2 * j + m + 1))
                    if m == 0:
                        arrived(pe, n0 + 3 * j + 2, i)
                    w = piece_down(n0 + 3 * j + 2)
                    for d in range(KD):
                        last = mm(B[d // 2][:, (d % 2) * T:(d % 2 + 1) * T], w[:, m, d * P:(d + 1) * P],
                                  ffn_a[:, m, :], start=(first and d % 2 == 0), stop=last_tile,
                                  skip_group_check=True)
                    last.then_inc(sem("down_done"), 1)

                up(0, 0)
                loops = (steps - 1) // U
                for j in range(U):
                    up(j, 1)
                    down(j, 0, first=(j == 0))
                    up(j + 1, 0)
                    down(j, 1)
                with pe.Fori(1, loops) as i:
                    for j in range(U):
                        up(j, 1, i)
                        down(j, 0, i)
                        up(j + 1, 0, i)
                        down(j, 1, i)
                for s in range(U * loops, steps):
                    up(s, 1)
                    down(s, 0)
                    if s + 1 < steps:
                        up(s + 1, 0)
                    down(s, 1, last_tile=(s + 1 == steps))

            def mixer2():
                n0 = marks["win2"][0]
                pe.wait_ge(sem("h_norm"), 6)
                pe.wait_ge(sem("h_norm"), 7)
                x_t = [lambda k, a=a: hcat[:, k, a * P:(a + 1) * P] for a in range(4)]
                for j in range(12):
                    bk = [2 * (j % 2), 2 * (j % 2) + 1]
                    if j >= 2:
                        pe.wait_ge(sem("z2_in"), j - 1)
                    if j == 0:
                        project_T(n0, 0, hcat)
                    elif j == 1:
                        arrived(pe, n0 + 1)
                        w = piece(n0 + 1)
                        for m in range(2):
                            for k in range(KD):
                                mm(B[2][:, m * T:(m + 1) * T], w[:, k, m * P:(m + 1) * P], hcat[:, k, 0:T],
                                   start=(k == 0), stop=(k == KD - 1))
                        for a in range(2):
                            for k in range(KD):
                                last = mm(B[3][:, a * CW:(a + 1) * CW], hcat[:, k, (2 + a) * P:(3 + a) * P], w[:, k, :],
                                          start=(k == 0), stop=(k == KD - 1))
                        last.then_inc(sem("plain_used"), 1)
                    elif j in (2, 3, 6, 7):
                        project_nat(n0 + j, bk, x_t)
                    elif j in (4, 5):
                        project_T(n0 + j, bk, hcat, width=2 * T)
                    else:
                        project_T(n0 + j, bk[0], hcat)
                pe.wait_ge(sem("z2_in"), 12)
                for g in range(6):
                    if g >= 2:
                        pe.wait_ge(sem("rope_done"), g - 1)
                    for m in range(2):
                        src = [rq[:, m, :], rk[:, m, :], k2[:, m, T:], k2[:, 2 + m, T:], q2[:, m, :], q2[:, 2 + m, :]][g]
                        last = mm(B[4 + g % 2][:, m * T:(m + 1) * T], C[:, C_ROT:C_ROT + P], src, start=True, stop=True)
                    last.then_inc(sem("rot_ready"), 1)
                pe.wait_ge(sem("kdec_ready"), 1)
                for pr in range(2):
                    for dr in range(2):
                        for hh in range(2):
                            h = 2 * pr + hh
                            for a in range(2):
                                last = mm(B[6][64 * hh:64 * hh + 64, (pr * 2 + dr) * P:(pr * 2 + dr + 1) * P],
                                          kdec[:, dr, a, h * 64:(h + 1) * 64], rv[:, 2 + a, h * P:(h + 1) * P],
                                          start=(a == 0), stop=(a == 1))
                last.then_inc(sem("s2_psum"), 1)
                pe.wait_ge(sem("rope_done"), 2)
                for h in range(HEADS):
                    r = slice(64 * (h % 2), 64 * (h % 2) + 64)
                    if h >= 2:
                        pe.wait_ge(sem("sD_ready"), h - 1)
                    for a in range(2):
                        last = mm(B[h % 2][:, a * T:(a + 1) * T], rk[r, h // 2, a * P:(a + 1) * P], rq[r, h // 2, :],
                                  start=True, stop=True)
                    last.then_inc(sem("ret_s"), 1)
                    if h >= 1:
                        ret_out(h - 1)
                ret_out(HEADS - 1)
                for b in range(2):
                    pe.wait_ge(sem("ret_sq"), b + 1)
                    mm(B[b][:, :], ones[:], sqf[:, b * 512:(b + 1) * 512], start=True, stop=True).then_inc(sem("ret_ss"), 1)
                pe.wait_ge(sem("rope_done"), 6)
                pe.wait_ge(sem("ret_done"), 4)
                for g in range(8):
                    h, a = g // 2, g % 2
                    if g >= 2:
                        pe.wait_ge(sem("p_ready"), 2 * (g - 1))
                    for m in range(2):
                        r = slice(64 * m, 64 * m + 64)
                        mm(B[2 * (g % 2) + m][:, :], q2[r, h, a * P:(a + 1) * P], k2[r, h, :],
                           start=True, stop=True).then_inc(sem("att_s"), 1)
                    if g >= 1:
                        att_T(g - 1)
                    if g >= 3 and g % 2 == 1:
                        att_out((g - 3) // 2)
                att_T(7)
                att_out(3)
                pe.wait_ge(sem("mix_ready"), 3)
                out_proj("wout2", [0, 1, 2, 3], None)

            def ret_out(h):
                r = slice(64 * (h % 2), 64 * (h % 2) + 64)
                pe.wait_ge(sem("sD_ready"), h + 1)
                if h == 0:
                    pe.wait_ge(sem("S2_ready"), 1)
                    pe.wait_ge(sem("qdec_ready"), 1)
                dst = B[2 + h % 2][:, (h // 2) * T:(h // 2 + 1) * T]
                for a in range(2):
                    mm(dst, rv[:, a, h * P:(h + 1) * P], sD[:, h % 2, a * T:(a + 1) * T],
                       start=(a == 0), stop=False, skip_group_check=True)
                for dr in range(2):
                    last = mm(dst, S2[r, h // 2, dr, :], qdec[r, dr, h // 2, :], start=False, stop=(dr == 1),
                              skip_group_check=True)
                last.then_inc(sem("ret_o"), 1)

            def att_T(g):
                pe.wait_ge(sem("a2_ready"), g + 1)
                if g >= 1:
                    pe.wait_ge(sem("aT_ready"), g)
                for c in range(4):
                    last = nc.tensor.transpose(B[4][:, c * P:(c + 1) * P], pex[:, g % 2, 0, c * P:(c + 1) * P], ident)
                last.then_inc(sem("aT_psum"), 1)

            def att_out(h):
                pe.wait_ge(sem("aT_ready"), 2 * h + 2)
                for c in range(4):
                    vt = [2, 3, 0, 1][c]
                    last = mm(B[5 + h // 2][:, (h % 2) * T:(h % 2 + 1) * T], v2[:, vt, h * P:(h + 1) * P],
                              paT[:, h % 2, c, :], start=(c == 0), stop=(c == 3))
                last.then_inc(sem("att_o"), 1)
                if h % 2:
                    pe.wait_ge(sem("att_sq"), h // 2 + 1)
                    mm(B[7][:, :], ones[:], sqf[:, (h // 2) * 512:(h // 2 + 1) * 512], start=True, stop=True).then_inc(sem("att_ss"), 1)
                    pe.wait_ge(sem("att_rms"), h // 2 + 1)

            pe.wait_ge(sem("const_in"), 32)
            pe.wait_ge(sem("vec_in"), NVEC)
            for l, n in ((0, V_ROWS), (1, V_ROWS), (2, W_ROWS)):
                last = nc.tensor.transpose(B[6][:, l * P:l * P + n], VN[0:n, l, :], ident[0:n, 0:n])
            last.then_inc(sem("vec_ready"), 1)
            pe.wait_ge(sem("x_in"), 16)
            for a in range(TT):
                transpose_in(XN[:, a * D:(a + 1) * D], a)
            pe.wait_ge(sem("c_act"), 1)
            pe.wait_ge(sem("ones_ready"), 1)
            pe.wait_ge(sem("vec_done"), 1)
            norm(0)
            for l in range(LAYERS):
                ada(f"ada{l}", 1)
                if l:
                    norm(2)
                mixer1(l)
                norm(2 * l + 1)
                pe.wait_ge(sem("h_norm"), 2 * l + 2)
                if l == 1:
                    route(0, 8, lambda k, a: hT1[:, k, a * P:(a + 1) * P])
                ffn(f"f{l}", lambda k: hT1[:, k, :])
                pe.wait_ge(sem("x_ready"), l + 1)
            norm(4)
            ada("ada2", 2)
            norm(5)
            pe.wait_ge(sem("ctx_in"), 16)
            pe.wait_ge(sem("ctx_go"), 1)
            for a in range(TT):
                transpose_in(CN[:, a * D:(a + 1) * D], a)
            norm(6)
            mixer2()
            norm(7)
            pe.wait_ge(sem("h_norm"), 8)
            route(1, 64, lambda k, a: hT1[:, k, a * P:(a + 1) * P])
            ffn("f2", lambda k: hT1[:, k, :])
            norm(8)
            pe.wait_ge(sem("h_norm"), 9)
            for a in range(TT):
                for k in range(KD):
                    last = nc.tensor.transpose(B[2 * a + k // 4][:, (k % 4) * P:(k % 4 + 1) * P],
                                               xT[:, k, a * P:(a + 1) * P], ident)
                last.then_inc(sem("outT_ready"), 1)

        plain_at = {}
        for name in ("ada0", "win0", "wout0", "ada1", "win1", "wout1", "ada2", "win2", "wout2"):
            plain_at[name] = marks[name][1]

        @block.scalar
        def _(act):
            fn = nc.scalar.activation
            count = [0]

            def link(ins):
                count[0] += 1
                ins.then_inc(sem("act_chain"), 1)
                act.wait_ge(sem("act_chain"), count[0])

            eps = small[:, 20:21]
            one = small[:, 21:22]

            def norm(n, src):
                if n >= 1:
                    act.wait_ge(sem("h_norm"), n)
                fn(sq[:, :, :], src, ACT.Square).then_inc(sem("sq_ready"), 1)
                act.wait_ge(sem("ss_ready"), n + 1)
                fn(rstd[:], B[6][:, 0:T], ACT.Sqrt, bias=eps, scale=1.0 / D).then_inc(sem("rms_ready"), 1)

            def ffn(ph):
                t0, steps = base[ph], STEPS[ph]

                def tile(j, m, i=0):
                    act.wait_ge(sem("h_ready"), i * (2 * U) + (t0 + 2 * j + m + 1))
                    fn(ffn_s[:, m, :], B[4 + m][:, 0:T], ACT.Silu).then_inc(sem("s_ready"), 1)

                with act.Fori(0, steps // U) as i:
                    for j in range(U):
                        tile(j, 0, i)
                        tile(j, 1, i)
                for s in range(steps // U * U, steps):
                    tile(s, 0)
                    tile(s, 1)

            def mixer1(l):
                act.wait_ge(sem("flow_ready"), l + 1)
                fn(flT, B[4][0:16, 0:T], ACT.Copy).then_inc(sem("flT_ready"), 1)
                W = plain_at[f"win{l}"]
                for j in range(10):
                    act.wait_ge(sem("plain_used"), W + j + 1)
                    b = B[j % 4]
                    if j == 0:
                        ins = fn(qT, b[:, :], ACT.Copy, scale=0.125)
                    elif j == 1:
                        ins = fn(kT, b[:, :], ACT.Copy)
                    elif j in (2, 3):
                        c = 2 * (j - 2)
                        ins = fn(upad[:, c:c + 2, 3:], b[:, :].rearrange("p (c t) -> p c t", c=2), ACT.Copy)
                    elif j in (4, 5):
                        ins = fn(vn[:, :, (j - 4) * CW:(j - 3) * CW], b[:, :].rearrange("p (a f) -> p a f", a=2), ACT.Copy)
                    elif j in (6, 7):
                        ins = fn(gT[:, (j - 6) * 512:(j - 5) * 512], b[:, :], ACT.Silu)
                    else:
                        ins = fn(gate[:, (j - 8) * 512:(j - 7) * 512], b[:, :], ACT.Gelu_apprx_tanh)
                    ins.then_inc(sem("z_in"), 1)
                    if j == 1:
                        act.wait_ge(sem("lf_ready"), l + 1)
                        for m in range(2):
                            fn(tmp1[:, m * T:(m + 1) * T], B[5][:, m * T:(m + 1) * T], ACT.Abs,
                               bias=VT[:, l, V_BG + m:V_BG + m + 1]).then_inc(sem("act_chain"), 1)
                        count[0] += 2
                        act.wait_ge(sem("act_chain"), count[0])
                        link(fn(tmp1, tmp1, ACT.Exp, scale=-1.0))
                        fn(tmp1, tmp1, ACT.Ln, bias=one).then_inc(sem("lsig_ready"), 1)
                    if j == 5:
                        gla_exps(l)
                    if j == 6:
                        for g in range(4):
                            act.wait_ge(sem("rgate_ready"), 4 * l + g + 1)
                            bank, dst, row, pair = ((4, rr, V_BA, 0), (5, rr, V_BA, 1), (6, ri, V_BX, 0), (4, ri, V_BX, 1))[g]
                            for m in range(2):
                                c = 2 * pair + m
                                ins = fn(dst[:, c * T:(c + 1) * T], B[bank][:, m * T:(m + 1) * T], ACT.Sigmoid,
                                         bias=VT[:, l, row + c:row + c + 1])
                            ins.then_inc(sem("rgate_done"), 1)
                        act.wait_ge(sem("rgate_done"), 4 * l + 4)
                        for c in range(4):
                            ins = fn(ra[:, c * T:(c + 1) * T], rr[:, c * T:(c + 1) * T], ACT.Exp,
                                     scale=small[:, 64 + 4 * l + c:65 + 4 * l + c])
                        for c in range(4):
                            ins = fn(rm[:, c * T:(c + 1) * T], rr[:, c * T:(c + 1) * T], ACT.Tanh,
                                     scale=small[:, 48 + 4 * l + c:49 + 4 * l + c])
                        ins.then_inc(sem("rtanh_ready"), 1)
                        act.wait_ge(sem("rm2_ready"), l + 1)
                        fn(rm, rm, ACT.Sqrt).then_inc(sem("rmult_ready"), 1)
                act.wait_ge(sem("kendn_ready"), l + 1)
                fn(kendn[:, :, :], B[4][:, :].rearrange("p (a f) -> p a f", a=2), ACT.Copy).then_inc(sem("kendn_done"), 1)
                for b in range(2):
                    act.wait_ge(sem("gla_o_ready"), 2 * l + b + 1)
                    fn(sqf[:, b * 512:(b + 1) * 512], B[2 + b][:, :], ACT.Square).then_inc(sem("gla_sq_ready"), 1)
                for b in range(2):
                    act.wait_ge(sem("gla_ss_ready"), 2 * l + b + 1)
                    fn(sc_sig[:, b * 512:(b + 1) * 512], B[b][:, :], ACT.Sqrt, bias=eps, scale=1.0 / P).then_inc(sem("gla_rms"), 1)

            def gla_exps(l):
                act.wait_ge(sem("bdiff_ready"), l + 1)
                fn(qloc, d1, ACT.Exp, scale=1.0 / 16)
                fn(kloc, d1, ACT.Exp, scale=-1.0 / 16)
                fn(kend, d2, ACT.Exp, scale=1.0 / 16)
                fn(qin, lfs, ACT.Exp, scale=1.0 / 16)
                fn(small[:, 128:128 + 8], blast, ACT.Exp, scale=1.0 / 16).then_inc(sem("gla_e_ready"), 1)

            def mixer2():
                W = plain_at["win2"]
                for j in range(12):
                    act.wait_ge(sem("plain_used"), W + j + 1)
                    b0, b1 = B[2 * (j % 2)], B[2 * (j % 2) + 1]
                    if j == 0:
                        ins = fn(rq[:, :, :], b0[:, :].rearrange("p (h t) -> p h t", h=2), ACT.Copy)
                    elif j == 1:
                        fn(rk[:, :, :], b0[:, :].rearrange("p (h t) -> p h t", h=2), ACT.Copy, scale=0.125)
                        ins = fn(rkn[:, :, :], b1[:, :].rearrange("p (h t) -> p h t", h=2), ACT.Copy, scale=0.125)
                    elif j in (2, 3, 6, 7):
                        dst, c = (rv, j - 2) if j < 4 else (v2, j - 6)
                        fn(dst[:, 0:2, c * CW:(c + 1) * CW], b0[:, :].rearrange("p (h t) -> p h t", h=2), ACT.Copy)
                        ins = fn(dst[:, 2:4, c * CW:(c + 1) * CW], b1[:, :].rearrange("p (h t) -> p h t", h=2), ACT.Copy)
                    elif j in (4, 5):
                        c = 2 * (j - 4)
                        for m, b in enumerate((b0, b1)):
                            fn(k2[:, c + m, 0:T], b[:, T:2 * T], ACT.Copy)
                            ins = fn(k2[:, c + m, T:2 * T], b[:, 0:T], ACT.Copy)
                    elif j in (8, 9):
                        c = 2 * (j - 8)
                        ins = fn(q2[:, c:c + 2, :], b0[:, :].rearrange("p (h t) -> p h t", h=2), ACT.Copy, scale=0.125)
                    else:
                        c = 2 * (j - 10)
                        ins = fn(rg[:, c:c + 2, :], b0[:, :].rearrange("p (h t) -> p h t", h=2), ACT.Silu)
                    ins.then_inc(sem("z2_in"), 1)
                for dr in range(2):
                    for pr in range(2):
                        ins = fn(qdec[:, dr, pr, :], C[:, (C_UP, C_DOWN)[dr]:(C_UP, C_DOWN)[dr] + T], ACT.Exp,
                                 scale=small[:, 80 + 2 * dr + pr:81 + 2 * dr + pr])
                ins.then_inc(sem("qdec_exp"), 1)
                for dr in range(2):
                    for a in range(2):
                        ins = fn(small[:, 96 + 8 * dr + 4 * a:100 + 8 * dr + 4 * a], small[:, 72 + 4 * dr:76 + 4 * dr], ACT.Exp,
                                 scale=C[:, C_TOK + 2 * dr + a:C_TOK + 2 * dr + a + 1])
                ins.then_inc(sem("kw_ready"), 1)
                act.wait_ge(sem("s2_psum"), 1)
                fn(S2[:, :, :, :], B[6][:, :].rearrange("p (h r v) -> p h r v", h=2, r=2), ACT.Copy).then_inc(sem("S2_ready"), 1)
                for b in range(2):
                    act.wait_ge(sem("ret_o"), 2 * b + 2)
                    if b == 0:
                        act.wait_ge(sem("ret_o"), 4)
                    fn(sqf[:, b * 512:(b + 1) * 512], B[2 + b][:, :], ACT.Square).then_inc(sem("ret_sq"), 1)
                for b in range(2):
                    act.wait_ge(sem("ret_ss"), b + 1)
                    fn(hflat[:, b * 512:(b + 1) * 512], B[b][:, :], ACT.Sqrt, bias=eps, scale=1.0 / P).then_inc(sem("ret_rms"), 1)
                act.wait_ge(sem("ret_done"), 4)
                for g in range(8):
                    for m in range(2):
                        act.wait_ge(sem("nmax_ready"), 2 * g + m + 1)
                        fn(pex[:, g % 2, m, :], B[2 * (g % 2) + m][:, :], ACT.Exp, bias=small[:, 144 + 2 * g + m:145 + 2 * g + m],
                           accum_out=small[:, 160 + 2 * g + m:161 + 2 * g + m]).then_inc(sem("p_ready"), 1)
                    if g >= 1:
                        att_copy(g - 1)
                    if g == 5:
                        att_norm(0)
                att_copy(7)
                att_norm(1)

            def att_copy(g):
                h, a = g // 2, g % 2
                act.wait_ge(sem("aT_psum"), g + 1)
                if h >= 2 and a == 0:
                    act.wait_ge(sem("att_o"), h - 1)
                fn(paT[:, h % 2, :, a * P:(a + 1) * P], B[4][:, :].rearrange("p (c t) -> p c t", c=4), ACT.Copy).then_inc(sem("aT_ready"), 1)

            def att_norm(b):
                act.wait_ge(sem("att_o"), 2 * b + 2)
                fn(sqf[:, b * 512:(b + 1) * 512], B[5 + b][:, :], ACT.Square).then_inc(sem("att_sq"), 1)
                act.wait_ge(sem("att_ss"), b + 1)
                fn(sqf[:, 1024 + b * 512:1024 + (b + 1) * 512], B[7][:, :], ACT.Sqrt, bias=eps, scale=1.0 / P).then_inc(sem("att_rms"), 1)

            act.dma_start(C[:], cst).then_inc(sem("const_in"), 16)
            act.dma_start(mixT[:, :, :].rearrange("p k t -> p (k t)"), rel).then_inc(sem("const_in"), 16)
            act.dma_start(XN.rearrange("p (a d) -> p a d", a=TT), A["x"].rearrange("b (a p) d -> p (b a) d", p=P)).then_inc(sem("x_in"), 16)
            act.wait_ge(sem("small_set"), 1)
            act.wait_ge(sem("vec_done"), 1)
            link(fn(small[:, 24:32], VT[:, 0, V_EXTRA:V_EXTRA + 8], ACT.Silu))
            sview = small[:, 32:48].rearrange("p (k v) -> p v k", v=2)
            link(fn(sview[:, 0, :], VT[:, 2, W_C:W_C + 8], ACT.Silu))
            fn(sview[:, 1, :], VT[:, 2, W_CC:W_CC + 8], ACT.Silu).then_inc(sem("c_act"), 1)
            for a in range(TT):
                act.wait_ge(sem("xin_ready"), a + 1)
                for half in range(2):
                    ins = fn(xT[:, 4 * half:4 * half + 4, a * P:(a + 1) * P],
                             B[2 * a + half][:, :].rearrange("p (k t) -> p k t", k=4), ACT.Copy)
                ins.then_inc(sem("x_copied"), 1)
            act.wait_ge(sem("x_copied"), 2)
            norm(0, xT[:, :, :])
            act.wait_ge(sem("vec_in"), NVEC)
            act.wait_ge(sem("lam_dot"), 1)
            link(fn(small[:, 368:384], small[:, 0:16], ACT.Abs))
            fn(small[:, 384:400], small[:, 368:384], ACT.Exp, scale=-1.0).then_inc(sem("sp_exp"), 1)
            fn(small[:, 186:188], small[:, 184:186], ACT.Exp).then_inc(sem("lam_exp"), 1)
            act.wait_ge(sem("lg_ready"), 1)
            for h in range(HEADS):
                if h:
                    act.wait_ge(sem("D_ready"), h)
                for dr in range(2):
                    ins = fn(TMP[:, 4096 + dr * 512:4096 + (dr + 1) * 512], mixT[:, 2 * dr:2 * dr + 2, :].rearrange("p k t -> p (k t)"), ACT.Exp,
                             scale=small[:, 72 + 4 * dr + h:73 + 4 * dr + h])
                ins.then_inc(sem("Dexp_ready"), 1)
            for l in range(LAYERS):
                if l:
                    act.wait_ge(sem("x_ready"), 1)
                    norm(2, xT[:, :, :])
                mixer1(l)
                act.wait_ge(sem("x_part"), 4 * l + 4)
                norm(2 * l + 1, xT[:, :, :])
                if l == 1:
                    act.wait_ge(sem("top_diff"), 1)
                    fn(small[:, 400:402], small[:, 402:404], ACT.Exp).then_inc(sem("top_exp"), 1)
                    act.wait_ge(sem("gatesT_copied"), 1)
                    act.dma_start(gates_dram[0, 0:8, :], TMP[0:8, 0:T]).then_inc(sem("gates_stored"), 16)
                ffn(f"f{l}")
            act.wait_ge(sem("x_ready"), 2)
            norm(4, xT[:, :, :])
            act.wait_ge(sem("x_ready"), 3)
            act.dma_start(CN.rearrange("p (a d) -> p a d", a=TT), A["ctx_2"].rearrange("b (a p) d -> p (b a) d", p=P)).then_inc(sem("ctx_in"), 16)
            norm(5, xT[:, :, :])
            ctxT = mixT
            for a in range(TT):
                act.wait_ge(sem("xin_ready"), 2 + a + 1)
                for half in range(2):
                    ins = fn(ctxT[:, 4 * half:4 * half + 4, a * P:(a + 1) * P],
                             B[2 * a + half][:, :].rearrange("p (k t) -> p k t", k=4), ACT.Copy)
                ins.then_inc(sem("x_copied"), 1)
            act.wait_ge(sem("x_copied"), 4)
            norm(6, ctxT[:, :, :])
            act.wait_ge(sem("h_norm"), 7)
            mixer2()
            act.wait_ge(sem("x_part"), 12)
            norm(7, xT[:, :, :])
            act.wait_ge(sem("logits_ready"), 2)
            fn(TMP[:, 0:128], B[7][:, 0:128], ACT.Sigmoid).then_inc(sem("top_exp"), 1)
            act.wait_ge(sem("gatesT_copied"), 2)
            act.dma_start(gates_dram[1, 0:64, :], TMP[0:64, 2048:2048 + T]).then_inc(sem("gates_stored"), 16)
            ffn("f2")
            act.wait_ge(sem("x_ready"), 4)
            norm(8, xT[:, :, :])
            act.wait_ge(sem("stored"), 16)

        @block.vector
        def _(dve):
            V = nc.vector
            count = [0]

            def link(ins):
                count[0] += 1
                ins.then_inc(sem("dve_chain"), 1)
                dve.wait_ge(sem("dve_chain"), count[0])

            def done(ins, name, n):
                ins.then_inc(sem(name), 1)
                dve.wait_ge(sem(name), n)

            def recip(v):
                link(V.reciprocal(v, v))

            def scale_cols(row, l, v, sc_at, dst):
                link(V.tensor_scalar(dst, modc[:, v, sc_at:sc_at + 8], 1.0, None, ALU.add))
                link(V.tensor_tensor(dst, dst, VT[:, l, row:row + 8], ALU.mult))

            def norm(n, src, dst, gain, shift=None):
                dve.wait_ge(sem("rms_ready"), n + 1)
                recip(rstd[:])
                link(V.tensor_tensor(sq[:, :, :], src, rstd[:].unsqueeze(1).to_broadcast([P, KD, T]), ALU.mult))
                for k in range(KD):
                    if shift is None:
                        ins = V.tensor_scalar(dst(k), sq[:, k, :], gain[:, k:k + 1], None, ALU.mult)
                    else:
                        ins = V.tensor_scalar(dst(k), sq[:, k, :], gain[:, k:k + 1], shift[:, k:k + 1], ALU.mult, ALU.add)
                done(ins, "h_norm", n + 1)

            def ada(name, l, nv):
                dve.wait_ge(sem("plain_used"), plain_at[name] + 24)
                src = B[7][:, 0:48 * nv].rearrange("p (m v) -> p v m", v=nv)
                for v in range(nv):
                    link(V.tensor_tensor(modc[:, v, :], src[:, v, :], VT[:, l, V_ADAB:V_ADAB + 48], ALU.add))

            gcol = small[:, 376:384]
            gcol_f = small[:, 384:392]

            def ffn(ph):
                t0, steps = base[ph], STEPS[ph]
                gated = ph in GATED
                g0 = {j: len(range(j, 88, U)) for j in range(U)} if ph == "f2" else {}

                def tile(j, m, i=0, gated=gated):
                    dve.wait_ge(sem("s_ready"), i * (2 * U) + (t0 + 2 * j + m + 1))
                    if gated:
                        if m == 0:
                            dve.wait_ge(gate_sem[j % U], (i + (j // U + 1 + g0.get(j % U, 0))) * 16)
                        V.tensor_tensor(ffn_s[:, m, :], ffn_s[:, m, :], ffn_g[:, j % U, :], ALU.mult).then_inc(sem("sg_ready"), 1)
                        dve.wait_ge(sem("sg_ready"), i * (2 * U) + (gbase + 2 * j + m + 1))
                    V.tensor_tensor(ffn_a[:, m, :], ffn_s[:, m, :], B[4 + m][:, T:2 * T], ALU.mult).then_inc(sem("a_ready"), 1)

                gbase = 0 if ph == "f1" else 176
                with dve.Fori(0, steps // U) as i:
                    for j in range(U):
                        tile(j, 0, i)
                        tile(j, 1, i)
                for s in range(steps // U * U, steps):
                    tile(s, 0, gated=gated and s < GATED[ph])
                    tile(s, 1, gated=gated and s < GATED[ph])

            def add_ffn(ph, nth, v):
                dve.wait_ge(sem("down_done"), base[ph] + 2 * STEPS[ph])
                for d in range(KD):
                    ins = V.scalar_tensor_tensor(out=xT[:, d, :], in0=B[d // 2][:, (d % 2) * T:(d % 2 + 1) * T],
                                                 scalar=modc[:, v, 40 + d:41 + d], in1=xT[:, d, :], op0=ALU.mult, op1=ALU.add)
                done(ins, "x_ready", nth)

            def add_mix(name, nth, banks):
                for j in range(4):
                    dve.wait_ge(sem("plain_used"), plain_at[name] + j + 1)
                    for m in range(2):
                        d = 2 * j + m
                        ins = V.scalar_tensor_tensor(out=xT[:, d, :], in0=B[banks[j % len(banks)]][:, m * T:(m + 1) * T],
                                                     scalar=modc[:, 0, 16 + d:17 + d], in1=xT[:, d, :], op0=ALU.mult, op1=ALU.add)
                    ins.then_inc(sem("x_part"), 1)
                dve.wait_ge(sem("x_part"), 4 * nth + 4)

            def mixer1(l):
                link(V.memset(upad[:, :, 0:3], 0.0))
                link(V.memset(sT[:, :, :], 0.0))
                dve.wait_ge(sem("lsig_ready"), l + 1)
                for m in range(2):
                    link(V.tensor_scalar(d1[:, m * T:(m + 1) * T], B[5][:, m * T:(m + 1) * T],
                                         VT[:, l, V_BG + m:V_BG + m + 1], 0.0, ALU.add, ALU.min))
                done(V.tensor_tensor(d1, d1, tmp1, ALU.subtract), "lf_done", l + 1)
                for m in range(2):
                    link(V.tensor_tensor_scan(lfs[:, m * T:(m + 1) * T], C[:, C_SCAN:C_SCAN + T], d1[:, m * T:(m + 1) * T],
                                              0.0, ALU.mult, ALU.add))
                b3 = lfs.rearrange("p (n t) -> p n t", t=CH)
                link(V.tensor_tensor(d1.rearrange("p (n t) -> p n t", t=CH), b3, b3[:, :, CH // 2 - 1:CH // 2].to_broadcast([P, 8, CH]), ALU.subtract))
                link(V.tensor_copy(blast.unsqueeze(2), b3[:, :, CH - 1:CH]))
                link(V.tensor_tensor(d2.rearrange("p (n t) -> p n t", t=CH), b3[:, :, CH - 1:CH].to_broadcast([P, 8, CH]), b3, ALU.subtract))
                V.tensor_copy(small[:, 22:23], small[:, 20:21]).then_inc(sem("bdiff_ready"), 1)
                dve.wait_ge(sem("z_in"), 10 * l + 4)
                for c in range(4):
                    o = uc[:, c * T:(c + 1) * T]
                    link(V.tensor_scalar(o, upad[:, c, 0:T], VT[:, l, V_CONVW + c:V_CONVW + c + 1],
                                         VT[:, l, V_CONVB + c:V_CONVB + c + 1], ALU.mult, ALU.add))
                    for tap in range(1, 4):
                        w = V_CONVW + 4 * tap + c
                        ins = V.scalar_tensor_tensor(out=o, in0=upad[:, c, tap:tap + T], scalar=VT[:, l, w:w + 1], in1=o,
                                                     op0=ALU.mult, op1=ALU.add)
                        link(ins) if (c, tap) != (3, 3) else done(ins, "conv_ready", l + 1)
                dve.wait_ge(sem("gla_e_ready"), l + 1)
                for o, z in ((qloc, qT), (kloc, kT), (kend, kT), (qin, qT)):
                    ins = V.tensor_tensor(o, o, z, ALU.mult)
                ins.then_inc(sem("gla_in"), 1)
                dve.wait_ge(sem("rtanh_ready"), l + 1)
                link(V.tensor_scalar(rr, rm, 1.0, None, ALU.add))
                recip(rr)
                V.scalar_tensor_tensor(out=rm, in0=rm, scalar=2.0, in1=rr, op0=ALU.mult, op1=ALU.mult).then_inc(sem("rm2_ready"), 1)
                dve.wait_ge(sem("rmult_ready"), l + 1)
                link(V.memset(rm.rearrange("p (c t) -> p c t", c=4)[:, :, 0:1], 1.0))
                link(V.tensor_tensor(rm, rm, ri, ALU.mult))
                link(V.tensor_tensor(rm, rm, uc, ALU.mult))
                for c in range(4):
                    s = slice(c * T, (c + 1) * T)
                    link(V.tensor_tensor_scan(rr[:, s], ra[:, s], rm[:, s], 0.0, ALU.mult, ALU.add))
                dve.wait_ge(sem("z_in"), 10 * l + 10)
                link(V.tensor_tensor(mixT[:, 0:4, :].rearrange("p k t -> p (k t)"), rr, gate, ALU.mult))
                mask = C[:, C_CAUS:C_CAUS + P].bitcast(U32).unsqueeze(1).to_broadcast([P, 2, P])
                s5 = sT[:, :, :].rearrange("p a (h r t) -> p r h a t", h=2, r=2)
                for par in range(2):
                    dve.wait_ge(sem("gla_s_ready"), 2 * l + par + 1)
                    for h2 in range(2):
                        ins = V.copy_predicated(s5[:, par, h2], mask,
                                                B[par][:, h2 * T:(h2 + 1) * T].rearrange("p (a t) -> p a t", a=TT))
                    ins.then_inc(sem("gla_sT_done"), 1)
                dve.wait_ge(sem("gla_u_ready"), l + 1)
                for n in range(NCH - 1):
                    src = B[5 + n % 2][:, (n // 2) * T:(n // 2 + 1) * T].rearrange("p (a v) -> p a v", a=2)
                    if n == 0:
                        ins = V.tensor_copy(St[:, 0, :, :], src)
                    else:
                        for pr in range(2):
                            ins = V.scalar_tensor_tensor(out=St[:, n, pr, :], in0=St[:, n - 1, pr, :],
                                                         scalar=small[:, 128 + pr * 4 + n:129 + pr * 4 + n],
                                                         in1=src[:, pr, :], op0=ALU.mult, op1=ALU.add)
                    done(ins, "state_ready", 3 * l + n + 1)
                for b in range(2):
                    dve.wait_ge(sem("gla_rms"), 2 * l + b + 1)
                    s = slice(b * 512, (b + 1) * 512)
                    recip(sc_sig[:, s])
                    g2 = gT.rearrange("p (h r t) -> p r h t", h=2, r=2)[:, b]
                    link(V.scalar_tensor_tensor(out=g2, in0=g2, scalar=VT[:, l, V_GLAG:V_GLAG + 1],
                                                in1=sc_sig[:, s].rearrange("p (h t) -> p h t", h=2), op0=ALU.mult, op1=ALU.mult))
                    ins = V.tensor_tensor(mixT[:, 4:8, :].rearrange("p (h r) t -> p r h t", r=2)[:, b],
                                          B[2 + b][:, :].rearrange("p (h t) -> p h t", h=2), g2, ALU.mult)
                done(ins, "mix_ready", l + 1)
                add_mix(f"wout{l}", l, [4, 5, 6])

            def softplus():
                x, y, s, s2, p = (small[:, 0:16], small[:, 384:400], small[:, 400:416], small[:, 416:432],
                                  small[:, 432:448])
                dve.wait_ge(sem("sp_exp"), 1)
                link(V.tensor_scalar(s2, y, 2.0, None, ALU.add))
                recip(s2)
                link(V.tensor_tensor(s, y, s2, ALU.mult))
                link(V.tensor_tensor(s2, s, s, ALU.mult))
                link(V.tensor_scalar(p, s2, 1.0 / 17, None, ALU.mult))
                for n in (15, 13, 11, 9, 7, 5, 3):
                    link(V.scalar_tensor_tensor(out=p, in0=p, scalar=1.0 / n, in1=s2, op0=ALU.add, op1=ALU.mult))
                link(V.scalar_tensor_tensor(out=p, in0=p, scalar=1.0, in1=s, op0=ALU.add, op1=ALU.mult))
                link(V.tensor_scalar(y, x, -1.0, 0.0, ALU.mult, ALU.max))
                link(V.scalar_tensor_tensor(out=p, in0=p, scalar=2.0, in1=y, op0=ALU.mult, op1=ALU.add))
                link(V.tensor_scalar(small[:, 48:56], p[:, 0:8], 8.0, None, ALU.mult))
                link(V.tensor_scalar(small[:, 64:72], p[:, 0:8], -8.0, None, ALU.mult))
                link(V.tensor_scalar(small[:, 72:80], p[:, 8:16], -1.0, None, ALU.mult))
                for dr in range(2):
                    for pr in range(2):
                        for hh in range(2):
                            r = slice(64 * hh, 64 * hh + 64)
                            h = 2 * pr + hh
                            link(V.tensor_copy(small[r, 80 + 2 * dr + pr:81 + 2 * dr + pr], small[r, 72 + 4 * dr + h:73 + 4 * dr + h]))
                V.tensor_copy(small[:, 22:23], small[:, 20:21]).then_inc(sem("lg_ready"), 1)

            def decays():
                for h in range(HEADS):
                    dve.wait_ge(sem("Dexp_ready"), h + 1)
                    ef, eb = TMP[:, 4096:4608], TMP[:, 4608:5120]
                    link(V.tensor_tensor(ef, ef, mixT[:, 4:6, :].rearrange("p k t -> p (k t)"), ALU.mult))
                    link(V.tensor_tensor(eb, eb, mixT[:, 6:8, :].rearrange("p k t -> p (k t)"), ALU.mult))
                    done(V.tensor_tensor(Dret[:, h, :], ef, eb, ALU.add), "D_ready", h + 1)

            def top2_gates():
                dve.wait_ge(sem("logits_ready"), 1)
                lg = TMP[:, 512:528].rearrange("p (a e) -> p a e", a=2)
                link(V.tensor_copy(lg, B[7][:, 0:16].rearrange("p (a e) -> p a e", a=2)))
                top = TMP[:, 528:544].rearrange("p (a e) -> p a e", a=2)
                idx = TMP[:, 544:560].bitcast(U32).rearrange("p (a e) -> p a e", a=2)
                idf = TMP[:, 560:576].rearrange("p (a e) -> p a e", a=2)
                for a in range(TT):
                    link(V.max(top[:, a, :], lg[:, a, :]))
                    link(V.max_index(idx[:, a, :], top[:, a, :], lg[:, a, :]))
                    link(V.tensor_copy(idf[:, a, :], idx[:, a, :]))
                    link(V.tensor_tensor(small[:, 402 + a:403 + a], top[:, a, 1:2], top[:, a, 0:1], ALU.subtract))
                V.tensor_copy(small[:, 22:23], small[:, 20:21]).then_inc(sem("top_diff"), 1)
                dve.wait_ge(sem("top_exp"), 1)
                link(V.tensor_scalar(small[:, 404:406], small[:, 400:402], 1.0, None, ALU.add))
                recip(small[:, 404:406])
                link(V.tensor_tensor(small[:, 406:408], small[:, 404:406], small[:, 400:402], ALU.mult))
                for a in range(TT):
                    g = small[:, 512 + 64 * a:520 + 64 * a]
                    t8 = TMP[:, 576:584]
                    io = C[:, C_IOTA:C_IOTA + 8]
                    link(V.tensor_scalar(g, io, idf[:, a, 0:1], small[:, 404 + a:405 + a], ALU.is_equal, ALU.mult))
                    link(V.tensor_scalar(t8, io, idf[:, a, 1:2], small[:, 406 + a:407 + a], ALU.is_equal, ALU.mult))
                    link(V.tensor_tensor(g, g, t8, ALU.add))
                V.tensor_copy(small[:, 22:23], small[:, 20:21]).then_inc(sem("gates_ready"), 1)
                dve.wait_ge(sem("gatesT_ready"), 1)
                V.tensor_copy(TMP[0:8, 0:T], B[7][0:8, P:P + T]).then_inc(sem("gatesT_copied"), 1)

            def one_hot_sum(dst, idf, n, width):
                io = C[:, C_IOTA:C_IOTA + width]
                link(V.tensor_scalar(dst, io, idf[:, 0:1], None, ALU.is_equal))
                for j in range(1, n):
                    link(V.scalar_tensor_tensor(out=dst, in0=io, scalar=idf[:, j:j + 1], in1=dst, op0=ALU.is_equal, op1=ALU.add))

            def group_gates():
                dve.wait_ge(sem("top_exp"), 2)
                for a in range(TT):
                    sc = TMP[:, 64 * a:64 * a + 64]
                    sel = TMP[:, 128:192]
                    t8 = TMP[:, 192:256].rearrange("p (g e) -> p g e", g=8)
                    gs, tg, gm = TMP[:, 256:264], TMP[:, 264:272], TMP[:, 272:280]
                    ix = TMP[:, 280:288].bitcast(U32)
                    idf = TMP[:, 288:296]
                    msk = TMP[:, 320:384]
                    link(V.tensor_tensor(sel, sc, small[:, 192:256], ALU.add))
                    for g in range(8):
                        link(V.max(t8[:, g, :], sel[:, 8 * g:8 * g + 8]))
                    link(V.tensor_tensor(gs.unsqueeze(2), t8[:, :, 0:1], t8[:, :, 1:2], ALU.add))
                    link(V.max(tg, gs))
                    link(V.max_index(ix, tg, gs))
                    link(V.tensor_copy(idf, ix))
                    one_hot_sum(gm, idf, 4, 8)
                    s3 = sel.rearrange("p (g e) -> p g e", g=8)
                    link(V.tensor_tensor(s3, s3, gm.unsqueeze(2).to_broadcast([P, 8, 8]), ALU.mult))
                    link(V.tensor_scalar(gm, gm, -1.0, 3e38, ALU.add, ALU.mult))
                    link(V.tensor_tensor(s3, s3, gm.unsqueeze(2).to_broadcast([P, 8, 8]), ALU.add))
                    link(V.max(tg, sel))
                    link(V.max_index(ix, tg, sel))
                    link(V.tensor_copy(idf, ix))
                    one_hot_sum(msk, idf, 8, 64)
                    g = small[:, 512 + 64 * a:576 + 64 * a]
                    link(V.tensor_tensor(g, sc, msk, ALU.mult))
                    link(V.tensor_reduce(gs[:, 0:1], g, AX, ALU.add))
                    recip(gs[:, 0:1])
                    link(V.tensor_scalar(g, g, gs[:, 0:1], 2.5, ALU.mult, ALU.mult))
                V.tensor_copy(small[:, 22:23], small[:, 20:21]).then_inc(sem("gates_ready"), 1)
                dve.wait_ge(sem("gatesT_ready"), 2)
                V.tensor_copy(TMP[0:64, 2048:2048 + T], B[7][0:64, P:P + T]).then_inc(sem("gatesT_copied"), 1)

            def mixer2():
                dve.wait_ge(sem("z2_in"), 12)
                cos = C[:, C_COS:C_COS + T].unsqueeze(1).to_broadcast([P, 2, T])
                sin = C[:, C_SIN:C_SIN + T].unsqueeze(1).to_broadcast([P, 2, T])
                rt = rope_t.rearrange("p (h t) -> p h t", h=2)
                for g in range(6):
                    z = [rq[:, :, :], rk[:, :, :], k2[:, 0:2, T:], k2[:, 2:4, T:], q2[:, 0:2, :], q2[:, 2:4, :]][g]
                    dve.wait_ge(sem("rot_ready"), g + 1)
                    link(V.tensor_tensor(rt, B[4 + g % 2][:, :].rearrange("p (h t) -> p h t", h=2), sin, ALU.mult))
                    link(V.tensor_tensor(z, z, cos, ALU.mult))
                    done(V.tensor_tensor(z, z, rt, ALU.add), "rope_done", g + 1)
                    if g == 0:
                        dve.wait_ge(sem("qdec_exp"), 1)
                        for dr in range(2):
                            link(V.tensor_tensor(qdec[:, dr, :, :], qdec[:, dr, :, :], rq[:, :, :], ALU.mult))
                        V.tensor_copy(small[:, 22:23], small[:, 20:21]).then_inc(sem("qdec_ready"), 1)
                        dve.wait_ge(sem("kw_ready"), 1)
                        for dr in range(2):
                            w = small[:, 96 + 8 * dr:104 + 8 * dr].rearrange("p (a h) -> p a h", a=2)
                            for a in range(2):
                                ins = V.tensor_tensor(kdec[:, dr, a, :].rearrange("p (h d) -> p h d", h=HEADS),
                                                      rkn[:, a, :].rearrange("p (h d) -> p h d", h=HEADS),
                                                      w[:, a, :].unsqueeze(2).to_broadcast([P, HEADS, 64]), ALU.mult)
                        ins.then_inc(sem("kdec_ready"), 1)
                for h in range(HEADS):
                    dve.wait_ge(sem("ret_s"), h + 1)
                    if h >= 2:
                        dve.wait_ge(sem("ret_o"), h - 1)
                    V.tensor_tensor(sD[:, h % 2, :], B[h % 2][:, :], Dret[:, h, :], ALU.mult).then_inc(sem("sD_ready"), 1)
                for b in range(2):
                    dve.wait_ge(sem("ret_rms"), b + 1)
                    s = slice(b * 512, (b + 1) * 512)
                    recip(hflat[:, s])
                    r2 = rg[:, :, :].rearrange("p (h r) t -> p r h t", r=2)[:, b]
                    link(V.scalar_tensor_tensor(out=r2, in0=r2, scalar=VT[:, 2, W_RG:W_RG + 1],
                                                in1=hflat[:, s].rearrange("p (h t) -> p h t", h=2), op0=ALU.mult, op1=ALU.mult))
                    done(V.tensor_tensor(mixT[:, 4:8, :].rearrange("p (h r) t -> p r h t", r=2)[:, b],
                                         B[2 + b][:, :].rearrange("p (h t) -> p h t", h=2), r2, ALU.mult),
                         "ret_done", 2 * b + 1)
                    done(V.tensor_copy(small[:, 23:24], small[:, 20:21]), "ret_done", 2 * b + 2)
                for g in range(8):
                    for m in range(2):
                        dve.wait_ge(sem("att_s"), 2 * g + m + 1)
                        V.tensor_reduce(small[:, 144 + 2 * g + m:145 + 2 * g + m], B[2 * (g % 2) + m][:, :], AX, ALU.max,
                                        negate=True).then_inc(sem("nmax_ready"), 1)
                    if g >= 1:
                        combine(g - 1)
                    if g == 6:
                        att_norm(0)
                combine(7)
                att_norm(1)
                add_mix("wout2", 2, [0, 1, 2, 3])

            def combine(g):
                dve.wait_ge(sem("p_ready"), 2 * g + 2)
                rs = small[:, 176:178]
                link(V.reciprocal(rs, small[:, 160 + 2 * g:162 + 2 * g]))
                link(V.tensor_tensor(rs[:, 1:2], rs[:, 1:2], small[:, 188:189], ALU.mult))
                link(V.tensor_scalar(pex[:, g % 2, 1, :], pex[:, g % 2, 1, :], rs[:, 1:2], None, ALU.mult))
                done(V.scalar_tensor_tensor(out=pex[:, g % 2, 0, :], in0=pex[:, g % 2, 0, :], scalar=rs[:, 0:1],
                                            in1=pex[:, g % 2, 1, :], op0=ALU.mult, op1=ALU.subtract), "a2_ready", g + 1)

            def att_norm(b):
                dve.wait_ge(sem("att_rms"), b + 1)
                s = sqf[:, 1024 + b * 512:1024 + (b + 1) * 512]
                recip(s)
                ins = V.scalar_tensor_tensor(out=mixT[:, 2 * b:2 * b + 2, :].rearrange("p k t -> p (k t)"), in0=B[5 + b][:, :],
                                             scalar=small[:, 189:190], in1=s, op0=ALU.mult, op1=ALU.mult)
                if b:
                    done(ins, "mix_ready", 3)
                else:
                    link(ins)

            link(V.memset(small[:, 16:24], EPS))
            link(V.memset(small[:, 21:22], 1.0))
            dve.wait_ge(sem("vec_ready"), 1)
            link(V.tensor_copy(VT[:, 0:2, 0:V_ROWS], B[6][:, 0:2 * P].rearrange("p (l r) -> p l r", l=2)[:, :, 0:V_ROWS]))
            done(V.tensor_copy(VT[:, 2, 0:W_ROWS], B[6][:, 2 * P:2 * P + W_ROWS]), "vec_done", 1)
            link(V.tensor_copy(small[:, 0:4], VT[:, 0, V_LAM:V_LAM + 4]))
            link(V.tensor_copy(small[:, 4:8], VT[:, 1, V_LAM:V_LAM + 4]))
            V.tensor_copy(small[:, 22:23], small[:, 20:21]).then_inc(sem("small_set"), 1)
            dve.wait_ge(sem("vec_in"), NVEC)
            for k in range(2):
                v = small[:, 256 + 128 * k:256 + 128 * k + 64]
                w = small[:, 320 + 128 * k:320 + 128 * k + 64]
                link(V.tensor_tensor(v, v, w, ALU.mult))
                link(V.tensor_reduce(small[:, 184 + k:185 + k], v, AX, ALU.add))
            V.tensor_copy(small[:, 22:23], small[:, 20:21]).then_inc(sem("lam_dot"), 1)
            softplus()
            dve.wait_ge(sem("lam_exp"), 1)
            link(V.tensor_tensor(small[:, 188:189], small[:, 186:187], small[:, 187:188], ALU.subtract))
            link(V.tensor_scalar(small[:, 188:189], small[:, 188:189], LAM_INIT, None, ALU.add))
            link(V.tensor_scalar(small[:, 189:190], VT[:, 2, W_DG:W_DG + 1], 1.0 - LAM_INIT, None, ALU.mult))
            decays()
            for l in range(LAYERS):
                ada(f"ada{l}", l, 1)
                scale_cols(V_G1, l, 0, 8, gcol)
                scale_cols(V_G2, l, 0, 32, gcol_f)
                norm(2 * l, xT[:, :, :], lambda k: hT1[:, k, :], gcol, modc[:, 0, 0:8])
                mixer1(l)
                norm(2 * l + 1, xT[:, :, :], lambda k: hT1[:, k, :], gcol_f, modc[:, 0, 24:32])
                if l == 1:
                    top2_gates()
                ffn(f"f{l}")
                add_ffn(f"f{l}", l + 1, 0)
            norm(4, xT[:, :, :], lambda k: xT[:, k, :], VT[:, 1, V_EXTRA:V_EXTRA + 8])
            V.tensor_copy(small[:, 22:23], small[:, 20:21]).then_inc(sem("x_ready"), 1)
            ada("ada2", 2, 2)
            scale_cols(V_G1, 2, 0, 8, gcol)
            norm(5, xT[:, :, :], lambda k: hcat[:, k, 0:T], gcol, modc[:, 0, 0:8])
            V.tensor_copy(small[:, 22:23], small[:, 20:21]).then_inc(sem("ctx_go"), 1)
            scale_cols(V_G1, 2, 1, 8, gcol)
            norm(6, mixT[:, :, :], lambda k: hcat[:, k, T:2 * T], gcol, modc[:, 1, 0:8])
            scale_cols(V_G2, 2, 0, 32, gcol_f)
            mixer2()
            norm(7, xT[:, :, :], lambda k: hT1[:, k, :], gcol_f, modc[:, 0, 24:32])
            group_gates()
            ffn("f2")
            add_ffn("f2", 4, 0)
            norm(8, xT[:, :, :], lambda k: xT[:, k, :], VT[:, 2, W_FG:W_FG + 8])
            for a in range(TT):
                dve.wait_ge(sem("outT_ready"), a + 1)
                for half in range(2):
                    ins = V.tensor_copy(hflat[:, a * D + half * 512:a * D + (half + 1) * 512], B[2 * a + half][:, :])
                ins.then_inc(sem("out_tile"), 1)


_INS = [
    "x", "c", "ada_w", "ada_b", "norm_mix_g", "norm_ffn_g", "w_in", "rg_conv_w", "rg_conv_b", "rg_wa", "rg_ba", "rg_wx",
    "rg_bx", "rg_lambda", "gla_wg2", "gla_bg", "gla_norm_g", "w_out", "ffn_w1", "ffn_w3", "ffn_w2", "router_w",
    "moe_w1", "moe_w3", "moe_w2", "final_g", "c_2", "ctx_2", "c_ctx_2", "ada_w_2", "ada_b_2", "norm1_g_2", "w_in_2",
    "lambda_q1_2", "lambda_k1_2", "lambda_q2_2", "lambda_k2_2", "dattn_norm_g_2", "ret_decay_fwd_2",
    "ret_decay_bwd_2", "ret_norm_g_2", "w_out_2", "norm2_g_2", "router_w_2", "router_bias_2", "exp_w1_2",
    "exp_w3_2", "exp_w2_2", "shared_w1_2", "shared_w3_2", "shared_w2_2", "final_norm_g_2",
]


def kernel(**inputs):
    import numpy as _np
    import concourse.bacc as _bacc
    from concourse import mybir as _mybir
    from concourse.bass_utils import run_bass_kernel_spmd as _run

    nc = _bacc.Bacc("TRN2", target_bir_lowering=False, num_devices=1)
    arrays, A = {}, {}
    for name in _INS:
        a = _np.ascontiguousarray(inputs[name])
        if a.ndim == 1 and name == "c_ctx_2":
            a = a.reshape(1, -1)
        arrays[f"in_{name}"] = a
        A[name] = nc.dram_tensor(f"in_{name}", a.shape, F32, kind="ExternalInput").ap()
    A["c_ctx_2"] = A["c_ctx_2"][0]
    extra = {}
    for name, a in zip(("constants", "relative"), constants()):
        arrays[name] = a
        extra[name] = nc.dram_tensor(name, a.shape, F32, kind="ExternalInput").ap()
    gates = nc.dram_tensor("gates", (2, 64, T), F32).ap()
    out = nc.dram_tensor("out", (1, T, D), F32, kind="ExternalOutput").ap()
    build(nc, A, extra["constants"], extra["relative"], gates, out)
    r = _run(nc, [arrays], core_ids=[0])
    return r.results[0]["out"]
```

```python
from contextlib import ExitStack

import concourse.bass as bass
from concourse import mybir

F32 = mybir.dt.float32
U32 = mybir.dt.uint32
ALU = mybir.AluOpType
ACT = mybir.ActivationFunctionType
AX = mybir.AxisListType.X

P = 128
T = 256
TT = T // P
D = 1024
KD = D // P
CW = 256
RING = 9
U = RING // 3
LAYERS = 2
RG = 512
CH = 64
NCH = T // CH
FF = 2816
EPS = 1e-6
LAM_INIT = 0.2
HEADS = 4
CLASSES = (128, 256)
E1, STEPS1, A1 = 8, FF // CW, 2 * T
E2, A2 = 64, 8 * T

C_ID, C_ROT, C_COS, C_SIN, C_SCAN, C_CAUS, C_UP, C_DOWN, C_TOK, C_IOTA = (
    0, 128, 256, 512, 768, 1024, 1152, 1408, 1664, 1668)
C_SU = C_IOTA + T
C_N = C_SU + P
V_ADAB, V_G1, V_G2 = 0, 48, 56
V_CONVW, V_CONVB, V_BA, V_BX, V_LAM, V_BG, V_GLAG, V_EXTRA = 64, 80, 84, 88, 92, 96, 98, 99
V_ROWS = 107
W_DG, W_RG, W_FG, W_C, W_CC = 64, 65, 66, 74, 82
W_ROWS = 90


def constants():
    import numpy as np
    c = np.zeros((P, C_N), np.float32)
    c[:, C_ID:C_ID + P] = np.eye(P)
    for p in range(P):
        if (p // 16) % 2 == 0:
            c[p + 16, C_ROT + p] = -1.0
        else:
            c[p - 16, C_ROT + p] = 1.0
    t = np.arange(T)
    inv = (10000.0 ** (-np.arange(16, dtype=np.float32) / 16)).astype(np.float32)
    for p in range(P):
        pos = (t // 64 if (p // 32) % 2 == 0 else t % 64).astype(np.float32)
        ang = pos * inv[p % 16]
        c[p, C_COS:C_COS + T] = np.cos(ang)
        c[p, C_SIN:C_SIN + T] = np.sin(ang)
    c[:, C_SCAN:C_SCAN + T] = (t % CH != 0)
    j = np.arange(P)[:, None]
    i = np.arange(P)[None, :]
    c[:, C_CAUS:C_CAUS + P] = (i >= j) & (i // CH == j // CH)
    c[:, C_UP:C_UP + T] = t + 1
    c[:, C_DOWN:C_DOWN + T] = T - t
    for jt in range(TT):
        tok = np.arange(P) + jt * P
        c[:, C_TOK + jt] = T - 1 - tok
        c[:, C_TOK + TT + jt] = tok
    c[:, C_IOTA:C_IOTA + T] = t
    c[:, C_SU:C_SU + P] = j < i
    r = np.zeros((P, 4, TT, T), np.float32)
    for jt in range(TT):
        rel = t[None, :] - (np.arange(P)[:, None] + jt * P)
        r[:, 0, jt], r[:, 1, jt] = np.maximum(rel, 0), np.maximum(-rel, 0)
        r[:, 2, jt], r[:, 3, jt] = rel >= 0, rel <= 0
    return c, r.reshape(P, -1)


def build(nc, A, cst, rel, out):
    with ExitStack() as ctx:
        def sb(name, shape, dt=F32):
            return ctx.enter_context(nc.sbuf_tensor(name, shape, dt))

        sems = {}

        def sem(name):
            if name not in sems:
                sems[name] = ctx.enter_context(nc.semaphore(name))
            return sems[name]

        SLOT = KD * CW
        arena = sb("arena", [P, RING * SLOT + 11264 + 3 * 2048])
        TMP = arena[:, RING * SLOT:RING * SLOT + 11264]
        o3 = RING * SLOT + 11264
        mixf, Dretf, sqf = (arena[:, o3 + 2048 * n:o3 + 2048 * (n + 1)] for n in range(3))
        mixT = mixf.rearrange("p (k t) -> p k t", k=KD)
        Dret = Dretf.rearrange("p (h t) -> p h t", h=HEADS)
        sq = sqf.rearrange("p (k t) -> p k t", k=KD)
        xT = sb("xT", [P, KD, T])
        hcat = sb("hcat", [P, KD, 2 * T])
        hT = hcat[:, :, 0:T]
        hflat = hcat[:, :, :].rearrange("p k t -> p (k t)")
        C = sb("C", [P, C_N])
        VT = sb("VT", [P, 3, P])
        VN = sb("VN", [P, 3, P])
        rstd = sb("rstd", [P, T])
        ffn_s = sb("ffn_s", [P, 2, T])
        ffn_a = sb("ffn_a", [P, 2, T])
        ffn_g = sb("ffn_g", [P, 4, T])
        ones = sb("ones", [P, P])
        small = sb("small", [P, 640])
        modc = sb("modc", [P, 4, 48])
        router = sb("router", [P, KD, 64])
        wf = sb("wf", [P, KD, 16])
        wa_bd = sb("wa_bd", [P, 4, P])
        wx_bd = sb("wx_bd", [P, 4, P])
        wg2 = sb("wg2", [16, T])
        hn = sb("hn", [P, TT, D])
        rank_t = sb("rank_t", [P, TT, E2])
        meta = sb("meta", [P, 2, E2], mybir.dt.int32)
        ident = C[:, C_ID:C_ID + P]

        B = [ctx.enter_context(nc.psum_tensor(f"B{i}", [P, 512], F32)) for i in range(8)]

        at = [0]

        def cut(n, **dims):
            v = TMP[:, at[0]:at[0] + n]
            at[0] += n
            return v

        UPW = T + 3
        upad = cut(4 * UPW).rearrange("p (c t) -> p c t", c=4)
        gate = cut(1024)
        qT = cut(512)
        kT = cut(512)
        gT = cut(1024)
        vn = cut(1024).rearrange("p (a f) -> p a f", a=TT)
        qloc, kloc, qin, kend = cut(512), cut(512), cut(512), cut(512)
        kendn = cut(512).rearrange("p (a f) -> p a f", a=TT)
        sT = cut(1024).rearrange("p (a f) -> p a f", a=TT)
        St = cut(3 * 256).rearrange("p (n a v) -> p n a v", n=3, a=2)
        uc = cut(1024)
        sc_sig = uc
        blast = cut(8)
        assert at[0] <= 11264
        rr, ri = hflat[:, 2048:3072], hflat[:, 3072:4096]
        hT1 = hflat[:, 0:2048].rearrange("p (k t) -> p k t", k=KD)
        d1, d2, lfs, tmp1 = sqf[:, 0:512], sqf[:, 512:1024], sqf[:, 1024:1536], sqf[:, 1536:2048]
        ra = ffn_g[:, :, :].rearrange("p s t -> p (s t)")
        rm = mixT[:, 4:8, :].rearrange("p k t -> p (k t)")
        flT = ffn_s[0:16, 0, :]
        at[0] = 0
        q2 = cut(1024).rearrange("p (h t) -> p h t", h=HEADS)
        k2 = cut(2048).rearrange("p (h t) -> p h t", h=HEADS)
        v2 = cut(2048).rearrange("p (a f) -> p a f", a=4)
        rq = cut(512).rearrange("p (h t) -> p h t", h=2)
        rk = cut(512).rearrange("p (h t) -> p h t", h=2)
        rkn = cut(512).rearrange("p (a f) -> p a f", a=2)
        rv = cut(2048).rearrange("p (a f) -> p a f", a=4)
        rg = cut(1024).rearrange("p (h t) -> p h t", h=HEADS)
        qdec = cut(1024).rearrange("p (r h t) -> p r h t", r=2, h=2)
        S2 = cut(512).rearrange("p (h r v) -> p h r v", h=2, r=2)
        assert at[0] <= 11264
        kdec = sqf[:, 0:1024].rearrange("p (r a f) -> p r a f", r=2, a=2)
        sD = sqf[:, 1024:2048].rearrange("p (b f) -> p b f", b=2)
        pex = hflat[:, 0:2048].rearrange("p (b m f) -> p b m f", b=2, m=2)
        paT = hflat[:, 2048:4096].rearrange("p (b c t) -> p b c t", b=2, c=4)
        rope_t = ffn_a[:, :, :].rearrange("p b t -> p (b t)")

        heT = hflat[:, 2048:4096]
        Pe = ffn_g[:, 0:2, :]
        y1 = TMP[:, 0:KD * (A1 + T)].rearrange("p (k s) -> p k s", k=KD)
        w1s = TMP[:, 6144:6144 + 2 * (A1 + T)].rearrange("p (a s) -> p a s", a=TT)
        o2 = 6 * SLOT
        y2 = arena[:, o2:o2 + KD * (A2 + T)].rearrange("p (k s) -> p k s", k=KD)
        w2s = arena[:, o2 + KD * (A2 + T):o2 + (KD + 2) * (A2 + T)].rearrange("p (a s) -> p a s", a=TT)
        RT = TMP[:, 8192:]
        rank = rank_t[:, :, :]
        gts = small[:, 512:640].rearrange("p (a e) -> p a e", a=TT)
        msk = RT[:, 2304:2304 + 2 * E2].rearrange("p (a e) -> p a e", a=TT)
        mskx = RT[:, 2432:2432 + 2 * E2].rearrange("p (a e) -> p a e", a=TT)
        Yn = heT.rearrange("p (b d) -> p b d", b=2)
        PTs = ffn_g[:, 2:4, :]

        def cols(w, c0):
            return w.rearrange("(k p) f -> p k f", p=P)[:, :, c0:c0 + CW]

        WIN1 = [1024, 1280, 0, 256, 1536, 1792, 2048, 2304, 512, 768]
        WIN2 = [1536, 1792, 2048, 2304, 512, 768, 1024, 1280, 0, 256, 2560, 2816]
        stream, uses, last_in = [], [0] * RING, [None] * RING
        n_plain = [0]

        def add(what, release, slot=None):
            if slot is None:
                slot = (stream[-1]["slot"] + 1) % RING if stream else 0
            uses[slot] += 1
            stream.append(dict(what=what, release=release, slot=slot, use=uses[slot], before=last_in[slot]))
            last_in[slot] = len(stream) - 1

        def plain(w, c0):
            n_plain[0] += 1
            add(cols(w, c0), ("plain_used", n_plain[0]))

        marks, base, tile0 = {}, {}, [0]
        ADA_UNITS = 24 // 2
        units = [("ada0", u) for u in range(ADA_UNITS)]
        for u in range(ADA_UNITS):
            units += [("ada1", u), ("ada2", 2 * u), ("ada2", 2 * u + 1)]
        unit_pieces, n_ada = [], [0]
        F0_STEPS = FF // CW
        F0_UNITS = ADA_UNITS + 24

        def add_unit():
            name, u = units[len(unit_pieces)]
            w = A["ada_w_2"][0] if name == "ada2" else A["ada_w"][int(name[-1])]
            js = (u,) if name == "ada2" else (2 * u, 2 * u + 1)
            unit_pieces.append([len(stream) + i for i in range(len(js))])
            for j in js:
                n_ada[0] += 1
                add(cols(w, j * CW), ("ada_used", n_ada[0]))

        def units_after(f):
            upto = lambda f: min(F0_UNITS, (f * F0_UNITS + 20) // 21)
            return range(ADA_UNITS + upto(f), ADA_UNITS + upto(f + 1))

        def mark(name):
            marks[name] = (len(stream), n_plain[0])
            base[name] = tile0[0]

        def steps_of(ph, n, first_slot=None, wrap=None):
            mark(ph)
            for s in range(n):
                for part in range(3):
                    slot = None if wrap is None else (first_slot + 3 * wrap(s) + part) % (3 * 3 if ph == "f1" else 6)
                    name = "down_done" if part == 2 else "h_ready"
                    add((ph, s, part), (name, tile0[0] + 2 * s + 2), slot)
            tile0[0] += 2 * n

        for u in range(ADA_UNITS):
            add_unit()
        step_at = {}
        for l in range(LAYERS):
            mark(f"win{l}")
            for c0 in WIN1:
                plain(A["w_in"][l], c0)
            mark(f"wout{l}")
            for j in range(4):
                plain(A["w_out"][l], j * CW)
            if l == 0:
                mark("f0")
                step_at["f0"] = []
                for st in range(F0_STEPS):
                    step_at["f0"].append(len(stream))
                    for part in range(3):
                        add(("f0", st, part), ("down_done" if part == 2 else "h_ready", 2 * st + 2))
                    for f in (2 * st, 2 * st + 1):
                        for _ in units_after(f):
                            add_unit()
                    assert len(stream) - step_at["f0"][-1] + 2 <= RING + 2
                tile0[0] += 2 * F0_STEPS
            else:
                steps_of("f1", E1 * STEPS1, 0, lambda s: s % STEPS1 % 3)
        mark("win2")
        for c0 in WIN2:
            plain(A["w_in_2"][0], c0)
        mark("wout2")
        for j in range(4):
            plain(A["w_out_2"][0], j * CW)
        step_at["sh"] = [len(stream)]
        steps_of("sh", 1, 0, lambda s: 0)
        steps_of("f2", E2, 3, lambda s: s % 2)
        piece_sem = [sem(f"piece_in_{i}") for i in range(RING)]

        def ffn_weights(ph, s):
            if ph == "f0":
                w1, w3, w2, c = A["ffn_w1"][0], A["ffn_w3"][0], A["ffn_w2"][0], s
            elif ph == "f1":
                e, c = s
                w1, w3, w2 = A["moe_w1"][0][e], A["moe_w3"][0][e], A["moe_w2"][0][e]
            elif ph == "sh":
                w1, w3, w2, c = A["shared_w1_2"][0], A["shared_w3_2"][0], A["shared_w2_2"][0], 0
            else:
                w1, w3, w2, c = A["exp_w1_2"][0][s], A["exp_w3_2"][0][s], A["exp_w2_2"][0][s], 0
            v1, v3 = (w.rearrange("(k p) f -> p k f", p=P) for w in (w1, w3))
            v2_ = w2.rearrange("(c k p) n -> c p k n", p=P, k=2)
            if isinstance(c, int):
                return v1[:, :, c * CW:(c + 1) * CW], v3[:, :, c * CW:(c + 1) * CW], v2_[c]
            return v1[:, :, bass.ts(c, CW)], v3[:, :, bass.ts(c, CW)], v2_[c]

        def slot_view(n):
            return arena[:, stream[n]["slot"] * SLOT:(stream[n]["slot"] + 1) * SLOT]

        def piece(n):
            return slot_view(n).rearrange("p (k f) -> p k f", k=KD)

        def piece_down(n):
            return slot_view(n).rearrange("p (k f) -> p k f", k=2)

        def arrived(eng, n, later=0):
            eng.wait_ge(piece_sem[stream[n]["slot"]], (later + stream[n]["use"]) * 16)

        def uses_per_expert(n):
            return 4 if stream[n]["slot"] < 6 else 3

        def unit_pieces_before(n):
            return sum(len(p) for p in unit_pieces[:n])

        block = ctx.enter_context(nc.Block())

        @block.sync
        def _(sp):
            def load(n):
                p = stream[n]
                if p["before"] is not None:
                    name, value = stream[p["before"]]["release"]
                    sp.wait_ge(sem(name), value)
                if isinstance(p["what"], tuple):
                    ph, s, part = p["what"]
                    dst = piece_down(n) if part == 2 else piece(n)
                    src = ffn_weights(ph, (s // STEPS1, s % STEPS1) if ph == "f1" else s)[part]
                else:
                    dst, src = piece(n), p["what"]
                sp.dma_start(dst, src).then_inc(piece_sem[p["slot"]], 16)

            def load_loop(ph, count, step):
                n0 = marks[ph][0]
                tiles = 2 * step(0, 0)[1]
                pieces = tiles // 2 * 3
                for n in range(n0, n0 + pieces):
                    load(n)
                with sp.Fori(1, count) as i:
                    for n in range(n0 + pieces, n0 + 2 * pieces):
                        name, value = stream[stream[n]["before"]]["release"]
                        sp.wait_ge(sem(name), i * tiles + (value - tiles))
                        part = (n - n0) % 3
                        dst = piece_down(n) if part == 2 else piece(n)
                        sp.dma_start(dst, ffn_weights(ph, step(i, (n - n0 - pieces) // 3)[0])[part])\
                          .then_inc(piece_sem[stream[n]["slot"]], 16)

            for n in range(marks["f1"][0]):
                load(n)
            load_loop("f1", E1, lambda i, s: ((i, s), STEPS1))
            for n in range(marks["win2"][0], marks["f2"][0]):
                load(n)
            load_loop("f2", E2 // 2, lambda i, s: (i * 2 + s, 2))
            sp.wait_ge(sem("out_tile"), 2)
            sp.dma_start(out.rearrange("b (a p) d -> p (b a) d", p=P),
                         hflat[:, 0:2048].rearrange("p (a d) -> p a d", a=TT)).then_inc(sem("stored"), 16)
            sp.wait_ge(sem("stored"), 16)

        XN, CN = TMP[:, 0:2048], TMP[:, 2048:4096]

        @block.gpsimd
        def _(pool):
            nc.gpsimd.memset(ones[:], 1.0).then_inc(sem("ones_ready"), 1)
            nc.gpsimd.memset(wa_bd[:], 0.0).then_inc(sem("pool_zero"), 1)
            nc.gpsimd.memset(wx_bd[:], 0.0).then_inc(sem("pool_zero"), 1)

            def rows(l, row, ap):
                n = ap.shape[0]
                pool.dma_start(VN[row:row + n, l, :], ap).then_inc(sem("vec_in"), 16)

            for l in range(LAYERS):
                rows(l, V_ADAB, A["ada_b"][l].rearrange("(a p) -> a p", p=P))
                rows(l, V_G1, A["norm_mix_g"][l].rearrange("(a p) -> a p", p=P))
                rows(l, V_G2, A["norm_ffn_g"][l].rearrange("(a p) -> a p", p=P))
                rows(l, V_CONVW, A["rg_conv_w"][l].rearrange("w (a p) -> (w a) p", p=P))
                rows(l, V_CONVB, A["rg_conv_b"][l].rearrange("(a p) -> a p", p=P))
                rows(l, V_BA, A["rg_ba"][l].rearrange("(a p) -> a p", p=P))
                rows(l, V_BX, A["rg_bx"][l].rearrange("(a p) -> a p", p=P))
                rows(l, V_LAM, A["rg_lambda"][l].rearrange("(a p) -> a p", p=P))
                rows(l, V_BG, A["gla_bg"][l].rearrange("(a p) -> a p", p=P))
                rows(l, V_GLAG, A["gla_norm_g"][l].rearrange("(a p) -> a p", p=P))
                rows(l, V_EXTRA, (A["c"][0] if l == 0 else A["final_g"]).rearrange("(a p) -> a p", p=P))
            for row, name in ((V_ADAB, "ada_b_2"), (V_G1, "norm1_g_2"), (V_G2, "norm2_g_2"),
                              (W_DG, "dattn_norm_g_2"), (W_RG, "ret_norm_g_2"), (W_C, "c_2")):
                rows(2, row, A[name][0].rearrange("(a p) -> a p", p=P))
            rows(2, W_FG, A["final_norm_g_2"].rearrange("(a p) -> a p", p=P))
            rows(2, W_CC, A["c_ctx_2"].rearrange("(a p) -> a p", p=P))
            for k, name in enumerate(("ret_decay_fwd_2", "ret_decay_bwd_2")):
                pool.dma_start(small[:, 8 + 4 * k:12 + 4 * k],
                               A[name][0:1, :].to_broadcast([P, 4])).then_inc(sem("vec_in"), 16)
            for k, name in enumerate(("lambda_q1_2", "lambda_k1_2", "lambda_q2_2", "lambda_k2_2")):
                pool.dma_start(small[:, 256 + 64 * k:320 + 64 * k],
                               A[name][0:1, :].to_broadcast([P, 64])).then_inc(sem("vec_in"), 16)

            def layer_weights(l):
                s = sem("small_w_in")
                pool.dma_start(wf[:], A["w_in"][l].rearrange("(k p) f -> p k f", p=P)[:, :, 2560:2576]).then_inc(s, 16)
                pool.dma_start(wg2[:], A["gla_wg2"][l]).then_inc(s, 16)
                for bd, name in ((wa_bd, "rg_wa"), (wx_bd, "rg_wx")):
                    for half in range(2):
                        src = A[name][l].rearrange("(c b) d e -> b d c e", b=2)[half]
                        pool.dma_start(bd[64 * half:64 * half + 64, :, 64 * half:64 * half + 64],
                                       src).then_inc(s, 16)

            pool.wait_ge(sem("pool_zero"), 2)
            layer_weights(0)
            pool.dma_start(router[:, :, 0:8], A["router_w"][0].rearrange("(k p) f -> p k f", p=P)).then_inc(sem("router_in"), 16)
            pool.wait_ge(sem("gla_u_ready"), 1)
            layer_weights(1)
            pool.wait_ge(sem("logits_ready"), 1)
            pool.dma_start(router[:], A["router_w_2"][0].rearrange("(k p) f -> p k f", p=P)).then_inc(sem("router_in"), 16)
            pool.dma_start(small[:, 192:256], A["router_bias_2"][0:1, :].to_broadcast([P, 64])).then_inc(sem("router_in"), 16)

        def by_class(eng, c, body):
            for k, width in enumerate(CLASSES):
                with eng.If(c == k):
                    body(width)

        def load_meta(eng, row, e, most):
            return eng.value_load(meta[0:1, row, bass.ds(e, 1)], min_val=0, max_val=most)

        NVEC = 16 * (2 * 11 + 8 + 6)

        @block.tensor
        def _(pe):
            mm = nc.tensor.matmul

            def transpose_in(src, half):
                for k in range(KD):
                    last = nc.tensor.transpose(B[2 * half + k // 4][:, (k % 4) * P:(k % 4 + 1) * P],
                                               src[:, k * P:(k + 1) * P], ident)
                last.then_inc(sem("xin_ready"), 1)

            def ada_unit(n):
                name, u = units[n]
                pe.wait_ge(sem("ada_used"), unit_pieces_before(n + 1))
                for i in range(2):
                    for m in range(2):
                        o = 64 + 48 * i + 2 * u + m if name == "ada2" else 2 * (2 * u + i) + m
                        last = mm(B[7][:, o:o + 1], ffn_g[:, 2 * (n % 2) + i, m * P:(m + 1) * P], ones[:, 0:1],
                                  start=True, stop=True)
                last.then_inc(sem("ada_psum"), 1)

            def norm(n, bank=6):
                pe.wait_ge(sem("sq_ready"), n + 1)
                for k in range(KD):
                    last = mm(B[bank][:, 0:T], ones[:], sq[:, k, :], start=(k == 0), stop=(k == KD - 1))
                last.then_inc(sem("ss_ready"), 1)

            def project_T(n, bank, rhs, width=T):
                arrived(pe, n)
                w = piece(n)
                for m in range(2):
                    dst = B[bank[m]][:, 0:width] if width > T else B[bank][:, m * T:(m + 1) * T]
                    for k in range(KD):
                        last = mm(dst, w[:, k, m * P:(m + 1) * P], rhs[:, k, 0:width],
                                  start=(k == 0), stop=(k == KD - 1))
                last.then_inc(sem("plain_used"), 1)

            def project_nat(n, bank, lhs):
                arrived(pe, n)
                w = piece(n)
                for a in range(len(lhs)):
                    for k in range(KD):
                        last = mm(B[bank[a // 2]][:, (a % 2) * CW:(a % 2 + 1) * CW], lhs[a](k), w[:, k, :],
                                  start=(k == 0), stop=(k == KD - 1))
                last.then_inc(sem("plain_used"), 1)

            def out_proj(name, banks, release):
                n0 = marks[name][0]
                for j in range(4):
                    if j >= len(banks):
                        pe.wait_ge(*release(j))
                    arrived(pe, n0 + j)
                    w = piece(n0 + j)
                    for m in range(2):
                        for k in range(KD):
                            last = mm(B[banks[j % len(banks)]][:, m * T:(m + 1) * T], w[:, k, m * P:(m + 1) * P],
                                      mixT[:, k, :], start=(k == 0), stop=(k == KD - 1))
                    last.then_inc(sem("plain_used"), 1)

            def mixer1(l):
                pe.wait_ge(sem("h_norm"), 2 * l + 1)
                pe.wait_ge(sem("small_w_in"), 16 * 6 * (l + 1))
                for k in range(KD):
                    last = mm(B[4][0:16, 0:T], wf[:, k, :], hT1[:, k, :], start=(k == 0), stop=(k == KD - 1))
                last.then_inc(sem("flow_ready"), 1)
                n0 = marks[f"win{l}"][0]
                for j in range(10):
                    if j >= 4:
                        pe.wait_ge(sem("z_in"), 10 * l + j - 3)
                    if j in (4, 5):
                        project_nat(n0 + j, [j % 4], [lambda k, a=a: hT1[:, k, a * P:(a + 1) * P] for a in range(TT)])
                    else:
                        project_T(n0 + j, j % 4, hT1)
                    if j == 1:
                        pe.wait_ge(sem("flT_ready"), l + 1)
                        for m in range(2):
                            last = mm(B[5][:, m * T:(m + 1) * T], wg2[:, m * P:(m + 1) * P], flT[:, :], start=True, stop=True)
                        last.then_inc(sem("lf_ready"), 1)
                    if j == 6:
                        pe.wait_ge(sem("conv_ready"), l + 1)
                        pe.wait_ge(sem("lf_done"), l + 1)
                        for g, (bank, bd, pair) in enumerate(((4, wa_bd, 0), (5, wa_bd, 1), (6, wx_bd, 0), (4, wx_bd, 1))):
                            if g == 3:
                                pe.wait_ge(sem("rgate_done"), 4 * l + 1)
                            for m in range(2):
                                c = 2 * pair + m
                                last = mm(B[bank][:, m * T:(m + 1) * T], bd[:, c, :], uc[:, c * T:(c + 1) * T], start=True, stop=True)
                            last.then_inc(sem("rgate_ready"), 1)
                pe.wait_ge(sem("gla_in"), l + 1)
                pe.wait_ge(sem("rgate_done"), 4 * l + 4)
                for a in range(TT):
                    for pr in range(2):
                        last = nc.tensor.transpose(B[4][:, a * T + pr * P:a * T + (pr + 1) * P],
                                                   kend[:, pr * T + a * P:pr * T + (a + 1) * P], ident)
                last.then_inc(sem("kendn_ready"), 1)
                pe.wait_ge(sem("z_in"), 10 * l + 10)
                for par in range(2):
                    r = slice(64 * par, 64 * par + 64)
                    for o in range(0, 512, P):
                        last = mm(B[par][:, o:o + P], kloc[r, o:o + P], qloc[r, o:o + P], start=True, stop=True)
                    last.then_inc(sem("gla_s_ready"), 1)
                pe.wait_ge(sem("kendn_done"), l + 1)
                for n in range(NCH - 1):
                    for h in range(HEADS):
                        r = slice(64 * (n % 2), 64 * (n % 2) + 64)
                        bank, o = 5 + n % 2, (n // 2) * T + (h // 2) * P
                        last = mm(B[bank][64 * (h % 2):64 * (h % 2) + 64, o:o + P],
                                  kendn[r, n // 2, h * 64:(h + 1) * 64], vn[r, n // 2, h * P:(h + 1) * P],
                                  start=True, stop=True)
                last.then_inc(sem("gla_u_ready"), 1)
                pe.wait_ge(sem("gla_sT_done"), 2 * (l + 1))
                pe.wait_ge(sem("state_ready"), 3 * (l + 1))
                for h in range(HEADS):
                    rows = slice(64 * (h % 2), 64 * (h % 2) + 64)
                    for a in range(TT):
                        o = (h // 2) * T + a * P
                        bank = B[2 + h % 2]
                        last = mm(bank[:, o:o + P], vn[:, a, h * P:(h + 1) * P], sT[:, a, h * P:(h + 1) * P],
                                  start=True, stop=False, skip_group_check=True)
                        for n in range(max(2 * a, 1), 2 * a + 2):
                            oo = (h // 2) * T + n * CH
                            last = mm(bank[:, oo:oo + CH], St[rows, n - 1, h // 2, :],
                                      qin[rows, (h // 2) * T + n * CH:(h // 2) * T + (n + 1) * CH],
                                      start=False, stop=(n == 2 * a + 1), skip_group_check=True)
                    if h >= 2:
                        last.then_inc(sem("gla_o_ready"), 1)
                for b in range(2):
                    pe.wait_ge(sem("gla_sq_ready"), 2 * l + b + 1)
                    mm(B[b][:, :], ones[:], sqf[:, b * 512:(b + 1) * 512], start=True, stop=True).then_inc(sem("gla_ss_ready"), 1)
                pe.wait_ge(sem("mix_ready"), l + 1)
                out_proj(f"wout{l}", [4, 5, 6], lambda j: (sem("x_part"), 4 * l + 1))

            def route(l, E):
                pe.wait_ge(sem("router_in"), 16 if l == 0 else 48)
                for a in range(TT):
                    for k in range(KD):
                        last = mm(B[7][:, a * E:(a + 1) * E], hT1[:, k, a * P:(a + 1) * P], router[:, k, 0:E],
                                  start=(k == 0), stop=(k == KD - 1))
                last.then_inc(sem("logits_ready"), 1)
                for a in range(TT):
                    for k in range(KD):
                        last = nc.tensor.transpose(B[2 * a + k // 4][:, (k % 4) * P:(k % 4 + 1) * P],
                                                   hT1[:, k, a * P:(a + 1) * P], ident)
                    last.then_inc(sem("hn_psum"), 1)

            def places(l, E):
                pe.wait_ge(sem("mask_ready"), l + 1)
                su = C[:, C_SU:C_SU + P]
                for o, parts in ((0, ((ones[:], msk[:, 0, 0:E]), (ones[:], msk[:, 1, 0:E]))),
                                 (1, ((ones[:], mskx[:, 0, 0:E]), (ones[:], mskx[:, 1, 0:E]))),
                                 (2, ((su, msk[:, 0, 0:E]),)),
                                 (3, ((ones[:], msk[:, 0, 0:E]), (su, msk[:, 1, 0:E])))):
                    for n, (w, m) in enumerate(parts):
                        last = mm(B[7][:, o * E:(o + 1) * E], w, m, start=(n == 0), stop=(n == len(parts) - 1))
                last.then_inc(sem("places_psum"), 1)

            def up_tile(n, m, rhs, width, later=None, bank=4):
                for part in range(2):
                    if m == 0:
                        arrived(pe, n + part, 0 if later is None else later(n + part))
                    w = piece(n + part)
                    for k in range(KD):
                        last = mm(B[bank + m][:, part * T:part * T + width], w[:, k, m * P:(m + 1) * P], rhs(k),
                                  start=(k == 0), stop=(k == KD - 1))
                last.then_inc(sem("h_ready"), 1)

            def down_tile(n, m, a_value, width, first, last_tile, later=None):
                pe.wait_ge(sem("a_ready"), a_value)
                if m == 0:
                    arrived(pe, n + 2, 0 if later is None else later(n + 2))
                w = piece_down(n + 2)
                for d in range(KD):
                    o = d * width
                    last = mm(B[o // 512][:, o % 512:o % 512 + width], w[:, m, d * P:(d + 1) * P],
                              ffn_a[:, m, 0:width], start=(first and o % 512 == 0), stop=last_tile,
                              skip_group_check=True)
                last.then_inc(sem("down_done"), 1)

            def dense(ph):
                starts, t0 = step_at[ph], base[ph]
                tiles = 2 * len(starts)
                hh = lambda k: hT1[:, k, :]
                up_tile(starts[0], 0, hh, T)
                for f in range(tiles):
                    if f + 1 < tiles:
                        up_tile(starts[(f + 1) // 2], (f + 1) % 2, hh, T)
                    if ph == "f0" and f >= 1:
                        for n in units_after(f - 1):
                            ada_unit(n)
                    down_tile(starts[f // 2], f % 2, t0 + f + 1, T, f == 0, f + 1 == tiles)
                if ph == "f0":
                    for n in units_after(tiles - 1):
                        ada_unit(n)

            def gather(g0, e, width):
                pe.wait_ge(sem("Pe_ready"), e + (g0 + 1))
                for half in range(2):
                    if width == 256 and half == 1:
                        pe.wait_ge(sem("heT_ready"), e * 2 + (2 * g0 + 1))
                    for kk in range(4):
                        k = 4 * half + kk
                        o = (half * 512 if width <= P else 0) + kk * width
                        for a in range(TT):
                            last = mm(B[6 + o // 512][:, o % 512:o % 512 + width], hn[:, a, k * P:(k + 1) * P],
                                      Pe[:, a, 0:width], start=(a == 0), stop=(a == 1))
                    last.then_inc(sem("he_psum"), 1)

            def experts1():
                n0, t0 = marks["f1"][0], base["f1"]
                pe.wait_ge(sem("outs_read"), 2)
                pe.wait_ge(sem("meta_ready"), 1)
                with pe.Fori(0, E1) as e:
                    c = load_meta(pe, 0, e, 1)

                    def expert(width):
                        gather(0, e, width)
                        hh = lambda k: heT[:, k * width:(k + 1) * width]

                        def step(s, i=0, first=False, end=False):
                            n = n0 + 3 * s
                            later = lambda n: e * uses_per_expert(n) + i
                            av = e * (2 * STEPS1) + i * 6 + (t0 + 2 * s)
                            up_tile(n, 1, hh, width, later)
                            if first:
                                pe.wait_ge(sem("outs_read"), e + 2)
                            down_tile(n, 0, av + 1, width, first, False, later)
                            if not end:
                                up_tile(n + 3, 0, hh, width, later)
                            down_tile(n, 1, av + 2, width, False, end, later)

                        pe.wait_ge(sem("heT_ready"), e * 2 + 2)
                        up_tile(n0, 0, hh, width, lambda n: e * uses_per_expert(n))
                        for s in range(3):
                            step(s, first=(s == 0))
                        with pe.Fori(1, 3) as i:
                            for s in range(3):
                                step(s, i)
                        for s in range(9, STEPS1):
                            step(s, end=(s + 1 == STEPS1))

                    by_class(pe, c, expert)

            def experts2():
                n0, t0 = marks["f2"][0], base["f2"]

                def expert(e, j, i, last_one=False):
                    n = n0 + 3 * j
                    later = (lambda n: i) if i is not None else None
                    c = load_meta(pe, 0, e, 1)

                    def ups(width):
                        hh = lambda k: heT[:, k * width:(k + 1) * width]
                        pe.wait_ge(sem("heT_ready"), e * 2 + (2 * E1 + 2))
                        up_tile(n, 0, hh, width, later)
                        up_tile(n, 1, hh, width, later)

                    def downs(width):
                        pe.wait_ge(sem("outs_read"), e + (E1 + 5))
                        down_tile(n, 0, e * 2 + (t0 + 1), width, True, False, later)
                        down_tile(n, 1, e * 2 + (t0 + 2), width, False, True, later)

                    by_class(pe, c, ups)
                    if not last_one:
                        cn = load_meta(pe, 0, e + 1, 1)
                        by_class(pe, cn, lambda width: gather(E1, e + 1, width))
                    by_class(pe, c, downs)

                pe.wait_ge(sem("meta_ready"), 2)
                c0 = load_meta(pe, 0, 0, 1)
                by_class(pe, c0, lambda width: gather(E1, 0, width))
                with pe.Fori(0, E2 // 2 - 1) as i:
                    for j in range(2):
                        expert(i * 2 + j, j, i)
                for e in range(E2 - 2, E2):
                    expert(e, e, None, e == E2 - 1)

            def combine_slots(b0, blocks, y, ws):
                def turn(b):
                    if b:
                        pe.wait_ge(sem("block_in"), 2 * (b0 + b))
                    else:
                        pe.wait_ge(sem("outs_read"), E1 + 2 if y is y1 else E1 + 5 + E2)
                        pe.wait_ge(sem("w_kept"), E1 if y is y1 else E1 + E2)
                    for k in range(KD):
                        nc.tensor.transpose(B[4 + k // 4][:, (k % 4) * P:(k % 4 + 1) * P], y[:, k, b * P:(b + 1) * P], ident)
                    for a in range(TT):
                        last = nc.tensor.transpose(B[6][:, a * P:(a + 1) * P], ws[:, a, b * P:(b + 1) * P], ident)
                    last.then_inc(sem("block_psum"), 1)

                turn(0)
                for b in range(blocks):
                    if b + 1 < blocks:
                        turn(b + 1)
                    pe.wait_ge(sem("block_in"), 2 * (b0 + b + 1))
                    for k in range(KD):
                        last = mm(B[k // 2][:, (k % 2) * T:(k % 2 + 1) * T], Yn[:, b % 2, k * P:(k + 1) * P], PTs[:, b % 2, :],
                                  start=(b == 0 and k % 2 == 0), stop=(b + 1 == blocks), skip_group_check=True)
                    last.then_inc(sem("block_done"), 1)

            def mixer2():
                n0 = marks["win2"][0]
                pe.wait_ge(sem("h_norm"), 6)
                pe.wait_ge(sem("h_norm"), 7)
                x_t = [lambda k, a=a: hcat[:, k, a * P:(a + 1) * P] for a in range(4)]
                for j in range(12):
                    bk = [2 * (j % 2), 2 * (j % 2) + 1]
                    if j >= 2:
                        pe.wait_ge(sem("z2_in"), j - 1)
                    if j == 0:
                        project_T(n0, 0, hcat)
                    elif j == 1:
                        arrived(pe, n0 + 1)
                        w = piece(n0 + 1)
                        for m in range(2):
                            for k in range(KD):
                                mm(B[2][:, m * T:(m + 1) * T], w[:, k, m * P:(m + 1) * P], hcat[:, k, 0:T],
                                   start=(k == 0), stop=(k == KD - 1))
                        for a in range(2):
                            for k in range(KD):
                                last = mm(B[3][:, a * CW:(a + 1) * CW], hcat[:, k, (2 + a) * P:(3 + a) * P], w[:, k, :],
                                          start=(k == 0), stop=(k == KD - 1))
                        last.then_inc(sem("plain_used"), 1)
                    elif j in (2, 3, 6, 7):
                        project_nat(n0 + j, bk, x_t)
                    elif j in (4, 5):
                        project_T(n0 + j, bk, hcat, width=2 * T)
                    else:
                        project_T(n0 + j, bk[0], hcat)
                pe.wait_ge(sem("z2_in"), 12)
                for g in range(6):
                    if g >= 2:
                        pe.wait_ge(sem("rope_done"), g - 1)
                    for m in range(2):
                        src = [rq[:, m, :], rk[:, m, :], k2[:, m, T:], k2[:, 2 + m, T:], q2[:, m, :], q2[:, 2 + m, :]][g]
                        last = mm(B[4 + g % 2][:, m * T:(m + 1) * T], C[:, C_ROT:C_ROT + P], src, start=True, stop=True)
                    last.then_inc(sem("rot_ready"), 1)
                pe.wait_ge(sem("kdec_ready"), 1)
                for pr in range(2):
                    for dr in range(2):
                        for hh in range(2):
                            h = 2 * pr + hh
                            for a in range(2):
                                last = mm(B[6][64 * hh:64 * hh + 64, (pr * 2 + dr) * P:(pr * 2 + dr + 1) * P],
                                          kdec[:, dr, a, h * 64:(h + 1) * 64], rv[:, 2 + a, h * P:(h + 1) * P],
                                          start=(a == 0), stop=(a == 1))
                last.then_inc(sem("s2_psum"), 1)
                pe.wait_ge(sem("rope_done"), 2)
                for h in range(HEADS):
                    r = slice(64 * (h % 2), 64 * (h % 2) + 64)
                    if h >= 2:
                        pe.wait_ge(sem("sD_ready"), h - 1)
                    for a in range(2):
                        last = mm(B[h % 2][:, a * T:(a + 1) * T], rk[r, h // 2, a * P:(a + 1) * P], rq[r, h // 2, :],
                                  start=True, stop=True)
                    last.then_inc(sem("ret_s"), 1)
                    if h >= 1:
                        ret_out(h - 1)
                ret_out(HEADS - 1)
                for b in range(2):
                    pe.wait_ge(sem("ret_sq"), b + 1)
                    mm(B[b][:, :], ones[:], sqf[:, b * 512:(b + 1) * 512], start=True, stop=True).then_inc(sem("ret_ss"), 1)
                pe.wait_ge(sem("rope_done"), 6)
                pe.wait_ge(sem("ret_done"), 4)
                for g in range(8):
                    h, a = g // 2, g % 2
                    if g >= 2:
                        pe.wait_ge(sem("p_ready"), 2 * (g - 1))
                    for m in range(2):
                        r = slice(64 * m, 64 * m + 64)
                        mm(B[2 * (g % 2) + m][:, :], q2[r, h, a * P:(a + 1) * P], k2[r, h, :],
                           start=True, stop=True).then_inc(sem("att_s"), 1)
                    if g >= 1:
                        att_T(g - 1)
                    if g >= 3 and g % 2 == 1:
                        att_out((g - 3) // 2)
                att_T(7)
                att_out(3)
                pe.wait_ge(sem("mix_ready"), 3)
                out_proj("wout2", [0, 1, 2, 3], None)

            def ret_out(h):
                r = slice(64 * (h % 2), 64 * (h % 2) + 64)
                pe.wait_ge(sem("sD_ready"), h + 1)
                if h == 0:
                    pe.wait_ge(sem("S2_ready"), 1)
                    pe.wait_ge(sem("qdec_ready"), 1)
                dst = B[2 + h % 2][:, (h // 2) * T:(h // 2 + 1) * T]
                for a in range(2):
                    mm(dst, rv[:, a, h * P:(h + 1) * P], sD[:, h % 2, a * T:(a + 1) * T],
                       start=(a == 0), stop=False, skip_group_check=True)
                for dr in range(2):
                    last = mm(dst, S2[r, h // 2, dr, :], qdec[r, dr, h // 2, :], start=False, stop=(dr == 1),
                              skip_group_check=True)
                last.then_inc(sem("ret_o"), 1)

            def att_T(g):
                pe.wait_ge(sem("a2_ready"), g + 1)
                if g >= 1:
                    pe.wait_ge(sem("aT_ready"), g)
                for c in range(4):
                    last = nc.tensor.transpose(B[4][:, c * P:(c + 1) * P], pex[:, g % 2, 0, c * P:(c + 1) * P], ident)
                last.then_inc(sem("aT_psum"), 1)

            def att_out(h):
                pe.wait_ge(sem("aT_ready"), 2 * h + 2)
                for c in range(4):
                    vt = [2, 3, 0, 1][c]
                    last = mm(B[5 + h // 2][:, (h % 2) * T:(h % 2 + 1) * T], v2[:, vt, h * P:(h + 1) * P],
                              paT[:, h % 2, c, :], start=(c == 0), stop=(c == 3))
                last.then_inc(sem("att_o"), 1)
                if h % 2:
                    pe.wait_ge(sem("att_sq"), h // 2 + 1)
                    mm(B[7][:, :], ones[:], sqf[:, (h // 2) * 512:(h // 2 + 1) * 512], start=True, stop=True).then_inc(sem("att_ss"), 1)
                    pe.wait_ge(sem("att_rms"), h // 2 + 1)

            pe.wait_ge(sem("const_in"), 32)
            pe.wait_ge(sem("vec_in"), NVEC)
            for l, n in ((0, V_ROWS), (1, V_ROWS), (2, W_ROWS)):
                last = nc.tensor.transpose(B[6][:, l * P:l * P + n], VN[0:n, l, :], ident[0:n, 0:n])
            last.then_inc(sem("vec_ready"), 1)
            pe.wait_ge(sem("x_in"), 16)
            for a in range(TT):
                transpose_in(XN[:, a * D:(a + 1) * D], a)
            pe.wait_ge(sem("c_act"), 1)
            pe.wait_ge(sem("ones_ready"), 1)
            pe.wait_ge(sem("vec_done"), 1)
            norm(0)
            for n in range(ADA_UNITS):
                ada_unit(n)
            for l in range(LAYERS):
                if l:
                    norm(2)
                mixer1(l)
                norm(2 * l + 1)
                pe.wait_ge(sem("h_norm"), 2 * l + 2)
                if l == 0:
                    dense("f0")
                else:
                    route(0, E1)
                    places(0, E1)
                    experts1()
                    combine_slots(0, A1 // P, y1, w1s)
                pe.wait_ge(sem("x_ready"), l + 1)
            norm(4)
            norm(5)
            pe.wait_ge(sem("ctx_in"), 16)
            pe.wait_ge(sem("ctx_go"), 1)
            for a in range(TT):
                transpose_in(CN[:, a * D:(a + 1) * D], a)
            norm(6)
            mixer2()
            norm(7)
            pe.wait_ge(sem("h_norm"), 8)
            route(1, E2)
            pe.wait_ge(sem("outs_read"), E1 + 4)
            dense("sh")
            places(1, E2)
            experts2()
            combine_slots(A1 // P, A2 // P, y2, w2s)
            norm(8)
            pe.wait_ge(sem("h_norm"), 9)
            for a in range(TT):
                for k in range(KD):
                    last = nc.tensor.transpose(B[2 * a + k // 4][:, (k % 4) * P:(k % 4 + 1) * P],
                                               xT[:, k, a * P:(a + 1) * P], ident)
                last.then_inc(sem("outT_ready"), 1)

        plain_at = {}
        for name in ("win0", "wout0", "win1", "wout1", "win2", "wout2"):
            plain_at[name] = marks[name][1]

        @block.scalar
        def _(act):
            fn = nc.scalar.activation
            count = [0]

            def link(ins):
                count[0] += 1
                ins.then_inc(sem("act_chain"), 1)
                act.wait_ge(sem("act_chain"), count[0])

            eps = small[:, 20:21]
            one = small[:, 21:22]

            def norm(n, src):
                if n >= 1:
                    act.wait_ge(sem("h_norm"), n)
                fn(sq[:, :, :], src, ACT.Square).then_inc(sem("sq_ready"), 1)
                act.wait_ge(sem("ss_ready"), n + 1)
                fn(rstd[:], B[6][:, 0:T], ACT.Sqrt, bias=eps, scale=1.0 / D).then_inc(sem("rms_ready"), 1)

            def silu(m, value, width):
                act.wait_ge(sem("h_ready"), value)
                fn(ffn_s[:, m, 0:width], B[4 + m][:, 0:width], ACT.Silu).then_inc(sem("s_ready"), 1)

            def dense(ph):
                for f in range(2 * len(step_at[ph])):
                    silu(f % 2, base[ph] + f + 1, T)

            def rows_of_h(l):
                for a in range(TT):
                    act.wait_ge(sem("hn_psum"), 2 * l + a + 1)
                    for half in range(2):
                        ins = fn(hn[:, a, half * 512:(half + 1) * 512], B[2 * a + half][:, :], ACT.Copy)
                    ins.then_inc(sem("outs_read"), 1)

            def keep_gathered(g0, e, width):
                for half in range(2):
                    act.wait_ge(sem("he_psum"), e * 2 + (2 * g0 + half + 1))
                    if width <= P:
                        ins = fn(heT[:, half * 4 * width:(half + 1) * 4 * width], B[6 + half][:, 0:4 * width], ACT.Copy)
                    else:
                        for b in range(2):
                            ins = fn(heT[:, half * 1024 + b * 512:half * 1024 + (b + 1) * 512], B[6 + b][:, :], ACT.Copy)
                    ins.then_inc(sem("heT_ready"), 1)

            def keep_outputs(y, value, start, width):
                act.wait_ge(sem("down_done"), value)
                per = 512 // width
                for b in range(KD // per):
                    ins = fn(y[:, b * per:(b + 1) * per, bass.ds(start, width)],
                             B[b][:, :].rearrange("p (k s) -> p k s", k=per), ACT.Copy)
                ins.then_inc(sem("outs_read"), 1)

            def experts1():
                act.wait_ge(sem("meta_ready"), 1)
                t0 = base["f1"]
                fn(small[:, 19:20], small[:, 20:21], ACT.Silu)
                with act.Fori(0, E1) as e:
                    c = load_meta(act, 0, e, 1)
                    start = load_meta(act, 1, e, A1)

                    def expert(width):
                        keep_gathered(0, e, width)
                        with act.Fori(0, STEPS1) as s:
                            for m in range(2):
                                silu(m, e * (2 * STEPS1) + s * 2 + (t0 + m + 1), width)
                        keep_outputs(y1, e * (2 * STEPS1) + (t0 + 2 * STEPS1), start, width)

                    by_class(act, c, expert)

            def experts2():
                act.wait_ge(sem("meta_ready"), 2)
                t0 = base["f2"]

                def expert(e, last_one=False):
                    c = load_meta(act, 0, e, 1)
                    start = load_meta(act, 1, e, A2)

                    def silus(width):
                        for m in range(2):
                            silu(m, e * 2 + (t0 + m + 1), width)

                    by_class(act, c, silus)
                    if not last_one:
                        cn = load_meta(act, 0, e + 1, 1)
                        by_class(act, cn, lambda width: keep_gathered(E1, e + 1, width))
                    by_class(act, c, lambda width: keep_outputs(y2, e * 2 + (t0 + 2), start, width))

                c0 = load_meta(act, 0, 0, 1)
                by_class(act, c0, lambda width: keep_gathered(E1, 0, width))
                with act.Fori(0, E2 - 1) as e:
                    expert(e)
                expert(E2 - 1, last_one=True)

            def combine_slots(b0, blocks):
                for b in range(blocks):
                    act.wait_ge(sem("block_psum"), b0 + b + 1)
                    if b >= 2:
                        act.wait_ge(sem("block_done"), b0 + b - 1)
                    fn(Yn[:, b % 2, 0:512], B[4][:, :], ACT.Copy).then_inc(sem("block_in"), 1)

            def mixer1(l):
                act.wait_ge(sem("flow_ready"), l + 1)
                fn(flT, B[4][0:16, 0:T], ACT.Copy).then_inc(sem("flT_ready"), 1)
                W = plain_at[f"win{l}"]
                for j in range(10):
                    act.wait_ge(sem("plain_used"), W + j + 1)
                    b = B[j % 4]
                    if j == 0:
                        ins = fn(qT, b[:, :], ACT.Copy, scale=0.125)
                    elif j == 1:
                        ins = fn(kT, b[:, :], ACT.Copy)
                    elif j in (2, 3):
                        c = 2 * (j - 2)
                        ins = fn(upad[:, c:c + 2, 3:], b[:, :].rearrange("p (c t) -> p c t", c=2), ACT.Copy)
                    elif j in (4, 5):
                        ins = fn(vn[:, :, (j - 4) * CW:(j - 3) * CW], b[:, :].rearrange("p (a f) -> p a f", a=2), ACT.Copy)
                    elif j in (6, 7):
                        ins = fn(gT[:, (j - 6) * 512:(j - 5) * 512], b[:, :], ACT.Silu)
                    else:
                        ins = fn(gate[:, (j - 8) * 512:(j - 7) * 512], b[:, :], ACT.Gelu_apprx_tanh)
                    ins.then_inc(sem("z_in"), 1)
                    if j == 1:
                        act.wait_ge(sem("lf_ready"), l + 1)
                        for m in range(2):
                            fn(tmp1[:, m * T:(m + 1) * T], B[5][:, m * T:(m + 1) * T], ACT.Abs,
                               bias=VT[:, l, V_BG + m:V_BG + m + 1]).then_inc(sem("act_chain"), 1)
                        count[0] += 2
                        act.wait_ge(sem("act_chain"), count[0])
                        link(fn(tmp1, tmp1, ACT.Exp, scale=-1.0))
                        fn(tmp1, tmp1, ACT.Ln, bias=one).then_inc(sem("lsig_ready"), 1)
                    if j == 5:
                        gla_exps(l)
                    if j == 6:
                        for g in range(4):
                            act.wait_ge(sem("rgate_ready"), 4 * l + g + 1)
                            bank, dst, row, pair = ((4, rr, V_BA, 0), (5, rr, V_BA, 1), (6, ri, V_BX, 0), (4, ri, V_BX, 1))[g]
                            for m in range(2):
                                c = 2 * pair + m
                                ins = fn(dst[:, c * T:(c + 1) * T], B[bank][:, m * T:(m + 1) * T], ACT.Sigmoid,
                                         bias=VT[:, l, row + c:row + c + 1])
                            ins.then_inc(sem("rgate_done"), 1)
                        act.wait_ge(sem("rgate_done"), 4 * l + 4)
                        for c in range(4):
                            ins = fn(ra[:, c * T:(c + 1) * T], rr[:, c * T:(c + 1) * T], ACT.Exp,
                                     scale=small[:, 64 + 4 * l + c:65 + 4 * l + c])
                        for c in range(4):
                            ins = fn(rm[:, c * T:(c + 1) * T], rr[:, c * T:(c + 1) * T], ACT.Tanh,
                                     scale=small[:, 48 + 4 * l + c:49 + 4 * l + c])
                        ins.then_inc(sem("rtanh_ready"), 1)
                        act.wait_ge(sem("rm2_ready"), l + 1)
                        fn(rm, rm, ACT.Sqrt).then_inc(sem("rmult_ready"), 1)
                act.wait_ge(sem("kendn_ready"), l + 1)
                fn(kendn[:, :, :], B[4][:, :].rearrange("p (a f) -> p a f", a=2), ACT.Copy).then_inc(sem("kendn_done"), 1)
                for b in range(2):
                    act.wait_ge(sem("gla_o_ready"), 2 * l + b + 1)
                    fn(sqf[:, b * 512:(b + 1) * 512], B[2 + b][:, :], ACT.Square).then_inc(sem("gla_sq_ready"), 1)
                for b in range(2):
                    act.wait_ge(sem("gla_ss_ready"), 2 * l + b + 1)
                    fn(sc_sig[:, b * 512:(b + 1) * 512], B[b][:, :], ACT.Sqrt, bias=eps, scale=1.0 / P).then_inc(sem("gla_rms"), 1)

            def gla_exps(l):
                act.wait_ge(sem("bdiff_ready"), l + 1)
                fn(qloc, d1, ACT.Exp, scale=1.0 / 16)
                fn(kloc, d1, ACT.Exp, scale=-1.0 / 16)
                fn(kend, d2, ACT.Exp, scale=1.0 / 16)
                fn(qin, lfs, ACT.Exp, scale=1.0 / 16)
                fn(small[:, 128:128 + 8], blast, ACT.Exp, scale=1.0 / 16).then_inc(sem("gla_e_ready"), 1)

            def mixer2():
                W = plain_at["win2"]
                for j in range(12):
                    act.wait_ge(sem("plain_used"), W + j + 1)
                    b0, b1 = B[2 * (j % 2)], B[2 * (j % 2) + 1]
                    if j == 0:
                        ins = fn(rq[:, :, :], b0[:, :].rearrange("p (h t) -> p h t", h=2), ACT.Copy)
                    elif j == 1:
                        fn(rk[:, :, :], b0[:, :].rearrange("p (h t) -> p h t", h=2), ACT.Copy, scale=0.125)
                        ins = fn(rkn[:, :, :], b1[:, :].rearrange("p (h t) -> p h t", h=2), ACT.Copy, scale=0.125)
                    elif j in (2, 3, 6, 7):
                        dst, c = (rv, j - 2) if j < 4 else (v2, j - 6)
                        fn(dst[:, 0:2, c * CW:(c + 1) * CW], b0[:, :].rearrange("p (h t) -> p h t", h=2), ACT.Copy)
                        ins = fn(dst[:, 2:4, c * CW:(c + 1) * CW], b1[:, :].rearrange("p (h t) -> p h t", h=2), ACT.Copy)
                    elif j in (4, 5):
                        c = 2 * (j - 4)
                        for m, b in enumerate((b0, b1)):
                            fn(k2[:, c + m, 0:T], b[:, T:2 * T], ACT.Copy)
                            ins = fn(k2[:, c + m, T:2 * T], b[:, 0:T], ACT.Copy)
                    elif j in (8, 9):
                        c = 2 * (j - 8)
                        ins = fn(q2[:, c:c + 2, :], b0[:, :].rearrange("p (h t) -> p h t", h=2), ACT.Copy, scale=0.125)
                    else:
                        c = 2 * (j - 10)
                        ins = fn(rg[:, c:c + 2, :], b0[:, :].rearrange("p (h t) -> p h t", h=2), ACT.Silu)
                    ins.then_inc(sem("z2_in"), 1)
                for dr in range(2):
                    for pr in range(2):
                        ins = fn(qdec[:, dr, pr, :], C[:, (C_UP, C_DOWN)[dr]:(C_UP, C_DOWN)[dr] + T], ACT.Exp,
                                 scale=small[:, 80 + 2 * dr + pr:81 + 2 * dr + pr])
                ins.then_inc(sem("qdec_exp"), 1)
                for dr in range(2):
                    for a in range(2):
                        ins = fn(small[:, 96 + 8 * dr + 4 * a:100 + 8 * dr + 4 * a], small[:, 72 + 4 * dr:76 + 4 * dr], ACT.Exp,
                                 scale=C[:, C_TOK + 2 * dr + a:C_TOK + 2 * dr + a + 1])
                ins.then_inc(sem("kw_ready"), 1)
                act.wait_ge(sem("s2_psum"), 1)
                fn(S2[:, :, :, :], B[6][:, :].rearrange("p (h r v) -> p h r v", h=2, r=2), ACT.Copy).then_inc(sem("S2_ready"), 1)
                for b in range(2):
                    act.wait_ge(sem("ret_o"), 2 * b + 2)
                    if b == 0:
                        act.wait_ge(sem("ret_o"), 4)
                    fn(sqf[:, b * 512:(b + 1) * 512], B[2 + b][:, :], ACT.Square).then_inc(sem("ret_sq"), 1)
                for b in range(2):
                    act.wait_ge(sem("ret_ss"), b + 1)
                    fn(hflat[:, b * 512:(b + 1) * 512], B[b][:, :], ACT.Sqrt, bias=eps, scale=1.0 / P).then_inc(sem("ret_rms"), 1)
                act.wait_ge(sem("ret_done"), 4)
                for g in range(8):
                    for m in range(2):
                        act.wait_ge(sem("nmax_ready"), 2 * g + m + 1)
                        fn(pex[:, g % 2, m, :], B[2 * (g % 2) + m][:, :], ACT.Exp, bias=small[:, 144 + 2 * g + m:145 + 2 * g + m],
                           accum_out=small[:, 160 + 2 * g + m:161 + 2 * g + m]).then_inc(sem("p_ready"), 1)
                    if g >= 1:
                        att_copy(g - 1)
                    if g == 5:
                        att_norm(0)
                att_copy(7)
                att_norm(1)

            def att_copy(g):
                h, a = g // 2, g % 2
                act.wait_ge(sem("aT_psum"), g + 1)
                if h >= 2 and a == 0:
                    act.wait_ge(sem("att_o"), h - 1)
                fn(paT[:, h % 2, :, a * P:(a + 1) * P], B[4][:, :].rearrange("p (c t) -> p c t", c=4), ACT.Copy).then_inc(sem("aT_ready"), 1)

            def att_norm(b):
                act.wait_ge(sem("att_o"), 2 * b + 2)
                fn(sqf[:, b * 512:(b + 1) * 512], B[5 + b][:, :], ACT.Square).then_inc(sem("att_sq"), 1)
                act.wait_ge(sem("att_ss"), b + 1)
                fn(sqf[:, 1024 + b * 512:1024 + (b + 1) * 512], B[7][:, :], ACT.Sqrt, bias=eps, scale=1.0 / P).then_inc(sem("att_rms"), 1)

            act.dma_start(C[:], cst).then_inc(sem("const_in"), 16)
            act.dma_start(mixT[:, :, :].rearrange("p k t -> p (k t)"), rel).then_inc(sem("const_in"), 16)
            act.dma_start(XN.rearrange("p (a d) -> p a d", a=TT), A["x"].rearrange("b (a p) d -> p (b a) d", p=P)).then_inc(sem("x_in"), 16)
            act.wait_ge(sem("small_set"), 1)
            act.wait_ge(sem("vec_done"), 1)
            link(fn(small[:, 24:32], VT[:, 0, V_EXTRA:V_EXTRA + 8], ACT.Silu))
            sview = small[:, 32:48].rearrange("p (k v) -> p v k", v=2)
            link(fn(sview[:, 0, :], VT[:, 2, W_C:W_C + 8], ACT.Silu))
            fn(sview[:, 1, :], VT[:, 2, W_CC:W_CC + 8], ACT.Silu).then_inc(sem("c_act"), 1)
            for a in range(TT):
                act.wait_ge(sem("xin_ready"), a + 1)
                for half in range(2):
                    ins = fn(xT[:, 4 * half:4 * half + 4, a * P:(a + 1) * P],
                             B[2 * a + half][:, :].rearrange("p (k t) -> p k t", k=4), ACT.Copy)
                ins.then_inc(sem("x_copied"), 1)
            act.wait_ge(sem("x_copied"), 2)
            norm(0, xT[:, :, :])
            act.wait_ge(sem("vec_in"), NVEC)
            act.wait_ge(sem("lam_dot"), 1)
            link(fn(small[:, 368:384], small[:, 0:16], ACT.Abs))
            fn(small[:, 384:400], small[:, 368:384], ACT.Exp, scale=-1.0).then_inc(sem("sp_exp"), 1)
            fn(small[:, 186:188], small[:, 184:186], ACT.Exp).then_inc(sem("lam_exp"), 1)
            act.wait_ge(sem("lg_ready"), 1)
            for h in range(HEADS):
                if h:
                    act.wait_ge(sem("D_ready"), h)
                for dr in range(2):
                    ins = fn(TMP[:, 4096 + dr * 512:4096 + (dr + 1) * 512], mixT[:, 2 * dr:2 * dr + 2, :].rearrange("p k t -> p (k t)"), ACT.Exp,
                             scale=small[:, 72 + 4 * dr + h:73 + 4 * dr + h])
                ins.then_inc(sem("Dexp_ready"), 1)
            for l in range(LAYERS):
                if l:
                    act.wait_ge(sem("x_ready"), 1)
                    norm(2, xT[:, :, :])
                mixer1(l)
                act.wait_ge(sem("x_part"), 4 * l + 4)
                norm(2 * l + 1, xT[:, :, :])
                if l == 0:
                    dense("f0")
                else:
                    act.wait_ge(sem("h_norm"), 4)
                    rows_of_h(0)
                    act.wait_ge(sem("top_diff"), 1)
                    fn(small[:, 400:402], small[:, 402:404], ACT.Exp).then_inc(sem("top_exp"), 1)
                    experts1()
                    combine_slots(0, A1 // P)
            act.wait_ge(sem("x_ready"), 2)
            norm(4, xT[:, :, :])
            act.wait_ge(sem("x_ready"), 3)
            act.dma_start(CN.rearrange("p (a d) -> p a d", a=TT), A["ctx_2"].rearrange("b (a p) d -> p (b a) d", p=P)).then_inc(sem("ctx_in"), 16)
            norm(5, xT[:, :, :])
            ctxT = mixT
            for a in range(TT):
                act.wait_ge(sem("xin_ready"), 2 + a + 1)
                for half in range(2):
                    ins = fn(ctxT[:, 4 * half:4 * half + 4, a * P:(a + 1) * P],
                             B[2 * a + half][:, :].rearrange("p (k t) -> p k t", k=4), ACT.Copy)
                ins.then_inc(sem("x_copied"), 1)
            act.wait_ge(sem("x_copied"), 4)
            norm(6, ctxT[:, :, :])
            act.wait_ge(sem("h_norm"), 7)
            mixer2()
            act.wait_ge(sem("x_part"), 12)
            norm(7, xT[:, :, :])
            act.wait_ge(sem("logits_ready"), 2)
            fn(RT[:, 0:128], B[7][:, 0:128], ACT.Sigmoid).then_inc(sem("top_exp"), 1)
            rows_of_h(1)
            dense("sh")
            experts2()
            combine_slots(A1 // P, A2 // P)
            act.wait_ge(sem("x_ready"), 4)
            norm(8, xT[:, :, :])
            act.wait_ge(sem("stored"), 16)

        @block.vector
        def _(dve):
            V = nc.vector
            count = [0]

            def link(ins):
                count[0] += 1
                ins.then_inc(sem("dve_chain"), 1)
                dve.wait_ge(sem("dve_chain"), count[0])

            def done(ins, name, n):
                ins.then_inc(sem(name), 1)
                dve.wait_ge(sem(name), n)

            def recip(v):
                link(V.reciprocal(v, v))

            def scale_cols(row, l, v, sc_at, dst):
                link(V.tensor_scalar(dst, modc[:, v, sc_at:sc_at + 8], 1.0, None, ALU.add))
                link(V.tensor_tensor(dst, dst, VT[:, l, row:row + 8], ALU.mult))

            def norm(n, src, dst, gain, shift=None):
                dve.wait_ge(sem("rms_ready"), n + 1)
                recip(rstd[:])
                link(V.tensor_tensor(sq[:, :, :], src, rstd[:].unsqueeze(1).to_broadcast([P, KD, T]), ALU.mult))
                for k in range(KD):
                    if shift is None:
                        ins = V.tensor_scalar(dst(k), sq[:, k, :], gain[:, k:k + 1], None, ALU.mult)
                    else:
                        ins = V.tensor_scalar(dst(k), sq[:, k, :], gain[:, k:k + 1], shift[:, k:k + 1], ALU.mult, ALU.add)
                done(ins, "h_norm", n + 1)

            def ada_unit(n):
                name, _ = units[n]
                pieces = unit_pieces[n]
                written = [0, 0]
                for p in pieces:
                    arrived(dve, p)
                if n >= 2:
                    dve.wait_ge(sem("ada_psum"), n - 1)
                for k in range(KD):
                    for i in range(2):
                        acc = ffn_g[:, 2 * (n % 2) + i, :]
                        w = piece(pieces[i % len(pieces)])[:, k, :]
                        c = small[:, 32 + 2 * k + i:33 + 2 * k + i] if name == "ada2" else small[:, 24 + k:25 + k]
                        if k == 0:
                            ins = V.tensor_scalar(acc, w, c, None, ALU.mult)
                        else:
                            dve.wait_ge(sem("dve_chain"), written[i])
                            ins = V.scalar_tensor_tensor(out=acc, in0=w, scalar=c, in1=acc, op0=ALU.mult, op1=ALU.add)
                        if k == KD - 1 and (len(pieces) == 2 or i == 1):
                            ins.then_inc(sem("ada_used"), 1)
                        else:
                            ins.then_inc(sem("dve_chain"), 1)
                            count[0] += 1
                            written[i] = count[0]

            def modulation(v, nv, col, units_done):
                dve.wait_ge(sem("ada_psum"), units_done)
                for i in range(nv):
                    link(V.tensor_tensor(modc[:, v + i, :], B[7][:, col + 48 * i:col + 48 * (i + 1)],
                                         VT[:, v if v < 2 else 2, V_ADAB:V_ADAB + 48], ALU.add))

            gcol = small[:, 376:384]
            gcol_f = small[:, 384:392]

            def product(m, value, width):
                dve.wait_ge(sem("s_ready"), value)
                V.tensor_tensor(ffn_a[:, m, 0:width], ffn_s[:, m, 0:width], B[4 + m][:, T:T + width],
                                ALU.mult).then_inc(sem("a_ready"), 1)

            def dense(ph):
                for f in range(2 * len(step_at[ph])):
                    product(f % 2, base[ph] + f + 1, T)
                    if ph == "f0":
                        for n in units_after(f):
                            ada_unit(n)

            def matrices(g0, e, ws, start):
                if isinstance(e, int):
                    if e > 0 or g0 > 0:
                        dve.wait_ge(sem("he_psum"), 2 * (e + g0))
                else:
                    dve.wait_ge(sem("he_psum"), e * 2 + 2 * g0)
                iota = C[:, C_IOTA:C_IOTA + T]
                for a in range(TT):
                    ins = V.tensor_scalar(Pe[:, a, :], iota, rank[:, a, bass.ds(e, 1)], None, ALU.is_equal)
                ins.then_inc(sem("Pe_ready"), 1)
                if not isinstance(e, int):
                    dve.wait_ge(sem("w_kept"), e + g0)
                for a in range(TT):
                    ins = V.tensor_scalar(ws[:, a, bass.ds(start, T)], iota, rank[:, a, bass.ds(e, 1)],
                                          gts[:, a, bass.ds(e, 1)], ALU.is_equal, ALU.mult)
                ins.then_inc(sem("w_kept"), 1)

            def experts1():
                t0 = base["f1"]

                def tiles(e):
                    c = load_meta(dve, 0, e, 1)

                    def body(width):
                        with dve.Fori(0, STEPS1) as s:
                            for m in range(2):
                                product(m, e * (2 * STEPS1) + s * 2 + (t0 + m + 1), width)

                    by_class(dve, c, body)

                matrices(0, 0, w1s, load_meta(dve, 1, 0, A1))
                with dve.Fori(0, E1 - 1) as e:
                    start = load_meta(dve, 1, e + 1, A1)
                    matrices(0, e + 1, w1s, start)
                    tiles(e)
                tiles(E1 - 1)

            def experts2():
                t0 = base["f2"]

                def tiles(e):
                    c = load_meta(dve, 0, e, 1)

                    def body(width):
                        for m in range(2):
                            product(m, e * 2 + (t0 + m + 1), width)

                    by_class(dve, c, body)

                matrices(E1, 0, w2s, load_meta(dve, 1, 0, A2))
                with dve.Fori(0, E2 - 1) as e:
                    start = load_meta(dve, 1, e + 1, A2)
                    matrices(E1, e + 1, w2s, start)
                    tiles(e)
                tiles(E2 - 1)

            def combine_slots(b0, blocks):
                for b in range(blocks):
                    dve.wait_ge(sem("block_psum"), b0 + b + 1)
                    if b >= 2:
                        dve.wait_ge(sem("block_done"), b0 + b - 1)
                    V.tensor_copy(Yn[:, b % 2, 512:1024], B[5][:, :])
                    V.tensor_copy(PTs[:, b % 2, :], B[6][:, 0:T]).then_inc(sem("block_in"), 1)

            def places(l, E):
                for a in range(TT):
                    link(V.tensor_tensor_scan(mskx[:, a, 0:E], C[:, C_UP:C_UP + 1].to_broadcast([P, E]), msk[:, a, 0:E], 0.0,
                                              ALU.mult, ALU.add))
                    ins = V.tensor_tensor(mskx[:, a, 0:E], mskx[:, a, 0:E], msk[:, a, 0:E], ALU.subtract)
                    link(ins) if a == 0 else done(ins, "mask_ready", l + 1)
                dve.wait_ge(sem("places_psum"), l + 1)
                cnt, first = B[7][:, 0:E], B[7][:, E:2 * E]
                link(V.tensor_scalar(meta[:, 0, 0:E], cnt, float(CLASSES[0]), None, ALU.is_gt))
                link(V.tensor_copy(meta[:, 1, 0:E], first))
                for a in range(TT):
                    link(V.scalar_tensor_tensor(out=rank[:, a, 0:E], in0=B[7][:, (2 + a) * E:(3 + a) * E], scalar=1.0,
                                                in1=msk[:, a, 0:E], op0=ALU.add, op1=ALU.mult))
                    ins = V.tensor_scalar(rank[:, a, 0:E], rank[:, a, 0:E], -1.0, None, ALU.add)
                    link(ins) if a == 0 else done(ins, "meta_ready", l + 1)

            def add_ffn(name, value, nth, v):
                dve.wait_ge(sem(name), value)
                for d in range(KD):
                    ins = V.scalar_tensor_tensor(out=xT[:, d, :], in0=B[d // 2][:, (d % 2) * T:(d % 2 + 1) * T],
                                                 scalar=modc[:, v, 40 + d:41 + d], in1=xT[:, d, :], op0=ALU.mult, op1=ALU.add)
                if nth:
                    done(ins, "x_ready", nth)
                else:
                    ins.then_inc(sem("outs_read"), 1)

            def add_mix(name, nth, banks, v):
                for j in range(4):
                    dve.wait_ge(sem("plain_used"), plain_at[name] + j + 1)
                    for m in range(2):
                        d = 2 * j + m
                        ins = V.scalar_tensor_tensor(out=xT[:, d, :], in0=B[banks[j % len(banks)]][:, m * T:(m + 1) * T],
                                                     scalar=modc[:, v, 16 + d:17 + d], in1=xT[:, d, :], op0=ALU.mult, op1=ALU.add)
                    ins.then_inc(sem("x_part"), 1)
                dve.wait_ge(sem("x_part"), 4 * nth + 4)

            def mixer1(l):
                link(V.memset(upad[:, :, 0:3], 0.0))
                link(V.memset(sT[:, :, :], 0.0))
                dve.wait_ge(sem("lsig_ready"), l + 1)
                for m in range(2):
                    link(V.tensor_scalar(d1[:, m * T:(m + 1) * T], B[5][:, m * T:(m + 1) * T],
                                         VT[:, l, V_BG + m:V_BG + m + 1], 0.0, ALU.add, ALU.min))
                done(V.tensor_tensor(d1, d1, tmp1, ALU.subtract), "lf_done", l + 1)
                for m in range(2):
                    link(V.tensor_tensor_scan(lfs[:, m * T:(m + 1) * T], C[:, C_SCAN:C_SCAN + T], d1[:, m * T:(m + 1) * T],
                                              0.0, ALU.mult, ALU.add))
                b3 = lfs.rearrange("p (n t) -> p n t", t=CH)
                link(V.tensor_tensor(d1.rearrange("p (n t) -> p n t", t=CH), b3, b3[:, :, CH // 2 - 1:CH // 2].to_broadcast([P, 8, CH]), ALU.subtract))
                link(V.tensor_copy(blast.unsqueeze(2), b3[:, :, CH - 1:CH]))
                link(V.tensor_tensor(d2.rearrange("p (n t) -> p n t", t=CH), b3[:, :, CH - 1:CH].to_broadcast([P, 8, CH]), b3, ALU.subtract))
                V.tensor_copy(small[:, 22:23], small[:, 20:21]).then_inc(sem("bdiff_ready"), 1)
                dve.wait_ge(sem("z_in"), 10 * l + 4)
                for c in range(4):
                    o = uc[:, c * T:(c + 1) * T]
                    link(V.tensor_scalar(o, upad[:, c, 0:T], VT[:, l, V_CONVW + c:V_CONVW + c + 1],
                                         VT[:, l, V_CONVB + c:V_CONVB + c + 1], ALU.mult, ALU.add))
                    for tap in range(1, 4):
                        w = V_CONVW + 4 * tap + c
                        ins = V.scalar_tensor_tensor(out=o, in0=upad[:, c, tap:tap + T], scalar=VT[:, l, w:w + 1], in1=o,
                                                     op0=ALU.mult, op1=ALU.add)
                        link(ins) if (c, tap) != (3, 3) else done(ins, "conv_ready", l + 1)
                dve.wait_ge(sem("gla_e_ready"), l + 1)
                for o, z in ((qloc, qT), (kloc, kT), (kend, kT), (qin, qT)):
                    ins = V.tensor_tensor(o, o, z, ALU.mult)
                ins.then_inc(sem("gla_in"), 1)
                dve.wait_ge(sem("rtanh_ready"), l + 1)
                link(V.tensor_scalar(rr, rm, 1.0, None, ALU.add))
                recip(rr)
                V.scalar_tensor_tensor(out=rm, in0=rm, scalar=2.0, in1=rr, op0=ALU.mult, op1=ALU.mult).then_inc(sem("rm2_ready"), 1)
                dve.wait_ge(sem("rmult_ready"), l + 1)
                link(V.memset(rm.rearrange("p (c t) -> p c t", c=4)[:, :, 0:1], 1.0))
                link(V.tensor_tensor(rm, rm, ri, ALU.mult))
                link(V.tensor_tensor(rm, rm, uc, ALU.mult))
                for c in range(4):
                    s = slice(c * T, (c + 1) * T)
                    link(V.tensor_tensor_scan(rr[:, s], ra[:, s], rm[:, s], 0.0, ALU.mult, ALU.add))
                dve.wait_ge(sem("z_in"), 10 * l + 10)
                link(V.tensor_tensor(mixT[:, 0:4, :].rearrange("p k t -> p (k t)"), rr, gate, ALU.mult))
                mask = C[:, C_CAUS:C_CAUS + P].bitcast(U32).unsqueeze(1).to_broadcast([P, 2, P])
                s5 = sT[:, :, :].rearrange("p a (h r t) -> p r h a t", h=2, r=2)
                for par in range(2):
                    dve.wait_ge(sem("gla_s_ready"), 2 * l + par + 1)
                    for h2 in range(2):
                        ins = V.copy_predicated(s5[:, par, h2], mask,
                                                B[par][:, h2 * T:(h2 + 1) * T].rearrange("p (a t) -> p a t", a=TT))
                    ins.then_inc(sem("gla_sT_done"), 1)
                dve.wait_ge(sem("gla_u_ready"), l + 1)
                for n in range(NCH - 1):
                    src = B[5 + n % 2][:, (n // 2) * T:(n // 2 + 1) * T].rearrange("p (a v) -> p a v", a=2)
                    if n == 0:
                        ins = V.tensor_copy(St[:, 0, :, :], src)
                    else:
                        for pr in range(2):
                            ins = V.scalar_tensor_tensor(out=St[:, n, pr, :], in0=St[:, n - 1, pr, :],
                                                         scalar=small[:, 128 + pr * 4 + n:129 + pr * 4 + n],
                                                         in1=src[:, pr, :], op0=ALU.mult, op1=ALU.add)
                    done(ins, "state_ready", 3 * l + n + 1)
                for b in range(2):
                    dve.wait_ge(sem("gla_rms"), 2 * l + b + 1)
                    s = slice(b * 512, (b + 1) * 512)
                    recip(sc_sig[:, s])
                    g2 = gT.rearrange("p (h r t) -> p r h t", h=2, r=2)[:, b]
                    link(V.scalar_tensor_tensor(out=g2, in0=g2, scalar=VT[:, l, V_GLAG:V_GLAG + 1],
                                                in1=sc_sig[:, s].rearrange("p (h t) -> p h t", h=2), op0=ALU.mult, op1=ALU.mult))
                    ins = V.tensor_tensor(mixT[:, 4:8, :].rearrange("p (h r) t -> p r h t", r=2)[:, b],
                                          B[2 + b][:, :].rearrange("p (h t) -> p h t", h=2), g2, ALU.mult)
                done(ins, "mix_ready", l + 1)
                add_mix(f"wout{l}", l, [4, 5, 6], l)

            def softplus():
                x, y, s, s2, p = (small[:, 0:16], small[:, 384:400], small[:, 400:416], small[:, 416:432],
                                  small[:, 432:448])
                dve.wait_ge(sem("sp_exp"), 1)
                link(V.tensor_scalar(s2, y, 2.0, None, ALU.add))
                recip(s2)
                link(V.tensor_tensor(s, y, s2, ALU.mult))
                link(V.tensor_tensor(s2, s, s, ALU.mult))
                link(V.tensor_scalar(p, s2, 1.0 / 17, None, ALU.mult))
                for n in (15, 13, 11, 9, 7, 5, 3):
                    link(V.scalar_tensor_tensor(out=p, in0=p, scalar=1.0 / n, in1=s2, op0=ALU.add, op1=ALU.mult))
                link(V.scalar_tensor_tensor(out=p, in0=p, scalar=1.0, in1=s, op0=ALU.add, op1=ALU.mult))
                link(V.tensor_scalar(y, x, -1.0, 0.0, ALU.mult, ALU.max))
                link(V.scalar_tensor_tensor(out=p, in0=p, scalar=2.0, in1=y, op0=ALU.mult, op1=ALU.add))
                link(V.tensor_scalar(small[:, 48:56], p[:, 0:8], 8.0, None, ALU.mult))
                link(V.tensor_scalar(small[:, 64:72], p[:, 0:8], -8.0, None, ALU.mult))
                link(V.tensor_scalar(small[:, 72:80], p[:, 8:16], -1.0, None, ALU.mult))
                for dr in range(2):
                    for pr in range(2):
                        for hh in range(2):
                            r = slice(64 * hh, 64 * hh + 64)
                            h = 2 * pr + hh
                            link(V.tensor_copy(small[r, 80 + 2 * dr + pr:81 + 2 * dr + pr], small[r, 72 + 4 * dr + h:73 + 4 * dr + h]))
                V.tensor_copy(small[:, 22:23], small[:, 20:21]).then_inc(sem("lg_ready"), 1)

            def decays():
                for h in range(HEADS):
                    dve.wait_ge(sem("Dexp_ready"), h + 1)
                    ef, eb = TMP[:, 4096:4608], TMP[:, 4608:5120]
                    link(V.tensor_tensor(ef, ef, mixT[:, 4:6, :].rearrange("p k t -> p (k t)"), ALU.mult))
                    link(V.tensor_tensor(eb, eb, mixT[:, 6:8, :].rearrange("p k t -> p (k t)"), ALU.mult))
                    done(V.tensor_tensor(Dret[:, h, :], ef, eb, ALU.add), "D_ready", h + 1)

            def top2_gates():
                dve.wait_ge(sem("logits_ready"), 1)
                lg, top, idx, idf = (RT[:, 16 * n:16 * n + 16].rearrange("p (a e) -> p a e", a=2) for n in range(4))
                idx = RT[:, 32:48].bitcast(U32).rearrange("p (a e) -> p a e", a=2)
                link(V.tensor_copy(lg, B[7][:, 0:16].rearrange("p (a e) -> p a e", a=2)))
                for a in range(TT):
                    link(V.max(top[:, a, :], lg[:, a, :]))
                    link(V.max_index(idx[:, a, :], top[:, a, :], lg[:, a, :]))
                    link(V.tensor_copy(idf[:, a, :], idx[:, a, :]))
                    link(V.tensor_tensor(small[:, 402 + a:403 + a], top[:, a, 1:2], top[:, a, 0:1], ALU.subtract))
                V.tensor_copy(small[:, 22:23], small[:, 20:21]).then_inc(sem("top_diff"), 1)
                dve.wait_ge(sem("top_exp"), 1)
                link(V.tensor_scalar(small[:, 404:406], small[:, 400:402], 1.0, None, ALU.add))
                recip(small[:, 404:406])
                link(V.tensor_tensor(small[:, 406:408], small[:, 404:406], small[:, 400:402], ALU.mult))
                for a in range(TT):
                    g = gts[:, a, 0:8]
                    t8, u8 = RT[:, 64:72], RT[:, 72:80]
                    io = C[:, C_IOTA:C_IOTA + 8]
                    link(V.tensor_scalar(t8, io, idf[:, a, 0:1], None, ALU.is_equal))
                    link(V.tensor_scalar(u8, io, idf[:, a, 1:2], None, ALU.is_equal))
                    link(V.tensor_tensor(msk[:, a, 0:8], t8, u8, ALU.add))
                    link(V.tensor_scalar(t8, t8, small[:, 404 + a:405 + a], None, ALU.mult))
                    link(V.scalar_tensor_tensor(out=g, in0=u8, scalar=small[:, 406 + a:407 + a], in1=t8,
                                                op0=ALU.mult, op1=ALU.add))

            def one_hot_sum(dst, idf, n, width):
                io = C[:, C_IOTA:C_IOTA + width]
                link(V.tensor_scalar(dst, io, idf[:, 0:1], None, ALU.is_equal))
                for j in range(1, n):
                    link(V.scalar_tensor_tensor(out=dst, in0=io, scalar=idf[:, j:j + 1], in1=dst, op0=ALU.is_equal, op1=ALU.add))

            def group_gates():
                dve.wait_ge(sem("top_exp"), 2)
                for a in range(TT):
                    sc = RT[:, 64 * a:64 * a + 64]
                    sel = RT[:, 128:192]
                    t8 = RT[:, 192:256].rearrange("p (g e) -> p g e", g=8)
                    gs, tg, gm = RT[:, 256:264], RT[:, 264:272], RT[:, 272:280]
                    ix = RT[:, 280:288].bitcast(U32)
                    idf = RT[:, 288:296]
                    link(V.tensor_tensor(sel, sc, small[:, 192:256], ALU.add))
                    for g in range(8):
                        link(V.max(t8[:, g, :], sel[:, 8 * g:8 * g + 8]))
                    link(V.tensor_tensor(gs.unsqueeze(2), t8[:, :, 0:1], t8[:, :, 1:2], ALU.add))
                    link(V.max(tg, gs))
                    link(V.max_index(ix, tg, gs))
                    link(V.tensor_copy(idf, ix))
                    one_hot_sum(gm, idf, 4, 8)
                    s3 = sel.rearrange("p (g e) -> p g e", g=8)
                    link(V.tensor_tensor(s3, s3, gm.unsqueeze(2).to_broadcast([P, 8, 8]), ALU.mult))
                    link(V.tensor_scalar(gm, gm, -1.0, 3e38, ALU.add, ALU.mult))
                    link(V.tensor_tensor(s3, s3, gm.unsqueeze(2).to_broadcast([P, 8, 8]), ALU.add))
                    link(V.max(tg, sel))
                    link(V.max_index(ix, tg, sel))
                    link(V.tensor_copy(idf, ix))
                    one_hot_sum(msk[:, a, :], idf, 8, 64)
                    g = small[:, 512 + 64 * a:576 + 64 * a]
                    link(V.tensor_tensor(g, sc, msk[:, a, :], ALU.mult))
                    link(V.tensor_reduce(gs[:, 0:1], g, AX, ALU.add))
                    recip(gs[:, 0:1])
                    link(V.tensor_scalar(g, g, gs[:, 0:1], 2.5, ALU.mult, ALU.mult))

            def mixer2():
                dve.wait_ge(sem("z2_in"), 12)
                cos = C[:, C_COS:C_COS + T].unsqueeze(1).to_broadcast([P, 2, T])
                sin = C[:, C_SIN:C_SIN + T].unsqueeze(1).to_broadcast([P, 2, T])
                rt = rope_t.rearrange("p (h t) -> p h t", h=2)
                for g in range(6):
                    z = [rq[:, :, :], rk[:, :, :], k2[:, 0:2, T:], k2[:, 2:4, T:], q2[:, 0:2, :], q2[:, 2:4, :]][g]
                    dve.wait_ge(sem("rot_ready"), g + 1)
                    link(V.tensor_tensor(rt, B[4 + g % 2][:, :].rearrange("p (h t) -> p h t", h=2), sin, ALU.mult))
                    link(V.tensor_tensor(z, z, cos, ALU.mult))
                    done(V.tensor_tensor(z, z, rt, ALU.add), "rope_done", g + 1)
                    if g == 0:
                        dve.wait_ge(sem("qdec_exp"), 1)
                        for dr in range(2):
                            link(V.tensor_tensor(qdec[:, dr, :, :], qdec[:, dr, :, :], rq[:, :, :], ALU.mult))
                        V.tensor_copy(small[:, 22:23], small[:, 20:21]).then_inc(sem("qdec_ready"), 1)
                        dve.wait_ge(sem("kw_ready"), 1)
                        for dr in range(2):
                            w = small[:, 96 + 8 * dr:104 + 8 * dr].rearrange("p (a h) -> p a h", a=2)
                            for a in range(2):
                                ins = V.tensor_tensor(kdec[:, dr, a, :].rearrange("p (h d) -> p h d", h=HEADS),
                                                      rkn[:, a, :].rearrange("p (h d) -> p h d", h=HEADS),
                                                      w[:, a, :].unsqueeze(2).to_broadcast([P, HEADS, 64]), ALU.mult)
                        ins.then_inc(sem("kdec_ready"), 1)
                for h in range(HEADS):
                    dve.wait_ge(sem("ret_s"), h + 1)
                    if h >= 2:
                        dve.wait_ge(sem("ret_o"), h - 1)
                    V.tensor_tensor(sD[:, h % 2, :], B[h % 2][:, :], Dret[:, h, :], ALU.mult).then_inc(sem("sD_ready"), 1)
                for b in range(2):
                    dve.wait_ge(sem("ret_rms"), b + 1)
                    s = slice(b * 512, (b + 1) * 512)
                    recip(hflat[:, s])
                    r2 = rg[:, :, :].rearrange("p (h r) t -> p r h t", r=2)[:, b]
                    link(V.scalar_tensor_tensor(out=r2, in0=r2, scalar=VT[:, 2, W_RG:W_RG + 1],
                                                in1=hflat[:, s].rearrange("p (h t) -> p h t", h=2), op0=ALU.mult, op1=ALU.mult))
                    done(V.tensor_tensor(mixT[:, 4:8, :].rearrange("p (h r) t -> p r h t", r=2)[:, b],
                                         B[2 + b][:, :].rearrange("p (h t) -> p h t", h=2), r2, ALU.mult),
                         "ret_done", 2 * b + 1)
                    done(V.tensor_copy(small[:, 23:24], small[:, 20:21]), "ret_done", 2 * b + 2)
                for g in range(8):
                    for m in range(2):
                        dve.wait_ge(sem("att_s"), 2 * g + m + 1)
                        V.tensor_reduce(small[:, 144 + 2 * g + m:145 + 2 * g + m], B[2 * (g % 2) + m][:, :], AX, ALU.max,
                                        negate=True).then_inc(sem("nmax_ready"), 1)
                    if g >= 1:
                        combine(g - 1)
                    if g == 6:
                        att_norm(0)
                combine(7)
                att_norm(1)
                add_mix("wout2", 2, [0, 1, 2, 3], 2)

            def combine(g):
                dve.wait_ge(sem("p_ready"), 2 * g + 2)
                rs = small[:, 176:178]
                link(V.reciprocal(rs, small[:, 160 + 2 * g:162 + 2 * g]))
                link(V.tensor_tensor(rs[:, 1:2], rs[:, 1:2], small[:, 188:189], ALU.mult))
                link(V.tensor_scalar(pex[:, g % 2, 1, :], pex[:, g % 2, 1, :], rs[:, 1:2], None, ALU.mult))
                done(V.scalar_tensor_tensor(out=pex[:, g % 2, 0, :], in0=pex[:, g % 2, 0, :], scalar=rs[:, 0:1],
                                            in1=pex[:, g % 2, 1, :], op0=ALU.mult, op1=ALU.subtract), "a2_ready", g + 1)

            def att_norm(b):
                dve.wait_ge(sem("att_rms"), b + 1)
                s = sqf[:, 1024 + b * 512:1024 + (b + 1) * 512]
                recip(s)
                ins = V.scalar_tensor_tensor(out=mixT[:, 2 * b:2 * b + 2, :].rearrange("p k t -> p (k t)"), in0=B[5 + b][:, :],
                                             scalar=small[:, 189:190], in1=s, op0=ALU.mult, op1=ALU.mult)
                if b:
                    done(ins, "mix_ready", 3)
                else:
                    link(ins)

            link(V.memset(small[:, 16:24], EPS))
            link(V.memset(small[:, 21:22], 1.0))
            dve.wait_ge(sem("vec_ready"), 1)
            link(V.tensor_copy(VT[:, 0:2, 0:V_ROWS], B[6][:, 0:2 * P].rearrange("p (l r) -> p l r", l=2)[:, :, 0:V_ROWS]))
            done(V.tensor_copy(VT[:, 2, 0:W_ROWS], B[6][:, 2 * P:2 * P + W_ROWS]), "vec_done", 1)
            link(V.tensor_copy(small[:, 0:4], VT[:, 0, V_LAM:V_LAM + 4]))
            link(V.tensor_copy(small[:, 4:8], VT[:, 1, V_LAM:V_LAM + 4]))
            V.tensor_copy(small[:, 22:23], small[:, 20:21]).then_inc(sem("small_set"), 1)
            dve.wait_ge(sem("vec_in"), NVEC)
            for k in range(2):
                v = small[:, 256 + 128 * k:256 + 128 * k + 64]
                w = small[:, 320 + 128 * k:320 + 128 * k + 64]
                link(V.tensor_tensor(v, v, w, ALU.mult))
                link(V.tensor_reduce(small[:, 184 + k:185 + k], v, AX, ALU.add))
            V.tensor_copy(small[:, 22:23], small[:, 20:21]).then_inc(sem("lam_dot"), 1)
            softplus()
            dve.wait_ge(sem("lam_exp"), 1)
            link(V.tensor_tensor(small[:, 188:189], small[:, 186:187], small[:, 187:188], ALU.subtract))
            link(V.tensor_scalar(small[:, 188:189], small[:, 188:189], LAM_INIT, None, ALU.add))
            link(V.tensor_scalar(small[:, 189:190], VT[:, 2, W_DG:W_DG + 1], 1.0 - LAM_INIT, None, ALU.mult))
            decays()
            dve.wait_ge(sem("c_act"), 1)
            for n in range(ADA_UNITS):
                ada_unit(n)
            modulation(0, 1, 0, ADA_UNITS)
            for l in range(LAYERS):
                scale_cols(V_G1, l, l, 8, gcol)
                scale_cols(V_G2, l, l, 32, gcol_f)
                norm(2 * l, xT[:, :, :], lambda k: hT1[:, k, :], gcol, modc[:, l, 0:8])
                mixer1(l)
                norm(2 * l + 1, xT[:, :, :], lambda k: hT1[:, k, :], gcol_f, modc[:, l, 24:32])
                if l == 0:
                    dense("f0")
                    add_ffn("down_done", base["f0"] + 22, 1, 0)
                    modulation(1, 1, 0, ADA_UNITS + F0_UNITS)
                    modulation(2, 2, 64, ADA_UNITS + F0_UNITS)
                else:
                    top2_gates()
                    places(0, E1)
                    experts1()
                    combine_slots(0, A1 // P)
                    add_ffn("block_done", A1 // P, 2, 1)
            norm(4, xT[:, :, :], lambda k: xT[:, k, :], VT[:, 1, V_EXTRA:V_EXTRA + 8])
            V.tensor_copy(small[:, 22:23], small[:, 20:21]).then_inc(sem("x_ready"), 1)
            scale_cols(V_G1, 2, 2, 8, gcol)
            norm(5, xT[:, :, :], lambda k: hcat[:, k, 0:T], gcol, modc[:, 2, 0:8])
            V.tensor_copy(small[:, 22:23], small[:, 20:21]).then_inc(sem("ctx_go"), 1)
            scale_cols(V_G1, 2, 3, 8, gcol)
            norm(6, mixT[:, :, :], lambda k: hcat[:, k, T:2 * T], gcol, modc[:, 3, 0:8])
            scale_cols(V_G2, 2, 2, 32, gcol_f)
            mixer2()
            norm(7, xT[:, :, :], lambda k: hT1[:, k, :], gcol_f, modc[:, 2, 24:32])
            group_gates()
            dense("sh")
            add_ffn("down_done", base["sh"] + 2, 0, 2)
            places(1, E2)
            experts2()
            combine_slots(A1 // P, A2 // P)
            add_ffn("block_done", (A1 + A2) // P, 4, 2)
            norm(8, xT[:, :, :], lambda k: xT[:, k, :], VT[:, 2, W_FG:W_FG + 8])
            for a in range(TT):
                dve.wait_ge(sem("outT_ready"), a + 1)
                for half in range(2):
                    ins = V.tensor_copy(hflat[:, a * D + half * 512:a * D + (half + 1) * 512], B[2 * a + half][:, :])
                ins.then_inc(sem("out_tile"), 1)


_INS = [
    "x", "c", "ada_w", "ada_b", "norm_mix_g", "norm_ffn_g", "w_in", "rg_conv_w", "rg_conv_b", "rg_wa", "rg_ba", "rg_wx",
    "rg_bx", "rg_lambda", "gla_wg2", "gla_bg", "gla_norm_g", "w_out", "ffn_w1", "ffn_w3", "ffn_w2", "router_w",
    "moe_w1", "moe_w3", "moe_w2", "final_g", "c_2", "ctx_2", "c_ctx_2", "ada_w_2", "ada_b_2", "norm1_g_2", "w_in_2",
    "lambda_q1_2", "lambda_k1_2", "lambda_q2_2", "lambda_k2_2", "dattn_norm_g_2", "ret_decay_fwd_2",
    "ret_decay_bwd_2", "ret_norm_g_2", "w_out_2", "norm2_g_2", "router_w_2", "router_bias_2", "exp_w1_2",
    "exp_w3_2", "exp_w2_2", "shared_w1_2", "shared_w3_2", "shared_w2_2", "final_norm_g_2",
]


def kernel(**inputs):
    import numpy as _np
    import concourse.bacc as _bacc
    from concourse import mybir as _mybir
    from concourse.bass_utils import run_bass_kernel_spmd as _run

    nc = _bacc.Bacc("TRN2", target_bir_lowering=False, num_devices=1)
    arrays, A = {}, {}
    for name in _INS:
        a = _np.ascontiguousarray(inputs[name])
        if a.ndim == 1 and name == "c_ctx_2":
            a = a.reshape(1, -1)
        arrays[f"in_{name}"] = a
        A[name] = nc.dram_tensor(f"in_{name}", a.shape, F32, kind="ExternalInput").ap()
    A["c_ctx_2"] = A["c_ctx_2"][0]
    extra = {}
    for name, a in zip(("constants", "relative"), constants()):
        arrays[name] = a
        extra[name] = nc.dram_tensor(name, a.shape, F32, kind="ExternalInput").ap()
    out = nc.dram_tensor("out", (1, T, D), F32, kind="ExternalOutput").ap()
    build(nc, A, extra["constants"], extra["relative"], out)
    r = _run(nc, [arrays], core_ids=[0])
    return r.results[0]["out"]
```

```python
from contextlib import ExitStack

import concourse.bass as bass
from concourse import mybir

F32 = mybir.dt.float32
U32 = mybir.dt.uint32
ALU = mybir.AluOpType
ACT = mybir.ActivationFunctionType
AX = mybir.AxisListType.X

P = 128
T = 256
TT = T // P
D = 1024
KD = D // P
CW = 256
RING = 9
BESIDE = 5
PAIR_SLOTS = 12
LAYERS = 2
CH = 64
NCH = T // CH
FF = 2816
EPS = 1e-6
LAM_INIT = 0.2
HEADS = 4
CLASSES = (64, 128, 256)
E1, STEPS1, A1 = 8, FF // CW, 2 * T
E2, PAIRS, HALF = 64, 32, 64

C_ID, C_ROT, C_COS, C_SIN, C_SCAN, C_CAUS, C_UP, C_DOWN, C_TOK, C_IOTA = (
    0, 128, 256, 512, 768, 1024, 1152, 1408, 1664, 1668)
C_SU = C_IOTA + T
C_N = C_SU + P
V_ADAB, V_G1, V_G2 = 0, 48, 56
V_CONVW, V_CONVB, V_BA, V_BX, V_LAM, V_BG, V_GLAG, V_EXTRA = 64, 80, 84, 88, 92, 96, 98, 99
V_ROWS = 107
W_DG, W_RG, W_FG, W_C, W_CC = 64, 65, 66, 74, 82
W_ROWS = 90


def constants():
    import numpy as np
    c = np.zeros((P, C_N), np.float32)
    c[:, C_ID:C_ID + P] = np.eye(P)
    for p in range(P):
        if (p // 16) % 2 == 0:
            c[p + 16, C_ROT + p] = -1.0
        else:
            c[p - 16, C_ROT + p] = 1.0
    t = np.arange(T)
    inv = (10000.0 ** (-np.arange(16, dtype=np.float32) / 16)).astype(np.float32)
    for p in range(P):
        pos = (t // 64 if (p // 32) % 2 == 0 else t % 64).astype(np.float32)
        ang = pos * inv[p % 16]
        c[p, C_COS:C_COS + T] = np.cos(ang)
        c[p, C_SIN:C_SIN + T] = np.sin(ang)
    c[:, C_SCAN:C_SCAN + T] = (t % CH != 0)
    j = np.arange(P)[:, None]
    i = np.arange(P)[None, :]
    c[:, C_CAUS:C_CAUS + P] = (i >= j) & (i // CH == j // CH)
    c[:, C_UP:C_UP + T] = t + 1
    c[:, C_DOWN:C_DOWN + T] = T - t
    for jt in range(TT):
        tok = np.arange(P) + jt * P
        c[:, C_TOK + jt] = T - 1 - tok
        c[:, C_TOK + TT + jt] = tok
    c[:, C_IOTA:C_IOTA + T] = t
    c[:, C_SU:C_SU + P] = j < i
    r = np.zeros((P, 4, TT, T), np.float32)
    for jt in range(TT):
        rel = t[None, :] - (np.arange(P)[:, None] + jt * P)
        r[:, 0, jt], r[:, 1, jt] = np.maximum(rel, 0), np.maximum(-rel, 0)
        r[:, 2, jt], r[:, 3, jt] = rel >= 0, rel <= 0
    return c, r.reshape(P, -1)


def build(nc, A, cst, rel, out):
    with ExitStack() as ctx:
        def sb(name, shape, dt=F32):
            return ctx.enter_context(nc.sbuf_tensor(name, shape, dt))

        sems = {}

        def sem(name):
            if name not in sems:
                sems[name] = ctx.enter_context(nc.semaphore(name))
            return sems[name]

        SLOT = KD * CW
        arena = sb("arena", [P, RING * SLOT + 11264 + 3 * 2048])
        TMP = arena[:, RING * SLOT:RING * SLOT + 11264]
        o3 = RING * SLOT + 11264
        mixf, Dretf, sqf = (arena[:, o3 + 2048 * n:o3 + 2048 * (n + 1)] for n in range(3))
        mixT = mixf.rearrange("p (k t) -> p k t", k=KD)
        Dret = Dretf.rearrange("p (h t) -> p h t", h=HEADS)
        sq = sqf.rearrange("p (k t) -> p k t", k=KD)
        xT = sb("xT", [P, KD, T])
        hcat = sb("hcat", [P, KD, 2 * T])
        hflat = hcat[:, :, :].rearrange("p k t -> p (k t)")
        C = sb("C", [P, C_N])
        VT = sb("VT", [P, 3, P])
        VN = sb("VN", [P, 3, P])
        rstd = sb("rstd", [P, T])
        ffn_s = sb("ffn_s", [P, 2, T])
        ffn_a = sb("ffn_a", [P, 2, T])
        ffn_g = sb("ffn_g", [P, 4, T])
        ones = sb("ones", [P, P])
        small = sb("small", [P, 640])
        modc = sb("modc", [P, 4, 48])
        router = sb("router", [P, KD, 64])
        wf = sb("wf", [P, KD, 16])
        wa_bd = sb("wa_bd", [P, 4, P])
        wx_bd = sb("wx_bd", [P, 4, P])
        wg2 = sb("wg2", [16, T])
        hn = sb("hn", [P, TT, D])
        rank_t = sb("rank_t", [P, TT, E2])
        meta = sb("meta", [P, 6, E2], mybir.dt.int32)
        ident = C[:, C_ID:C_ID + P]

        B = [ctx.enter_context(nc.psum_tensor(f"B{i}", [P, 512], F32)) for i in range(8)]

        at = [0]

        def cut(n, **dims):
            v = TMP[:, at[0]:at[0] + n]
            at[0] += n
            return v

        UPW = T + 3
        upad = cut(4 * UPW).rearrange("p (c t) -> p c t", c=4)
        gate = cut(1024)
        qT = cut(512)
        kT = cut(512)
        gT = cut(1024)
        vn = cut(1024).rearrange("p (a f) -> p a f", a=TT)
        qloc, kloc, qin, kend = cut(512), cut(512), cut(512), cut(512)
        kendn = cut(512).rearrange("p (a f) -> p a f", a=TT)
        sT = cut(1024).rearrange("p (a f) -> p a f", a=TT)
        St = cut(3 * 256).rearrange("p (n a v) -> p n a v", n=3, a=2)
        uc = cut(1024)
        sc_sig = uc
        blast = cut(8)
        assert at[0] <= 11264
        rr, ri = hflat[:, 2048:3072], hflat[:, 3072:4096]
        hT1 = hflat[:, 0:2048].rearrange("p (k t) -> p k t", k=KD)
        d1, d2, lfs, tmp1 = sqf[:, 0:512], sqf[:, 512:1024], sqf[:, 1024:1536], sqf[:, 1536:2048]
        ra = ffn_g[:, :, :].rearrange("p s t -> p (s t)")
        rm = mixT[:, 4:8, :].rearrange("p k t -> p (k t)")
        flT = ffn_s[0:16, 0, :]
        at[0] = 0
        q2 = cut(1024).rearrange("p (h t) -> p h t", h=HEADS)
        k2 = cut(2048).rearrange("p (h t) -> p h t", h=HEADS)
        v2 = cut(2048).rearrange("p (a f) -> p a f", a=4)
        rq = cut(512).rearrange("p (h t) -> p h t", h=2)
        rk = cut(512).rearrange("p (h t) -> p h t", h=2)
        rkn = cut(512).rearrange("p (a f) -> p a f", a=2)
        rv = cut(2048).rearrange("p (a f) -> p a f", a=4)
        rg = cut(1024).rearrange("p (h t) -> p h t", h=HEADS)
        qdec = cut(1024).rearrange("p (r h t) -> p r h t", r=2, h=2)
        S2 = cut(512).rearrange("p (h r v) -> p h r v", h=2, r=2)
        assert at[0] <= 11264
        kdec = sqf[:, 0:1024].rearrange("p (r a f) -> p r a f", r=2, a=2)
        sD = sqf[:, 1024:2048].rearrange("p (b f) -> p b f", b=2)
        pex = hflat[:, 0:2048].rearrange("p (b m f) -> p b m f", b=2, m=2)
        paT = hflat[:, 2048:4096].rearrange("p (b c t) -> p b c t", b=2, c=4)
        rope_t = ffn_a[:, :, :].rearrange("p b t -> p (b t)")

        heT = hflat[:, 2048:4096]
        Pe = ffn_g[:, 0:2, :]
        y1 = TMP[:, 0:KD * (A1 + T)].rearrange("p (k s) -> p k s", k=KD)
        w1s = TMP[:, 6144:6144 + 2 * (A1 + T)].rearrange("p (a s) -> p a s", a=TT)
        o2 = PAIR_SLOTS * SLOT
        first_round = dict(name="pair", P=ffn_g[:, 2, :], W=ffn_g[:, 3, :], heT=hflat[:, 2048:3072],
                           s=ffn_s[:, 0, :], a=ffn_a[:, 0, :], aw=ffn_g[:, 0:2, :].rearrange("p s t -> p (s t)"),
                           Y=hflat[:, 3072:4096])
        more_round = dict(name="more", P=arena[:, o2:o2 + 256], W=arena[:, o2 + 256:o2 + 512],
                          heT=arena[:, o2 + 512:o2 + 1536], s=ffn_s[:, 1, :], a=ffn_a[:, 1, :],
                          aw=arena[:, o2 + 1536:o2 + 2048], Y=arena[:, o2 + 2048:o2 + 3072])
        RT = TMP[:, 8192:]
        rank = rank_t[:, :, :]
        gts = small[:, 512:640].rearrange("p (a e) -> p a e", a=TT)
        msk = RT[:, 2304:2304 + 2 * E2].rearrange("p (a e) -> p a e", a=TT)
        mskx = RT[:, 2432:2432 + 2 * E2].rearrange("p (a e) -> p a e", a=TT)
        Yn = heT.rearrange("p (b d) -> p b d", b=2)
        PTs = ffn_g[:, 2:4, :]
        ns, na = (v[:, :, :].rearrange("p b t -> p (b t)") for v in (ffn_s, ffn_a))
        naT = PTs.rearrange("p b t -> p (b t)")

        def cols(w, c0):
            return w.rearrange("(k p) f -> p k f", p=P)[:, :, c0:c0 + CW]

        WIN1 = [1024, 1280, 0, 256, 1536, 1792, 2048, 2304, 512, 768]
        WIN2 = [1536, 1792, 2048, 2304, 512, 768, 1024, 1280, 0, 256, 2560, 2816]
        stream, uses, last_in = [], [0] * (RING + BESIDE), [None] * (RING + BESIDE)
        n_plain, next_slot, beside = [0], [0], range(RING, RING + BESIDE)

        def add(what, release, slot=None):
            if slot is None:
                slot = next_slot[0]
                next_slot[0] = (slot + 1) % RING
            uses[slot] += 1
            if last_in[slot] is not None:
                free = stream[last_in[slot]]["release"]
            elif slot in beside:
                free = ("x_part", 4)
            else:
                free = None
            stream.append(dict(what=what, release=release, slot=slot, use=uses[slot], free=free))
            last_in[slot] = len(stream) - 1

        def plain(w, c0):
            n_plain[0] += 1
            add(cols(w, c0), ("plain_used", n_plain[0]))

        marks, base, tile0 = {}, {}, [0]
        ADA_UNITS = 24 // 2
        units = [("ada0", u) for u in range(ADA_UNITS)]
        for u in range(ADA_UNITS):
            units += [("ada1", u), ("ada2", 2 * u), ("ada2", 2 * u + 1)]
        unit_pieces, n_ada = [], [0]
        F0_STEPS = FF // CW
        F0_UNITS = ADA_UNITS + 24

        def add_unit(slots=None):
            name, u = units[len(unit_pieces)]
            w = A["ada_w_2"][0] if name == "ada2" else A["ada_w"][int(name[-1])]
            js = (u,) if name == "ada2" else (2 * u, 2 * u + 1)
            unit_pieces.append([len(stream) + i for i in range(len(js))])
            for j in js:
                n_ada[0] += 1
                add(cols(w, j * CW), ("ada_used", n_ada[0]), slots and slots[(n_ada[0] - 1) % len(slots)])

        def units_after(f):
            upto = lambda f: min(F0_UNITS, (f * F0_UNITS + 20) // 21)
            return range(ADA_UNITS + upto(f), ADA_UNITS + upto(f + 1))

        def mark(name):
            marks[name] = (len(stream), n_plain[0])
            base[name] = tile0[0]

        def steps_of(ph, n, first_slot=None, wrap=None):
            mark(ph)
            for s in range(n):
                for part in range(3):
                    slot = None if wrap is None else (first_slot + 3 * wrap(s) + part) % (3 * 3 if ph == "f1" else 6)
                    name = "down_done" if part == 2 else "h_ready"
                    add((ph, s, part), (name, tile0[0] + 2 * s + 2), slot)
            tile0[0] += 2 * n

        for u in range(ADA_UNITS):
            add_unit()
        step_at = {}
        for l in range(LAYERS):
            mark(f"win{l}")
            for c0 in WIN1:
                plain(A["w_in"][l], c0)
            mark(f"wout{l}")
            for j in range(4):
                plain(A["w_out"][l], j * CW)
            if l == 0:
                mark("f0")
                step_at["f0"] = []
                for st in range(F0_STEPS + 2):
                    if st < F0_STEPS:
                        step_at["f0"].append(len(stream))
                        for part in range(3):
                            add(("f0", st, part), ("down_done" if part == 2 else "h_ready", 2 * st + 2))
                    if st >= 2:
                        for f in (2 * st - 4, 2 * st - 3):
                            for _ in units_after(f):
                                add_unit(beside)
                tile0[0] += 2 * F0_STEPS
            else:
                steps_of("f1", E1 * STEPS1, 0, lambda s: s % STEPS1 % 3)
        mark("win2")
        for c0 in WIN2:
            plain(A["w_in_2"][0], c0)
        mark("wout2")
        for j in range(4):
            plain(A["w_out_2"][0], j * CW)
        step_at["sh"] = [len(stream)]
        steps_of("sh", 1, 0, lambda s: 0)
        mark("f2")
        for p in range(2):
            for q in range(6):
                add(("f2", p, q), ("pair_h" if q < 4 else "pair_y1", p + 1), (3 + 6 * p + q) % PAIR_SLOTS)
                if p == 1 and stream[-1]["slot"] >= RING:
                    stream[-1]["free"] = ("x_part", 12)
        mark("end")
        piece_sem = [sem(f"piece_in_{i}") for i in range(RING + BESIDE)]

        def ffn_weights(ph, s):
            if ph == "f0":
                w1, w3, w2, c = A["ffn_w1"][0], A["ffn_w3"][0], A["ffn_w2"][0], s
            elif ph == "f1":
                e, c = s
                w1, w3, w2 = A["moe_w1"][0][e], A["moe_w3"][0][e], A["moe_w2"][0][e]
            elif ph == "sh":
                w1, w3, w2, c = A["shared_w1_2"][0], A["shared_w3_2"][0], A["shared_w2_2"][0], 0
            else:
                w1, w3, w2, c = A["exp_w1_2"][0][s], A["exp_w3_2"][0][s], A["exp_w2_2"][0][s], 0
            v1, v3 = (w.rearrange("(k p) f -> p k f", p=P) for w in (w1, w3))
            v2_ = w2.rearrange("(c k p) n -> c p k n", p=P, k=2)
            if isinstance(c, int):
                return v1[:, :, c * CW:(c + 1) * CW], v3[:, :, c * CW:(c + 1) * CW], v2_[c]
            return v1[:, :, bass.ts(c, CW)], v3[:, :, bass.ts(c, CW)], v2_[c]

        def slot_view(n):
            return arena[:, stream[n]["slot"] * SLOT:(stream[n]["slot"] + 1) * SLOT]

        def piece(n):
            return slot_view(n).rearrange("p (k f) -> p k f", k=KD)

        def piece_down(n):
            return slot_view(n).rearrange("p (k f) -> p k f", k=2)

        def arrived(eng, n, later=0):
            eng.wait_ge(piece_sem[stream[n]["slot"]], (later + stream[n]["use"]) * 16)

        def uses_per_expert(n):
            return 4 if stream[n]["slot"] < 6 else 3

        def unit_pieces_before(n):
            return sum(len(p) for p in unit_pieces[:n])

        block = ctx.enter_context(nc.Block())

        def rows(eng, l, row, ap):
            n = ap.shape[0]
            eng.dma_start(VN[row:row + n, l, :], ap).then_inc(sem("vec_in" if l == 2 else "layer_vec_in"), 16)

        @block.sync
        def _(sp):
            def load(n):
                p = stream[n]
                if p["free"] is not None:
                    name, value = p["free"]
                    sp.wait_ge(sem(name), value)
                if isinstance(p["what"], tuple):
                    ph, s, part = p["what"]
                    if ph == "f2":
                        s, part = 2 * s + part % 2, part // 2
                    dst = piece_down(n) if part == 2 else piece(n)
                    src = ffn_weights(ph, (s // STEPS1, s % STEPS1) if ph == "f1" else s)[part]
                else:
                    dst, src = piece(n), p["what"]
                sp.dma_start(dst, src).then_inc(piece_sem[p["slot"]], 16)

            def load_experts1():
                n0 = marks["f1"][0]
                tiles, pieces = 2 * STEPS1, 3 * STEPS1
                for n in range(n0, n0 + pieces):
                    load(n)
                with sp.Fori(1, E1) as e:
                    for n in range(n0 + pieces, n0 + 2 * pieces):
                        name, value = stream[n]["free"]
                        sp.wait_ge(sem(name), e * tiles + (value - tiles))
                        s, part = divmod(n - n0 - pieces, 3)
                        sp.dma_start(piece_down(n) if part == 2 else piece(n), ffn_weights("f1", (e, s))[part])\
                          .then_inc(piece_sem[stream[n]["slot"]], 16)

            for l in range(LAYERS):
                rows(sp, l, V_ADAB, A["ada_b"][l].rearrange("(a p) -> a p", p=P))
                rows(sp, l, V_G1, A["norm_mix_g"][l].rearrange("(a p) -> a p", p=P))
                rows(sp, l, V_G2, A["norm_ffn_g"][l].rearrange("(a p) -> a p", p=P))
                rows(sp, l, V_CONVW, A["rg_conv_w"][l].rearrange("w (a p) -> (w a) p", p=P))
                rows(sp, l, V_CONVB, A["rg_conv_b"][l].rearrange("(a p) -> a p", p=P))
                rows(sp, l, V_BA, A["rg_ba"][l].rearrange("(a p) -> a p", p=P))
                rows(sp, l, V_BX, A["rg_bx"][l].rearrange("(a p) -> a p", p=P))
                rows(sp, l, V_LAM, A["rg_lambda"][l].rearrange("(a p) -> a p", p=P))
                rows(sp, l, V_BG, A["gla_bg"][l].rearrange("(a p) -> a p", p=P))
                rows(sp, l, V_GLAG, A["gla_norm_g"][l].rearrange("(a p) -> a p", p=P))
                rows(sp, l, V_EXTRA, (A["c"][0] if l == 0 else A["final_g"]).rearrange("(a p) -> a p", p=P))
            for n in range(marks["f1"][0]):
                load(n)
            load_experts1()
            for n in range(marks["win2"][0], marks["end"][0]):
                load(n)
            with sp.Fori(1, PAIRS // 2) as i:
                for n in range(marks["f2"][0], marks["end"][0]):
                    name, value = stream[n]["release"]
                    sp.wait_ge(sem(name), (i - 1) * 2 + value)
                    _, p, q = stream[n]["what"]
                    sp.dma_start(piece(n) if q < 4 else piece_down(n), ffn_weights("f2", i * 4 + (2 * p + q % 2))[q // 2])\
                      .then_inc(piece_sem[stream[n]["slot"]], 16)
            sp.wait_ge(sem("out_tile"), 2)
            sp.dma_start(out.rearrange("b (a p) d -> p (b a) d", p=P),
                         hflat[:, 0:2048].rearrange("p (a d) -> p a d", a=TT)).then_inc(sem("stored"), 16)
            sp.wait_ge(sem("stored"), 16)

        XN, CN = TMP[:, 0:2048], TMP[:, 2048:4096]

        @block.gpsimd
        def _(pool):
            nc.gpsimd.memset(ones[:], 1.0).then_inc(sem("ones_ready"), 1)
            nc.gpsimd.memset(wa_bd[:], 0.0).then_inc(sem("pool_zero"), 1)
            nc.gpsimd.memset(wx_bd[:], 0.0).then_inc(sem("pool_zero"), 1)

            for row, name in ((V_ADAB, "ada_b_2"), (V_G1, "norm1_g_2"), (V_G2, "norm2_g_2"),
                              (W_DG, "dattn_norm_g_2"), (W_RG, "ret_norm_g_2"), (W_C, "c_2")):
                rows(pool, 2, row, A[name][0].rearrange("(a p) -> a p", p=P))
            rows(pool, 2, W_FG, A["final_norm_g_2"].rearrange("(a p) -> a p", p=P))
            rows(pool, 2, W_CC, A["c_ctx_2"].rearrange("(a p) -> a p", p=P))
            for k, name in enumerate(("ret_decay_fwd_2", "ret_decay_bwd_2")):
                pool.dma_start(small[:, 8 + 4 * k:12 + 4 * k],
                               A[name][0:1, :].to_broadcast([P, 4])).then_inc(sem("scalars_in"), 16)
            for k, name in enumerate(("lambda_q1_2", "lambda_k1_2", "lambda_q2_2", "lambda_k2_2")):
                pool.dma_start(small[:, 256 + 64 * k:320 + 64 * k],
                               A[name][0:1, :].to_broadcast([P, 64])).then_inc(sem("scalars_in"), 16)

            def layer_weights(l):
                s = sem("small_w_in")
                pool.dma_start(wf[:], A["w_in"][l].rearrange("(k p) f -> p k f", p=P)[:, :, 2560:2576]).then_inc(s, 16)
                pool.dma_start(wg2[:], A["gla_wg2"][l]).then_inc(s, 16)
                for bd, name in ((wa_bd, "rg_wa"), (wx_bd, "rg_wx")):
                    for half in range(2):
                        src = A[name][l].rearrange("(c b) d e -> b d c e", b=2)[half]
                        pool.dma_start(bd[64 * half:64 * half + 64, :, 64 * half:64 * half + 64],
                                       src).then_inc(s, 16)

            pool.wait_ge(sem("pool_zero"), 2)
            layer_weights(0)
            pool.dma_start(router[:, :, 0:8], A["router_w"][0].rearrange("(k p) f -> p k f", p=P)).then_inc(sem("router_in"), 16)
            pool.wait_ge(sem("gla_u_ready"), 1)
            layer_weights(1)
            pool.wait_ge(sem("logits_ready"), 1)
            pool.dma_start(router[:], A["router_w_2"][0].rearrange("(k p) f -> p k f", p=P)).then_inc(sem("router_in"), 16)
            pool.dma_start(small[:, 192:256], A["router_bias_2"][0:1, :].to_broadcast([P, 64])).then_inc(sem("router_in"), 16)

        def by_class(eng, c, body):
            for k, width in enumerate(CLASSES):
                with eng.If(c == k):
                    body(width)

        def load_meta(eng, row, e, most, least=0):
            return eng.value_load(meta[0:1, row, bass.ds(e, 1)], min_val=least, max_val=most)

        def further_rounds(eng, p, body):
            some = load_meta(eng, 0, p, 1)
            with eng.If(some == 1):
                for r in (3, 2):
                    flag = load_meta(eng, r, p, 1)
                    with eng.If(flag == 1):
                        body(load_meta(eng, 2 + r, p, 3 * PAIRS, 1), r)
                body(load_meta(eng, 1, p, 3 * PAIRS, 1), 1)

        def each_pair(eng, pair):
            pair(0, 0, 0, first=True)
            with eng.Fori(0, PAIRS // 2 - 1) as i:
                pair(i * 2 + 1, 1, i)
                pair(i * 2 + 2, 0, i + 1)
            pair(PAIRS - 1, 1, PAIRS // 2 - 1, last_one=True)

        NVEC, NVEC_LAYERS, NSCALARS = 16 * 8, 16 * 2 * 11, 16 * 6

        @block.tensor
        def _(pe):
            mm = nc.tensor.matmul

            def transpose_in(src, half):
                for k in range(KD):
                    last = nc.tensor.transpose(B[2 * half + k // 4][:, (k % 4) * P:(k % 4 + 1) * P],
                                               src[:, k * P:(k + 1) * P], ident)
                last.then_inc(sem("xin_ready"), 1)

            def ada_unit(n):
                name, u = units[n]
                pe.wait_ge(sem("ada_used"), unit_pieces_before(n + 1))
                for i in range(2):
                    for m in range(2):
                        o = 64 + 48 * i + 2 * u + m if name == "ada2" else 2 * (2 * u + i) + m
                        last = mm(B[7][:, o:o + 1], ffn_g[:, 2 * (n % 2) + i, m * P:(m + 1) * P], ones[:, 0:1],
                                  start=True, stop=True)
                last.then_inc(sem("ada_psum"), 1)

            def norm(n, bank=6):
                for k in range(KD):
                    if k % 4 == 0:
                        pe.wait_ge(sem("sq_ready"), 2 * n + 1 + k // 4)
                    last = mm(B[bank][:, 0:T], ones[:], sq[:, k, :], start=(k == 0), stop=(k == KD - 1))
                last.then_inc(sem("ss_ready"), 1)

            def project_T(n, bank, rhs, width=T):
                arrived(pe, n)
                w = piece(n)
                for m in range(2):
                    dst = B[bank[m]][:, 0:width] if width > T else B[bank][:, m * T:(m + 1) * T]
                    for k in range(KD):
                        last = mm(dst, w[:, k, m * P:(m + 1) * P], rhs[:, k, 0:width],
                                  start=(k == 0), stop=(k == KD - 1))
                last.then_inc(sem("plain_used"), 1)

            def project_nat(n, bank, lhs):
                arrived(pe, n)
                w = piece(n)
                for a in range(len(lhs)):
                    for k in range(KD):
                        last = mm(B[bank[a // 2]][:, (a % 2) * CW:(a % 2 + 1) * CW], lhs[a](k), w[:, k, :],
                                  start=(k == 0), stop=(k == KD - 1))
                last.then_inc(sem("plain_used"), 1)

            def out_proj(name, banks, release):
                n0 = marks[name][0]
                for j in range(4):
                    if j >= len(banks):
                        pe.wait_ge(*release(j))
                    arrived(pe, n0 + j)
                    w = piece(n0 + j)
                    for m in range(2):
                        for k in range(KD):
                            last = mm(B[banks[j % len(banks)]][:, m * T:(m + 1) * T], w[:, k, m * P:(m + 1) * P],
                                      mixT[:, k, :], start=(k == 0), stop=(k == KD - 1))
                    last.then_inc(sem("plain_used"), 1)

            def mixer1(l):
                pe.wait_ge(sem("h_norm"), 2 * l + 1)
                pe.wait_ge(sem("small_w_in"), 16 * 6 * (l + 1))
                for k in range(KD):
                    last = mm(B[4][0:16, 0:T], wf[:, k, :], hT1[:, k, :], start=(k == 0), stop=(k == KD - 1))
                last.then_inc(sem("flow_ready"), 1)
                n0 = marks[f"win{l}"][0]
                for j in range(10):
                    if j >= 4:
                        pe.wait_ge(sem("z_in"), 10 * l + j - 3)
                    if j in (4, 5):
                        project_nat(n0 + j, [j % 4], [lambda k, a=a: hT1[:, k, a * P:(a + 1) * P] for a in range(TT)])
                    else:
                        project_T(n0 + j, j % 4, hT1)
                    if j == 1:
                        pe.wait_ge(sem("flT_ready"), l + 1)
                        for m in range(2):
                            last = mm(B[5][:, m * T:(m + 1) * T], wg2[:, m * P:(m + 1) * P], flT[:, :], start=True, stop=True)
                        last.then_inc(sem("lf_ready"), 1)
                    if j == 6:
                        pe.wait_ge(sem("conv_ready"), l + 1)
                        pe.wait_ge(sem("lf_done"), l + 1)
                        for g, (bank, bd, pair) in enumerate(((4, wa_bd, 0), (5, wa_bd, 1), (6, wx_bd, 0), (4, wx_bd, 1))):
                            if g == 3:
                                pe.wait_ge(sem("rgate_done"), 4 * l + 1)
                            for m in range(2):
                                c = 2 * pair + m
                                last = mm(B[bank][:, m * T:(m + 1) * T], bd[:, c, :], uc[:, c * T:(c + 1) * T], start=True, stop=True)
                            last.then_inc(sem("rgate_ready"), 1)
                pe.wait_ge(sem("gla_in"), l + 1)
                pe.wait_ge(sem("rgate_done"), 4 * l + 4)
                for a in range(TT):
                    for pr in range(2):
                        last = nc.tensor.transpose(B[4][:, a * T + pr * P:a * T + (pr + 1) * P],
                                                   kend[:, pr * T + a * P:pr * T + (a + 1) * P], ident)
                last.then_inc(sem("kendn_ready"), 1)
                pe.wait_ge(sem("z_in"), 10 * l + 10)
                for par in range(2):
                    r = slice(64 * par, 64 * par + 64)
                    for o in range(0, 512, P):
                        last = mm(B[par][:, o:o + P], kloc[r, o:o + P], qloc[r, o:o + P], start=True, stop=True)
                    last.then_inc(sem("gla_s_ready"), 1)
                pe.wait_ge(sem("kendn_done"), l + 1)
                for n in range(NCH - 1):
                    for h in range(HEADS):
                        r = slice(64 * (n % 2), 64 * (n % 2) + 64)
                        bank, o = 5 + n % 2, (n // 2) * T + (h // 2) * P
                        last = mm(B[bank][64 * (h % 2):64 * (h % 2) + 64, o:o + P],
                                  kendn[r, n // 2, h * 64:(h + 1) * 64], vn[r, n // 2, h * P:(h + 1) * P],
                                  start=True, stop=True)
                last.then_inc(sem("gla_u_ready"), 1)
                pe.wait_ge(sem("gla_sT_done"), 2 * (l + 1))
                pe.wait_ge(sem("state_ready"), 3 * (l + 1))
                for h in range(HEADS):
                    rows = slice(64 * (h % 2), 64 * (h % 2) + 64)
                    for a in range(TT):
                        o = (h // 2) * T + a * P
                        bank = B[2 + h % 2]
                        last = mm(bank[:, o:o + P], vn[:, a, h * P:(h + 1) * P], sT[:, a, h * P:(h + 1) * P],
                                  start=True, stop=False, skip_group_check=True)
                        for n in range(max(2 * a, 1), 2 * a + 2):
                            oo = (h // 2) * T + n * CH
                            last = mm(bank[:, oo:oo + CH], St[rows, n - 1, h // 2, :],
                                      qin[rows, (h // 2) * T + n * CH:(h // 2) * T + (n + 1) * CH],
                                      start=False, stop=(n == 2 * a + 1), skip_group_check=True)
                    if h >= 2:
                        last.then_inc(sem("gla_o_ready"), 1)
                for b in range(2):
                    pe.wait_ge(sem("gla_sq_ready"), 2 * l + b + 1)
                    mm(B[b][:, :], ones[:], sqf[:, b * 512:(b + 1) * 512], start=True, stop=True).then_inc(sem("gla_ss_ready"), 1)
                pe.wait_ge(sem("mix_ready"), l + 1)
                out_proj(f"wout{l}", [4, 5, 6], lambda j: (sem("x_part"), 4 * l + 1))

            def route(l, E):
                pe.wait_ge(sem("router_in"), 16 if l == 0 else 48)
                for a in range(TT):
                    for k in range(KD):
                        last = mm(B[7][:, a * E:(a + 1) * E], hT1[:, k, a * P:(a + 1) * P], router[:, k, 0:E],
                                  start=(k == 0), stop=(k == KD - 1))
                last.then_inc(sem("logits_ready"), 1)
                for a in range(TT):
                    for k in range(KD):
                        last = nc.tensor.transpose(B[2 * a + k // 4][:, (k % 4) * P:(k % 4 + 1) * P],
                                                   hT1[:, k, a * P:(a + 1) * P], ident)
                    last.then_inc(sem("hn_psum"), 1)

            def places(l, E):
                pe.wait_ge(sem("mask_ready"), l + 1)
                su = C[:, C_SU:C_SU + P]
                for o, parts in ((0, ((ones[:], msk[:, 0, 0:E]), (ones[:], msk[:, 1, 0:E]))),
                                 (1, ((ones[:], mskx[:, 0, 0:E]), (ones[:], mskx[:, 1, 0:E]))),
                                 (2, ((su, msk[:, 0, 0:E]),)),
                                 (3, ((ones[:], msk[:, 0, 0:E]), (su, msk[:, 1, 0:E])))):
                    for n, (w, m) in enumerate(parts):
                        last = mm(B[7][:, o * E:(o + 1) * E], w, m, start=(n == 0), stop=(n == len(parts) - 1))
                last.then_inc(sem("places_psum"), 1)

            def up_tile(n, m, rhs, width, later=None, bank=4):
                for part in range(2):
                    if m == 0:
                        arrived(pe, n + part, 0 if later is None else later(n + part))
                    w = piece(n + part)
                    for k in range(KD):
                        last = mm(B[bank + m][:, part * T:part * T + width], w[:, k, m * P:(m + 1) * P], rhs(k),
                                  start=(k == 0), stop=(k == KD - 1))
                last.then_inc(sem("h_ready"), 1)

            def down_tile(n, m, a_value, width, first, last_tile, later=None):
                pe.wait_ge(sem("a_ready"), a_value)
                if m == 0:
                    arrived(pe, n + 2, 0 if later is None else later(n + 2))
                w = piece_down(n + 2)
                for d in range(KD):
                    o = d * width
                    last = mm(B[o // 512][:, o % 512:o % 512 + width], w[:, m, d * P:(d + 1) * P],
                              ffn_a[:, m, 0:width], start=(first and o % 512 == 0), stop=last_tile,
                              skip_group_check=True)
                last.then_inc(sem("down_done"), 1)

            def dense(ph):
                starts, t0 = step_at[ph], base[ph]
                tiles = 2 * len(starts)
                hh = lambda k: hT1[:, k, :]
                up_tile(starts[0], 0, hh, T)
                for f in range(tiles):
                    if f + 1 < tiles:
                        up_tile(starts[(f + 1) // 2], (f + 1) % 2, hh, T)
                    if ph == "f0" and f >= 1:
                        for n in units_after(f - 1):
                            ada_unit(n)
                    down_tile(starts[f // 2], f % 2, t0 + f + 1, T, f == 0, f + 1 == tiles)
                if ph == "f0":
                    for n in units_after(tiles - 1):
                        ada_unit(n)

            def gather(g0, e, width):
                pe.wait_ge(sem("Pe_ready"), e + (g0 + 1))
                for half in range(2):
                    if width == 256 and half == 1:
                        pe.wait_ge(sem("heT_ready"), e * 2 + (2 * g0 + 1))
                    for kk in range(4):
                        k = 4 * half + kk
                        o = (half * 512 if width <= P else 0) + kk * width
                        for a in range(TT):
                            last = mm(B[6 + o // 512][:, o % 512:o % 512 + width], hn[:, a, k * P:(k + 1) * P],
                                      Pe[:, a, 0:width], start=(a == 0), stop=(a == 1))
                    last.then_inc(sem("he_psum"), 1)

            def narrow_expert(e):
                n0, t0 = marks["f1"][0], base["f1"]
                turn0 = load_meta(pe, 2, e, E1 * STEPS1, 1)
                nth = load_meta(pe, 3, e, E1, 1)
                halves = [(x, slice(HALF * x, HALF * (x + 1))) for x in range(2)]

                def up(s, later):
                    n = n0 + 3 * s
                    for part in range(2):
                        arrived(pe, n + part, later(n + part))
                        for k in range(KD):
                            for x, r in halves:
                                last = mm(B[4 + s % 3][r, part * T:part * T + P], heT[:, k * HALF:(k + 1) * HALF],
                                          piece(n + part)[:, k, x * P:(x + 1) * P], start=(k == 0), stop=(k == KD - 1))
                        last.then_inc(sem("h_ready"), 1)

                def step(s, i=0, first=False, end=False):
                    n = n0 + 3 * s
                    later = lambda n: e * uses_per_expert(n) + i
                    if not end:
                        up(s + 1, later)
                    pe.wait_ge(sem("a_ready"), e * (2 * STEPS1) + i * 6 + (t0 + 2 * s + 2))
                    o = P * (s % 3)
                    nc.tensor.transpose(B[7][:, 0:P], na[:, o:o + P], ident).then_inc(sem("narrow_turned"), 1)
                    if first:
                        pe.wait_ge(sem("outs_read"), e + 2)
                    pe.wait_ge(sem("narrow_aT"), turn0 + i * 3 + s)
                    arrived(pe, n + 2, later(n + 2))
                    for m in range(2):
                        for x, r in halves:
                            last = mm(B[0][r, :], naT[:, o + HALF * m:o + HALF * (m + 1)],
                                      piece_down(n + 2)[:, m, x * 512:(x + 1) * 512],
                                      start=(first and m == 0), stop=end, skip_group_check=True)
                        last.then_inc(sem("down_done"), 1)

                pe.wait_ge(sem("heT_ready"), e * 2 + 2)
                up(0, lambda n: e * uses_per_expert(n))
                for s in range(3):
                    step(s, first=(s == 0))
                with pe.Fori(1, 3) as i:
                    for s in range(3):
                        step(s, i)
                for s in range(9, STEPS1):
                    step(s, end=(s + 1 == STEPS1))
                pe.wait_ge(sem("narrow_out"), nth)
                for j in range(4):
                    last = nc.tensor.transpose(B[1][:, j * P:(j + 1) * P], ns[:, j * P:(j + 1) * P], ident)
                last.then_inc(sem("narrow_outT"), 1)

            def experts1():
                n0, t0 = marks["f1"][0], base["f1"]
                pe.wait_ge(sem("outs_read"), 2)
                pe.wait_ge(sem("meta_ready"), 1)
                with pe.Fori(0, E1) as e:
                    c = load_meta(pe, 0, e, 2)

                    def expert(width):
                        gather(0, e, width)
                        if width == HALF:
                            return narrow_expert(e)
                        hh = lambda k: heT[:, k * width:(k + 1) * width]

                        def step(s, i=0, first=False, end=False):
                            n = n0 + 3 * s
                            later = lambda n: e * uses_per_expert(n) + i
                            av = e * (2 * STEPS1) + i * 6 + (t0 + 2 * s)
                            up_tile(n, 1, hh, width, later)
                            if first:
                                pe.wait_ge(sem("outs_read"), e + 2)
                            down_tile(n, 0, av + 1, width, first, False, later)
                            if not end:
                                up_tile(n + 3, 0, hh, width, later)
                            down_tile(n, 1, av + 2, width, False, end, later)

                        pe.wait_ge(sem("heT_ready"), e * 2 + 2)
                        up_tile(n0, 0, hh, width, lambda n: e * uses_per_expert(n))
                        for s in range(3):
                            step(s, first=(s == 0))
                        with pe.Fori(1, 3) as i:
                            for s in range(3):
                                step(s, i)
                        for s in range(9, STEPS1):
                            step(s, end=(s + 1 == STEPS1))

                    by_class(pe, c, expert)

            def pair_gather(b, v):
                pe.wait_ge(sem(b["name"] + "_P"), v)
                for half in range(2):
                    for kk in range(4):
                        k = 4 * half + kk
                        for a in range(TT):
                            last = mm(B[5 + half][:, kk * P:(kk + 1) * P], hn[:, a, k * P:(k + 1) * P],
                                      b["P"][:, a * P:(a + 1) * P], start=(a == 0), stop=(a == 1))
                    last.then_inc(sem(b["name"] + f"_he{half}"), 1)

            def pair_up(b, v, n, later):
                pe.wait_ge(sem(b["name"] + "_heT"), v * 2)
                for part in range(2):
                    arrived(pe, n + 2 * part, later)
                    arrived(pe, n + 2 * part + 1, later)
                    for k in range(KD):
                        for x in range(2):
                            r = slice(HALF * x, HALF * (x + 1))
                            last = mm(B[4][r, part * CW:(part + 1) * CW], b["heT"][:, k * P + HALF * x:k * P + HALF * (x + 1)],
                                      piece(n + 2 * part + x)[:, k, :], start=(k == 0), stop=(k == KD - 1))
                last.then_inc(sem(b["name"] + "_h"), 1)

            def pair_turn(b, v):
                pe.wait_ge(sem(b["name"] + "_a"), v)
                pe.wait_ge(sem(b["name"] + "_W"), v)
                for o, src in ((0, b["a"]), (2, b["W"])):
                    for m in range(2):
                        last = nc.tensor.transpose(B[7][:, (o + m) * P:(o + m + 1) * P], src[:, m * P:(m + 1) * P], ident)
                last.then_inc(sem(b["name"] + "_turned"), 1)

            def pair_down(b, v, n, later):
                pe.wait_ge(sem(b["name"] + "_aw"), v)
                for x in range(2):
                    arrived(pe, n + 4 + x, later)
                for half in range(2):
                    for m in range(2):
                        for x in range(2):
                            r = slice(HALF * x, HALF * (x + 1))
                            last = mm(B[4 + 3 * half][r, :], b["aw"][:, m * P + HALF * x:m * P + HALF * (x + 1)],
                                      piece_down(n + 4 + x)[:, m, half * 512:(half + 1) * 512], start=(m == 0), stop=(m == 1))
                    last.then_inc(sem(b["name"] + f"_y{half}"), 1)

            def pair_combine(b, v):
                pe.wait_ge(sem(b["name"] + "_Y0"), v)
                pe.wait_ge(sem(b["name"] + "_Y1"), v)
                for k in range(KD):
                    last = mm(B[k // 2][:, (k % 2) * T:(k % 2 + 1) * T], b["Y"][:, k * P:(k + 1) * P], b["aw"][:, T:2 * T],
                              start=False, stop=True, skip_group_check=True)
                return last

            def experts2():
                f = first_round

                def pair(p, parity, later, first=False, last_one=False):
                    n = marks["f2"][0] + 6 * parity

                    def more(v, r):
                        pe.wait_ge(sem("pair_heT"), p * 2 + 2)
                        pair_gather(more_round, v)
                        if not first:
                            pe.wait_ge(sem("pair_Y0"), p)
                            pe.wait_ge(sem("pair_Y1"), p)
                        pair_up(more_round, v, n, later)
                        pair_turn(more_round, v)
                        pair_down(more_round, v, n, later)
                        pair_combine(more_round, v)

                    further_rounds(pe, p, more)
                    if not first:
                        pe.wait_ge(sem("pair_Y0"), p)
                    pair_up(f, p + 1, n, later)
                    if not first:
                        pair_combine(f, p)
                    pair_turn(f, p + 1)
                    if not last_one:
                        pair_gather(f, p + 2)
                    pair_down(f, p + 1, n, later)

                pe.wait_ge(sem("meta_ready"), 2)
                pair_gather(f, 1)
                each_pair(pe, pair)
                pair_combine(f, PAIRS).then_inc(sem("sum_done"), 1)

            def combine_slots(b0, blocks, y, ws):
                def turn(b):
                    if b:
                        pe.wait_ge(sem("block_in"), 2 * (b0 + b))
                    else:
                        pe.wait_ge(sem("outs_read"), E1 + 2)
                        pe.wait_ge(sem("w_kept"), E1)
                    for k in range(KD):
                        nc.tensor.transpose(B[4 + k // 4][:, (k % 4) * P:(k % 4 + 1) * P], y[:, k, b * P:(b + 1) * P], ident)
                    for a in range(TT):
                        last = nc.tensor.transpose(B[6][:, a * P:(a + 1) * P], ws[:, a, b * P:(b + 1) * P], ident)
                    last.then_inc(sem("block_psum"), 1)

                turn(0)
                for b in range(blocks):
                    if b + 1 < blocks:
                        turn(b + 1)
                    pe.wait_ge(sem("block_in"), 2 * (b0 + b + 1))
                    for k in range(KD):
                        last = mm(B[k // 2][:, (k % 2) * T:(k % 2 + 1) * T], Yn[:, b % 2, k * P:(k + 1) * P], PTs[:, b % 2, :],
                                  start=(b == 0 and k % 2 == 0), stop=(b + 1 == blocks), skip_group_check=True)
                    last.then_inc(sem("block_done"), 1)

            def mixer2():
                n0 = marks["win2"][0]
                pe.wait_ge(sem("h_norm"), 6)
                pe.wait_ge(sem("h_norm"), 7)
                x_t = [lambda k, a=a: hcat[:, k, a * P:(a + 1) * P] for a in range(4)]
                for j in range(12):
                    bk = [2 * (j % 2), 2 * (j % 2) + 1]
                    if j >= 2:
                        pe.wait_ge(sem("z2_in"), j - 1)
                    if j == 0:
                        project_T(n0, 0, hcat)
                    elif j == 1:
                        arrived(pe, n0 + 1)
                        w = piece(n0 + 1)
                        for m in range(2):
                            for k in range(KD):
                                mm(B[2][:, m * T:(m + 1) * T], w[:, k, m * P:(m + 1) * P], hcat[:, k, 0:T],
                                   start=(k == 0), stop=(k == KD - 1))
                        for a in range(2):
                            for k in range(KD):
                                last = mm(B[3][:, a * CW:(a + 1) * CW], hcat[:, k, (2 + a) * P:(3 + a) * P], w[:, k, :],
                                          start=(k == 0), stop=(k == KD - 1))
                        last.then_inc(sem("plain_used"), 1)
                    elif j in (2, 3, 6, 7):
                        project_nat(n0 + j, bk, x_t)
                    elif j in (4, 5):
                        project_T(n0 + j, bk, hcat, width=2 * T)
                    else:
                        project_T(n0 + j, bk[0], hcat)
                pe.wait_ge(sem("z2_in"), 12)
                for g in range(6):
                    if g >= 2:
                        pe.wait_ge(sem("rope_done"), g - 1)
                    for m in range(2):
                        src = [rq[:, m, :], rk[:, m, :], k2[:, m, T:], k2[:, 2 + m, T:], q2[:, m, :], q2[:, 2 + m, :]][g]
                        last = mm(B[4 + g % 2][:, m * T:(m + 1) * T], C[:, C_ROT:C_ROT + P], src, start=True, stop=True)
                    last.then_inc(sem("rot_ready"), 1)
                pe.wait_ge(sem("kdec_ready"), 1)
                for pr in range(2):
                    for dr in range(2):
                        for hh in range(2):
                            h = 2 * pr + hh
                            for a in range(2):
                                last = mm(B[6][64 * hh:64 * hh + 64, (pr * 2 + dr) * P:(pr * 2 + dr + 1) * P],
                                          kdec[:, dr, a, h * 64:(h + 1) * 64], rv[:, 2 + a, h * P:(h + 1) * P],
                                          start=(a == 0), stop=(a == 1))
                last.then_inc(sem("s2_psum"), 1)
                pe.wait_ge(sem("rope_done"), 2)
                for h in range(HEADS):
                    r = slice(64 * (h % 2), 64 * (h % 2) + 64)
                    if h >= 2:
                        pe.wait_ge(sem("sD_ready"), h - 1)
                    for a in range(2):
                        last = mm(B[h % 2][:, a * T:(a + 1) * T], rk[r, h // 2, a * P:(a + 1) * P], rq[r, h // 2, :],
                                  start=True, stop=True)
                    last.then_inc(sem("ret_s"), 1)
                    if h >= 1:
                        ret_out(h - 1)
                ret_out(HEADS - 1)
                for b in range(2):
                    pe.wait_ge(sem("ret_sq"), b + 1)
                    mm(B[b][:, :], ones[:], sqf[:, b * 512:(b + 1) * 512], start=True, stop=True).then_inc(sem("ret_ss"), 1)
                pe.wait_ge(sem("rope_done"), 6)
                pe.wait_ge(sem("ret_done"), 4)
                for g in range(8):
                    h, a = g // 2, g % 2
                    if g >= 2:
                        pe.wait_ge(sem("p_ready"), 2 * (g - 1))
                    for m in range(2):
                        r = slice(64 * m, 64 * m + 64)
                        mm(B[2 * (g % 2) + m][:, :], q2[r, h, a * P:(a + 1) * P], k2[r, h, :],
                           start=True, stop=True).then_inc(sem("att_s"), 1)
                    if g >= 1:
                        att_T(g - 1)
                    if g >= 3 and g % 2 == 1:
                        att_out((g - 3) // 2)
                att_T(7)
                att_out(3)
                pe.wait_ge(sem("mix_ready"), 3)
                out_proj("wout2", [0, 1, 2, 3], None)

            def ret_out(h):
                r = slice(64 * (h % 2), 64 * (h % 2) + 64)
                pe.wait_ge(sem("sD_ready"), h + 1)
                if h == 0:
                    pe.wait_ge(sem("S2_ready"), 1)
                    pe.wait_ge(sem("qdec_ready"), 1)
                dst = B[2 + h % 2][:, (h // 2) * T:(h // 2 + 1) * T]
                for a in range(2):
                    mm(dst, rv[:, a, h * P:(h + 1) * P], sD[:, h % 2, a * T:(a + 1) * T],
                       start=(a == 0), stop=False, skip_group_check=True)
                for dr in range(2):
                    last = mm(dst, S2[r, h // 2, dr, :], qdec[r, dr, h // 2, :], start=False, stop=(dr == 1),
                              skip_group_check=True)
                last.then_inc(sem("ret_o"), 1)

            def att_T(g):
                pe.wait_ge(sem("a2_ready"), g + 1)
                if g >= 1:
                    pe.wait_ge(sem("aT_ready"), g)
                for c in range(4):
                    last = nc.tensor.transpose(B[4][:, c * P:(c + 1) * P], pex[:, g % 2, 0, c * P:(c + 1) * P], ident)
                last.then_inc(sem("aT_psum"), 1)

            def att_out(h):
                pe.wait_ge(sem("aT_ready"), 2 * h + 2)
                for c in range(4):
                    vt = [2, 3, 0, 1][c]
                    last = mm(B[5 + h // 2][:, (h % 2) * T:(h % 2 + 1) * T], v2[:, vt, h * P:(h + 1) * P],
                              paT[:, h % 2, c, :], start=(c == 0), stop=(c == 3))
                last.then_inc(sem("att_o"), 1)
                if h % 2:
                    pe.wait_ge(sem("att_sq"), h // 2 + 1)
                    mm(B[7][:, :], ones[:], sqf[:, (h // 2) * 512:(h // 2 + 1) * 512], start=True, stop=True).then_inc(sem("att_ss"), 1)
                    pe.wait_ge(sem("att_rms"), h // 2 + 1)

            pe.wait_ge(sem("const_in"), 32)
            pe.wait_ge(sem("vec_in"), NVEC)
            pe.wait_ge(sem("layer_vec_in"), NVEC_LAYERS)
            for l, n in ((0, V_ROWS), (1, V_ROWS), (2, W_ROWS)):
                last = nc.tensor.transpose(B[6][:, l * P:l * P + n], VN[0:n, l, :], ident[0:n, 0:n])
            last.then_inc(sem("vec_ready"), 1)
            pe.wait_ge(sem("x_in"), 16)
            for a in range(TT):
                transpose_in(XN[:, a * D:(a + 1) * D], a)
            pe.wait_ge(sem("c_act"), 1)
            pe.wait_ge(sem("ones_ready"), 1)
            pe.wait_ge(sem("vec_done"), 1)
            norm(0)
            for n in range(ADA_UNITS):
                ada_unit(n)
            for l in range(LAYERS):
                if l:
                    norm(2)
                mixer1(l)
                norm(2 * l + 1)
                pe.wait_ge(sem("h_norm"), 2 * l + 2)
                if l == 0:
                    dense("f0")
                else:
                    route(0, E1)
                    places(0, E1)
                    experts1()
                    combine_slots(0, A1 // P, y1, w1s)
                pe.wait_ge(sem("x_ready"), l + 1)
            norm(4)
            norm(5)
            pe.wait_ge(sem("ctx_in"), 16)
            pe.wait_ge(sem("ctx_go"), 1)
            for a in range(TT):
                transpose_in(CN[:, a * D:(a + 1) * D], a)
            norm(6)
            mixer2()
            norm(7)
            pe.wait_ge(sem("h_norm"), 8)
            route(1, E2)
            pe.wait_ge(sem("outs_read"), E1 + 4)
            dense("sh")
            places(1, E2)
            experts2()
            norm(8)
            pe.wait_ge(sem("h_norm"), 9)
            for a in range(TT):
                for k in range(KD):
                    last = nc.tensor.transpose(B[2 * a + k // 4][:, (k % 4) * P:(k % 4 + 1) * P],
                                               xT[:, k, a * P:(a + 1) * P], ident)
                last.then_inc(sem("outT_ready"), 1)

        plain_at = {}
        for name in ("win0", "wout0", "win1", "wout1", "win2", "wout2"):
            plain_at[name] = marks[name][1]

        @block.scalar
        def _(act):
            fn = nc.scalar.activation
            count = [0]

            def link(ins):
                count[0] += 1
                ins.then_inc(sem("act_chain"), 1)
                act.wait_ge(sem("act_chain"), count[0])

            eps = small[:, 20:21]
            one = small[:, 21:22]

            def norm(n, src):
                if n >= 1:
                    act.wait_ge(sem("h_norm"), n)
                for half in range(2):
                    k = slice(4 * half, 4 * half + 4)
                    fn(sq[:, k, :], src[:, k, :], ACT.Square).then_inc(sem("sq_ready"), 1)
                act.wait_ge(sem("ss_ready"), n + 1)
                fn(rstd[:], B[6][:, 0:T], ACT.Sqrt, bias=eps, scale=1.0 / D).then_inc(sem("rms_ready"), 1)

            def silu(m, value, width):
                act.wait_ge(sem("h_ready"), value)
                fn(ffn_s[:, m, 0:width], B[4 + m][:, 0:width], ACT.Silu).then_inc(sem("s_ready"), 1)

            def dense(ph):
                for f in range(2 * len(step_at[ph])):
                    silu(f % 2, base[ph] + f + 1, T)

            def rows_of_h(l):
                for a in range(TT):
                    act.wait_ge(sem("hn_psum"), 2 * l + a + 1)
                    for half in range(2):
                        ins = fn(hn[:, a, half * 512:(half + 1) * 512], B[2 * a + half][:, :], ACT.Copy)
                    ins.then_inc(sem("outs_read"), 1)

            def keep_gathered(g0, e, width):
                for half in range(2):
                    act.wait_ge(sem("he_psum"), e * 2 + (2 * g0 + half + 1))
                    if width <= P:
                        ins = fn(heT[:, half * 4 * width:(half + 1) * 4 * width], B[6 + half][:, 0:4 * width], ACT.Copy)
                    else:
                        for b in range(2):
                            ins = fn(heT[:, half * 1024 + b * 512:half * 1024 + (b + 1) * 512], B[6 + b][:, :], ACT.Copy)
                    ins.then_inc(sem("heT_ready"), 1)

            def keep_outputs(y, value, start, width):
                act.wait_ge(sem("down_done"), value)
                per = 512 // width
                for b in range(KD // per):
                    ins = fn(y[:, b * per:(b + 1) * per, bass.ds(start, width)],
                             B[b][:, :].rearrange("p (k s) -> p k s", k=per), ACT.Copy)
                ins.then_inc(sem("outs_read"), 1)

            def experts1():
                act.wait_ge(sem("meta_ready"), 1)
                t0 = base["f1"]
                fn(small[:, 19:20], small[:, 20:21], ACT.Silu)
                def narrow_expert(e, start):
                    nth = load_meta(act, 3, e, E1, 1)

                    def silus(s, i=0):
                        act.wait_ge(sem("h_ready"), e * (2 * STEPS1) + i * 6 + (t0 + 2 * s + 2))
                        for half in range(2):
                            o = HALF * half
                            fn(ns[:, P * (s % 3) + o:P * (s % 3) + o + HALF], B[4 + s % 3][:, o:o + HALF],
                               ACT.Silu).then_inc(sem("s_ready"), 1)

                    with act.Fori(0, 3) as i:
                        for s in range(3):
                            silus(s, i)
                    for s in range(9, STEPS1):
                        silus(s)
                    act.wait_ge(sem("down_done"), e * (2 * STEPS1) + (t0 + 2 * STEPS1))
                    fn(ns, B[0][:, :], ACT.Copy).then_inc(sem("narrow_out"), 1)
                    act.wait_ge(sem("narrow_outT"), nth)
                    fn(y1.rearrange("p (x j) s -> p j x s", x=2)[:, :, :, bass.ds(start, HALF)],
                       B[1][:, :].rearrange("p (j x s) -> p j x s", j=4, x=2), ACT.Copy).then_inc(sem("outs_read"), 1)

                with act.Fori(0, E1) as e:
                    c = load_meta(act, 0, e, 2)
                    start = load_meta(act, 1, e, A1)

                    def expert(width):
                        keep_gathered(0, e, width)
                        if width == HALF:
                            return narrow_expert(e, start)
                        with act.Fori(0, STEPS1) as s:
                            for m in range(2):
                                silu(m, e * (2 * STEPS1) + s * 2 + (t0 + m + 1), width)
                        keep_outputs(y1, e * (2 * STEPS1) + (t0 + 2 * STEPS1), start, width)

                    by_class(act, c, expert)

            def pair_keep_gathered(b, v):
                for half in range(2):
                    act.wait_ge(sem(b["name"] + f"_he{half}"), v)
                    fn(b["heT"][:, half * 512:(half + 1) * 512], B[5 + half][:, :], ACT.Copy).then_inc(sem(b["name"] + "_heT"), 1)

            def pair_silu(b, v):
                act.wait_ge(sem(b["name"] + "_h"), v)
                fn(b["s"], B[4][:, 0:CW], ACT.Silu).then_inc(sem(b["name"] + "_s"), 1)

            def pair_keep_outputs(b, v):
                act.wait_ge(sem(b["name"] + "_y0"), v)
                fn(b["Y"][:, 0:512], B[4][:, :], ACT.Copy).then_inc(sem(b["name"] + "_Y0"), 1)

            def experts2():
                f = first_round

                def pair(p, parity, later, first=False, last_one=False):
                    def more(v, r):
                        pair_keep_gathered(more_round, v)
                        pair_silu(more_round, v)
                        pair_keep_outputs(more_round, v)

                    further_rounds(act, p, more)
                    pair_silu(f, p + 1)
                    if not last_one:
                        pair_keep_gathered(f, p + 2)
                    pair_keep_outputs(f, p + 1)

                act.wait_ge(sem("meta_ready"), 2)
                pair_keep_gathered(f, 1)
                each_pair(act, pair)

            def combine_slots(b0, blocks):
                for b in range(blocks):
                    act.wait_ge(sem("block_psum"), b0 + b + 1)
                    if b >= 2:
                        act.wait_ge(sem("block_done"), b0 + b - 1)
                    fn(Yn[:, b % 2, 0:512], B[4][:, :], ACT.Copy).then_inc(sem("block_in"), 1)

            def mixer1(l):
                act.wait_ge(sem("flow_ready"), l + 1)
                fn(flT, B[4][0:16, 0:T], ACT.Copy).then_inc(sem("flT_ready"), 1)
                W = plain_at[f"win{l}"]
                for j in range(10):
                    act.wait_ge(sem("plain_used"), W + j + 1)
                    b = B[j % 4]
                    if j == 0:
                        ins = fn(qT, b[:, :], ACT.Copy, scale=0.125)
                    elif j == 1:
                        ins = fn(kT, b[:, :], ACT.Copy)
                    elif j in (2, 3):
                        c = 2 * (j - 2)
                        ins = fn(upad[:, c:c + 2, 3:], b[:, :].rearrange("p (c t) -> p c t", c=2), ACT.Copy)
                    elif j in (4, 5):
                        ins = fn(vn[:, :, (j - 4) * CW:(j - 3) * CW], b[:, :].rearrange("p (a f) -> p a f", a=2), ACT.Copy)
                    elif j in (6, 7):
                        ins = fn(gT[:, (j - 6) * 512:(j - 5) * 512], b[:, :], ACT.Silu)
                    else:
                        ins = fn(gate[:, (j - 8) * 512:(j - 7) * 512], b[:, :], ACT.Gelu_apprx_tanh)
                    ins.then_inc(sem("z_in"), 1)
                    if j == 1:
                        act.wait_ge(sem("lf_ready"), l + 1)
                        for m in range(2):
                            fn(tmp1[:, m * T:(m + 1) * T], B[5][:, m * T:(m + 1) * T], ACT.Abs,
                               bias=VT[:, l, V_BG + m:V_BG + m + 1]).then_inc(sem("act_chain"), 1)
                        count[0] += 2
                        act.wait_ge(sem("act_chain"), count[0])
                        link(fn(tmp1, tmp1, ACT.Exp, scale=-1.0))
                        fn(tmp1, tmp1, ACT.Ln, bias=one).then_inc(sem("lsig_ready"), 1)
                    if j == 5:
                        gla_exps(l)
                    if j == 6:
                        for g in range(4):
                            act.wait_ge(sem("rgate_ready"), 4 * l + g + 1)
                            bank, dst, row, pair = ((4, rr, V_BA, 0), (5, rr, V_BA, 1), (6, ri, V_BX, 0), (4, ri, V_BX, 1))[g]
                            for m in range(2):
                                c = 2 * pair + m
                                ins = fn(dst[:, c * T:(c + 1) * T], B[bank][:, m * T:(m + 1) * T], ACT.Sigmoid,
                                         bias=VT[:, l, row + c:row + c + 1])
                            ins.then_inc(sem("rgate_done"), 1)
                        act.wait_ge(sem("rgate_done"), 4 * l + 4)
                        for c in range(4):
                            ins = fn(ra[:, c * T:(c + 1) * T], rr[:, c * T:(c + 1) * T], ACT.Exp,
                                     scale=small[:, 64 + 4 * l + c:65 + 4 * l + c])
                        for c in range(4):
                            ins = fn(rm[:, c * T:(c + 1) * T], rr[:, c * T:(c + 1) * T], ACT.Tanh,
                                     scale=small[:, 48 + 4 * l + c:49 + 4 * l + c])
                        ins.then_inc(sem("rtanh_ready"), 1)
                        act.wait_ge(sem("rm2_ready"), l + 1)
                        fn(rm, rm, ACT.Sqrt).then_inc(sem("rmult_ready"), 1)
                act.wait_ge(sem("kendn_ready"), l + 1)
                fn(kendn[:, :, :], B[4][:, :].rearrange("p (a f) -> p a f", a=2), ACT.Copy).then_inc(sem("kendn_done"), 1)
                for b in range(2):
                    act.wait_ge(sem("gla_o_ready"), 2 * l + b + 1)
                    fn(sqf[:, b * 512:(b + 1) * 512], B[2 + b][:, :], ACT.Square).then_inc(sem("gla_sq_ready"), 1)
                for b in range(2):
                    act.wait_ge(sem("gla_ss_ready"), 2 * l + b + 1)
                    fn(sc_sig[:, b * 512:(b + 1) * 512], B[b][:, :], ACT.Sqrt, bias=eps, scale=1.0 / P).then_inc(sem("gla_rms"), 1)

            def gla_exps(l):
                act.wait_ge(sem("bdiff_ready"), l + 1)
                fn(qloc, d1, ACT.Exp, scale=1.0 / 16)
                fn(kloc, d1, ACT.Exp, scale=-1.0 / 16)
                fn(kend, d2, ACT.Exp, scale=1.0 / 16)
                fn(qin, lfs, ACT.Exp, scale=1.0 / 16)
                fn(small[:, 128:128 + 8], blast, ACT.Exp, scale=1.0 / 16).then_inc(sem("gla_e_ready"), 1)

            def mixer2():
                W = plain_at["win2"]
                for j in range(12):
                    act.wait_ge(sem("plain_used"), W + j + 1)
                    b0, b1 = B[2 * (j % 2)], B[2 * (j % 2) + 1]
                    if j == 0:
                        ins = fn(rq[:, :, :], b0[:, :].rearrange("p (h t) -> p h t", h=2), ACT.Copy)
                    elif j == 1:
                        fn(rk[:, :, :], b0[:, :].rearrange("p (h t) -> p h t", h=2), ACT.Copy, scale=0.125)
                        ins = fn(rkn[:, :, :], b1[:, :].rearrange("p (h t) -> p h t", h=2), ACT.Copy, scale=0.125)
                    elif j in (2, 3, 6, 7):
                        dst, c = (rv, j - 2) if j < 4 else (v2, j - 6)
                        fn(dst[:, 0:2, c * CW:(c + 1) * CW], b0[:, :].rearrange("p (h t) -> p h t", h=2), ACT.Copy)
                        ins = fn(dst[:, 2:4, c * CW:(c + 1) * CW], b1[:, :].rearrange("p (h t) -> p h t", h=2), ACT.Copy)
                    elif j in (4, 5):
                        c = 2 * (j - 4)
                        for m, b in enumerate((b0, b1)):
                            fn(k2[:, c + m, 0:T], b[:, T:2 * T], ACT.Copy)
                            ins = fn(k2[:, c + m, T:2 * T], b[:, 0:T], ACT.Copy)
                    elif j in (8, 9):
                        c = 2 * (j - 8)
                        ins = fn(q2[:, c:c + 2, :], b0[:, :].rearrange("p (h t) -> p h t", h=2), ACT.Copy, scale=0.125)
                    else:
                        c = 2 * (j - 10)
                        ins = fn(rg[:, c:c + 2, :], b0[:, :].rearrange("p (h t) -> p h t", h=2), ACT.Silu)
                    ins.then_inc(sem("z2_in"), 1)
                for dr in range(2):
                    for pr in range(2):
                        ins = fn(qdec[:, dr, pr, :], C[:, (C_UP, C_DOWN)[dr]:(C_UP, C_DOWN)[dr] + T], ACT.Exp,
                                 scale=small[:, 80 + 2 * dr + pr:81 + 2 * dr + pr])
                ins.then_inc(sem("qdec_exp"), 1)
                for dr in range(2):
                    for a in range(2):
                        ins = fn(small[:, 96 + 8 * dr + 4 * a:100 + 8 * dr + 4 * a], small[:, 72 + 4 * dr:76 + 4 * dr], ACT.Exp,
                                 scale=C[:, C_TOK + 2 * dr + a:C_TOK + 2 * dr + a + 1])
                ins.then_inc(sem("kw_ready"), 1)
                act.wait_ge(sem("s2_psum"), 1)
                fn(S2[:, :, :, :], B[6][:, :].rearrange("p (h r v) -> p h r v", h=2, r=2), ACT.Copy).then_inc(sem("S2_ready"), 1)
                for b in range(2):
                    act.wait_ge(sem("ret_o"), 2 * b + 2)
                    if b == 0:
                        act.wait_ge(sem("ret_o"), 4)
                    fn(sqf[:, b * 512:(b + 1) * 512], B[2 + b][:, :], ACT.Square).then_inc(sem("ret_sq"), 1)
                for b in range(2):
                    act.wait_ge(sem("ret_ss"), b + 1)
                    fn(hflat[:, b * 512:(b + 1) * 512], B[b][:, :], ACT.Sqrt, bias=eps, scale=1.0 / P).then_inc(sem("ret_rms"), 1)
                act.wait_ge(sem("ret_done"), 4)
                for g in range(8):
                    for m in range(2):
                        act.wait_ge(sem("nmax_ready"), 2 * g + m + 1)
                        fn(pex[:, g % 2, m, :], B[2 * (g % 2) + m][:, :], ACT.Exp, bias=small[:, 144 + 2 * g + m:145 + 2 * g + m],
                           accum_out=small[:, 160 + 2 * g + m:161 + 2 * g + m]).then_inc(sem("p_ready"), 1)
                    if g >= 1:
                        att_copy(g - 1)
                    if g == 5:
                        att_norm(0)
                att_copy(7)
                att_norm(1)

            def att_copy(g):
                h, a = g // 2, g % 2
                act.wait_ge(sem("aT_psum"), g + 1)
                if h >= 2 and a == 0:
                    act.wait_ge(sem("att_o"), h - 1)
                fn(paT[:, h % 2, :, a * P:(a + 1) * P], B[4][:, :].rearrange("p (c t) -> p c t", c=4), ACT.Copy).then_inc(sem("aT_ready"), 1)

            def att_norm(b):
                act.wait_ge(sem("att_o"), 2 * b + 2)
                fn(sqf[:, b * 512:(b + 1) * 512], B[5 + b][:, :], ACT.Square).then_inc(sem("att_sq"), 1)
                act.wait_ge(sem("att_ss"), b + 1)
                fn(sqf[:, 1024 + b * 512:1024 + (b + 1) * 512], B[7][:, :], ACT.Sqrt, bias=eps, scale=1.0 / P).then_inc(sem("att_rms"), 1)

            act.dma_start(C[:], cst).then_inc(sem("const_in"), 16)
            act.dma_start(mixT[:, :, :].rearrange("p k t -> p (k t)"), rel).then_inc(sem("const_in"), 16)
            act.dma_start(XN.rearrange("p (a d) -> p a d", a=TT), A["x"].rearrange("b (a p) d -> p (b a) d", p=P)).then_inc(sem("x_in"), 16)
            act.wait_ge(sem("small_set"), 1)
            act.wait_ge(sem("vec_done"), 1)
            link(fn(small[:, 24:32], VT[:, 0, V_EXTRA:V_EXTRA + 8], ACT.Silu))
            sview = small[:, 32:48].rearrange("p (k v) -> p v k", v=2)
            link(fn(sview[:, 0, :], VT[:, 2, W_C:W_C + 8], ACT.Silu))
            fn(sview[:, 1, :], VT[:, 2, W_CC:W_CC + 8], ACT.Silu).then_inc(sem("c_act"), 1)
            for a in range(TT):
                act.wait_ge(sem("xin_ready"), a + 1)
                for half in range(2):
                    ins = fn(xT[:, 4 * half:4 * half + 4, a * P:(a + 1) * P],
                             B[2 * a + half][:, :].rearrange("p (k t) -> p k t", k=4), ACT.Copy)
                ins.then_inc(sem("x_copied"), 1)
            act.wait_ge(sem("x_copied"), 2)
            norm(0, xT[:, :, :])
            act.wait_ge(sem("scalars_in"), NSCALARS)
            act.wait_ge(sem("lam_dot"), 1)
            link(fn(small[:, 368:384], small[:, 0:16], ACT.Abs))
            fn(small[:, 384:400], small[:, 368:384], ACT.Exp, scale=-1.0).then_inc(sem("sp_exp"), 1)
            fn(small[:, 186:188], small[:, 184:186], ACT.Exp).then_inc(sem("lam_exp"), 1)
            act.wait_ge(sem("lg_ready"), 1)
            for h in range(HEADS):
                if h:
                    act.wait_ge(sem("D_ready"), h)
                for dr in range(2):
                    ins = fn(TMP[:, 4096 + dr * 512:4096 + (dr + 1) * 512], mixT[:, 2 * dr:2 * dr + 2, :].rearrange("p k t -> p (k t)"), ACT.Exp,
                             scale=small[:, 72 + 4 * dr + h:73 + 4 * dr + h])
                ins.then_inc(sem("Dexp_ready"), 1)
            for l in range(LAYERS):
                if l:
                    act.wait_ge(sem("x_ready"), 1)
                    norm(2, xT[:, :, :])
                mixer1(l)
                act.wait_ge(sem("x_part"), 4 * l + 4)
                norm(2 * l + 1, xT[:, :, :])
                if l == 0:
                    dense("f0")
                else:
                    act.wait_ge(sem("h_norm"), 4)
                    rows_of_h(0)
                    act.wait_ge(sem("top_diff"), 1)
                    fn(small[:, 400:402], small[:, 402:404], ACT.Exp).then_inc(sem("top_exp"), 1)
                    experts1()
                    combine_slots(0, A1 // P)
            act.wait_ge(sem("x_ready"), 2)
            norm(4, xT[:, :, :])
            act.wait_ge(sem("x_ready"), 3)
            act.dma_start(CN.rearrange("p (a d) -> p a d", a=TT), A["ctx_2"].rearrange("b (a p) d -> p (b a) d", p=P)).then_inc(sem("ctx_in"), 16)
            norm(5, xT[:, :, :])
            ctxT = mixT
            for a in range(TT):
                act.wait_ge(sem("xin_ready"), 2 + a + 1)
                for half in range(2):
                    ins = fn(ctxT[:, 4 * half:4 * half + 4, a * P:(a + 1) * P],
                             B[2 * a + half][:, :].rearrange("p (k t) -> p k t", k=4), ACT.Copy)
                ins.then_inc(sem("x_copied"), 1)
            act.wait_ge(sem("x_copied"), 4)
            norm(6, ctxT[:, :, :])
            act.wait_ge(sem("h_norm"), 7)
            mixer2()
            act.wait_ge(sem("x_part"), 12)
            norm(7, xT[:, :, :])
            act.wait_ge(sem("logits_ready"), 2)
            fn(RT[:, 0:128], B[7][:, 0:128], ACT.Sigmoid).then_inc(sem("top_exp"), 1)
            rows_of_h(1)
            dense("sh")
            experts2()
            act.wait_ge(sem("x_ready"), 4)
            norm(8, xT[:, :, :])
            act.wait_ge(sem("stored"), 16)

        @block.vector
        def _(dve):
            V = nc.vector
            count = [0]

            def link(ins):
                count[0] += 1
                ins.then_inc(sem("dve_chain"), 1)
                dve.wait_ge(sem("dve_chain"), count[0])

            def done(ins, name, n):
                ins.then_inc(sem(name), 1)
                dve.wait_ge(sem(name), n)

            def recip(v):
                link(V.reciprocal(v, v))

            def scale_cols(row, l, v, sc_at, dst):
                link(V.tensor_scalar(dst, modc[:, v, sc_at:sc_at + 8], 1.0, None, ALU.add))
                link(V.tensor_tensor(dst, dst, VT[:, l, row:row + 8], ALU.mult))

            def norm(n, src, dst, gain, shift=None):
                dve.wait_ge(sem("rms_ready"), n + 1)
                recip(rstd[:])
                link(V.tensor_tensor(sq[:, :, :], src, rstd[:].unsqueeze(1).to_broadcast([P, KD, T]), ALU.mult))
                for k in range(KD):
                    if shift is None:
                        ins = V.tensor_scalar(dst(k), sq[:, k, :], gain[:, k:k + 1], None, ALU.mult)
                    else:
                        ins = V.tensor_scalar(dst(k), sq[:, k, :], gain[:, k:k + 1], shift[:, k:k + 1], ALU.mult, ALU.add)
                done(ins, "h_norm", n + 1)

            def ada_unit(n):
                name, _ = units[n]
                pieces = unit_pieces[n]
                written = [0, 0]
                for p in pieces:
                    arrived(dve, p)
                if n >= 2:
                    dve.wait_ge(sem("ada_psum"), n - 1)
                for k in range(KD):
                    for i in range(2):
                        acc = ffn_g[:, 2 * (n % 2) + i, :]
                        w = piece(pieces[i % len(pieces)])[:, k, :]
                        c = small[:, 32 + 2 * k + i:33 + 2 * k + i] if name == "ada2" else small[:, 24 + k:25 + k]
                        if k == 0:
                            ins = V.tensor_scalar(acc, w, c, None, ALU.mult)
                        else:
                            dve.wait_ge(sem("dve_chain"), written[i])
                            ins = V.scalar_tensor_tensor(out=acc, in0=w, scalar=c, in1=acc, op0=ALU.mult, op1=ALU.add)
                        if k == KD - 1 and (len(pieces) == 2 or i == 1):
                            ins.then_inc(sem("ada_used"), 1)
                        else:
                            ins.then_inc(sem("dve_chain"), 1)
                            count[0] += 1
                            written[i] = count[0]

            def modulation(v, nv, col, units_done):
                dve.wait_ge(sem("ada_psum"), units_done)
                for i in range(nv):
                    link(V.tensor_tensor(modc[:, v + i, :], B[7][:, col + 48 * i:col + 48 * (i + 1)],
                                         VT[:, v if v < 2 else 2, V_ADAB:V_ADAB + 48], ALU.add))

            gcol = small[:, 376:384]
            gcol_f = small[:, 384:392]

            def product(m, value, width):
                dve.wait_ge(sem("s_ready"), value)
                V.tensor_tensor(ffn_a[:, m, 0:width], ffn_s[:, m, 0:width], B[4 + m][:, T:T + width],
                                ALU.mult).then_inc(sem("a_ready"), 1)

            def dense(ph):
                for f in range(2 * len(step_at[ph])):
                    product(f % 2, base[ph] + f + 1, T)
                    if ph == "f0":
                        for n in units_after(f):
                            ada_unit(n)

            def matrices(g0, e, ws, start):
                if isinstance(e, int):
                    if e > 0 or g0 > 0:
                        dve.wait_ge(sem("he_psum"), 2 * (e + g0))
                else:
                    dve.wait_ge(sem("he_psum"), e * 2 + 2 * g0)
                iota = C[:, C_IOTA:C_IOTA + T]
                for a in range(TT):
                    ins = V.tensor_scalar(Pe[:, a, :], iota, rank[:, a, bass.ds(e, 1)], None, ALU.is_equal)
                ins.then_inc(sem("Pe_ready"), 1)
                if not isinstance(e, int):
                    dve.wait_ge(sem("w_kept"), e + g0)
                for a in range(TT):
                    ins = V.tensor_scalar(ws[:, a, bass.ds(start, T)], iota, rank[:, a, bass.ds(e, 1)],
                                          gts[:, a, bass.ds(e, 1)], ALU.is_equal, ALU.mult)
                ins.then_inc(sem("w_kept"), 1)

            def experts1():
                t0 = base["f1"]

                def narrow_expert(e):
                    turn0 = load_meta(dve, 2, e, E1 * STEPS1, 1)

                    def step(s, i=0):
                        o = P * (s % 3)
                        dve.wait_ge(sem("s_ready"), e * (2 * STEPS1) + i * 6 + (t0 + 2 * s + 2))
                        for half in range(2):
                            h = HALF * half
                            V.tensor_tensor(na[:, o + h:o + h + HALF], ns[:, o + h:o + h + HALF],
                                            B[4 + s % 3][:, T + h:T + h + HALF], ALU.mult).then_inc(sem("a_ready"), 1)
                        dve.wait_ge(sem("narrow_turned"), turn0 + i * 3 + s)
                        V.tensor_copy(naT[:, o:o + P], B[7][:, 0:P]).then_inc(sem("narrow_aT"), 1)

                    with dve.Fori(0, 3) as i:
                        for s in range(3):
                            step(s, i)
                    for s in range(9, STEPS1):
                        step(s)

                def tiles(e):
                    c = load_meta(dve, 0, e, 2)

                    def body(width):
                        if width == HALF:
                            return narrow_expert(e)
                        with dve.Fori(0, STEPS1) as s:
                            for m in range(2):
                                product(m, e * (2 * STEPS1) + s * 2 + (t0 + m + 1), width)

                    by_class(dve, c, body)

                matrices(0, 0, w1s, load_meta(dve, 1, 0, A1))
                with dve.Fori(0, E1 - 1) as e:
                    start = load_meta(dve, 1, e + 1, A1)
                    matrices(0, e + 1, w1s, start)
                    tiles(e)
                tiles(E1 - 1)

            def pair_places(b, e, r):
                iota = C[:, C_IOTA + HALF * r:C_IOTA + HALF * (r + 1)]
                for a in range(TT):
                    for x in range(2):
                        o = a * P + HALF * x
                        ins = V.tensor_scalar(b["P"][:, o:o + HALF], iota, rank[:, a, bass.ds(e + x, 1)], None, ALU.is_equal)
                ins.then_inc(sem(b["name"] + "_P"), 1)

            def pair_gates(b, e, r):
                iota = C[:, C_IOTA + HALF * r:C_IOTA + HALF * (r + 1)]
                for a in range(TT):
                    for x in range(2):
                        o = a * P + HALF * x
                        ins = V.tensor_scalar(b["W"][:, o:o + HALF], iota, rank[:, a, bass.ds(e + x, 1)],
                                              gts[:, a, bass.ds(e + x, 1)], ALU.is_equal, ALU.mult)
                ins.then_inc(sem(b["name"] + "_W"), 1)

            def pair_product(b, v):
                dve.wait_ge(sem(b["name"] + "_s"), v)
                V.tensor_tensor(b["a"], b["s"], B[4][:, CW:2 * CW], ALU.mult).then_inc(sem(b["name"] + "_a"), 1)

            def pair_keep_turned(b, v):
                dve.wait_ge(sem(b["name"] + "_turned"), v)
                V.tensor_copy(b["aw"], B[7][:, :]).then_inc(sem(b["name"] + "_aw"), 1)

            def pair_keep_outputs(b, v):
                dve.wait_ge(sem(b["name"] + "_y1"), v)
                V.tensor_copy(b["Y"][:, 512:1024], B[7][:, :]).then_inc(sem(b["name"] + "_Y1"), 1)

            def experts2():
                f = first_round

                def pair(p, parity, later, first=False, last_one=False):
                    def more(v, r):
                        pair_places(more_round, p * 2, r)
                        pair_gates(more_round, p * 2, r)
                        pair_product(more_round, v)
                        pair_keep_turned(more_round, v)
                        pair_keep_outputs(more_round, v)

                    further_rounds(dve, p, more)
                    if not last_one:
                        dve.wait_ge(sem("pair_he1"), p + 1)
                        pair_places(f, p * 2 + 2, 0)
                    pair_product(f, p + 1)
                    pair_keep_turned(f, p + 1)
                    if not last_one:
                        pair_gates(f, p * 2 + 2, 0)
                    pair_keep_outputs(f, p + 1)

                pair_places(f, 0, 0)
                pair_gates(f, 0, 0)
                each_pair(dve, pair)

            def combine_slots(b0, blocks):
                for b in range(blocks):
                    dve.wait_ge(sem("block_psum"), b0 + b + 1)
                    if b >= 2:
                        dve.wait_ge(sem("block_done"), b0 + b - 1)
                    V.tensor_copy(Yn[:, b % 2, 512:1024], B[5][:, :])
                    V.tensor_copy(PTs[:, b % 2, :], B[6][:, 0:T]).then_inc(sem("block_in"), 1)

            def places(l, E):
                for a in range(TT):
                    link(V.tensor_tensor_scan(mskx[:, a, 0:E], C[:, C_UP:C_UP + 1].to_broadcast([P, E]), msk[:, a, 0:E], 0.0,
                                              ALU.mult, ALU.add))
                    ins = V.tensor_tensor(mskx[:, a, 0:E], mskx[:, a, 0:E], msk[:, a, 0:E], ALU.subtract)
                    link(ins) if a == 0 else done(ins, "mask_ready", l + 1)
                dve.wait_ge(sem("places_psum"), l + 1)
                cnt, first = B[7][:, 0:E], B[7][:, E:2 * E]
                if l == 0:
                    big, narrow, nth = RT[:, 0:E], RT[:, 64:64 + E], RT[:, 72:72 + E]
                    link(V.tensor_scalar(big, cnt, float(CLASSES[0]), None, ALU.is_gt))
                    link(V.tensor_scalar(narrow, big, -1.0, 1.0, ALU.mult, ALU.add))
                    link(V.scalar_tensor_tensor(out=meta[:, 0, 0:E], in0=cnt, scalar=float(CLASSES[1]), in1=big,
                                                op0=ALU.is_gt, op1=ALU.add))
                    link(V.tensor_copy(meta[:, 1, 0:E], first))
                    link(V.tensor_tensor_scan(nth, C[:, C_UP:C_UP + 1].to_broadcast([P, E]), narrow, 0.0,
                                              ALU.mult, ALU.add))
                    link(V.tensor_scalar(meta[:, 2, 0:E], nth, float(STEPS1), 1.0 - STEPS1, ALU.mult, ALU.add))
                    link(V.tensor_copy(meta[:, 3, 0:E], nth))
                else:
                    most, flag, more = RT[:, 64:96], RT[:, 96:128], RT[:, 128:160]
                    link(V.tensor_copy(RT[:, 0:E], cnt))
                    c2 = RT[:, 0:E].rearrange("p (n x) -> p n x", x=2)
                    link(V.tensor_tensor(most.unsqueeze(2), c2[:, :, 0:1], c2[:, :, 1:2], ALU.max))
                    for r in (1, 2, 3):
                        link(V.tensor_scalar(more if r == 1 else flag, most, float(HALF * r), None, ALU.is_gt))
                        link(V.tensor_copy(meta[:, 0 if r == 1 else r, 0:PAIRS], more if r == 1 else flag))
                        if r > 1:
                            link(V.tensor_tensor(more, more, flag, ALU.add))
                    link(V.tensor_tensor_scan(flag, C[:, C_UP:C_UP + 1].to_broadcast([P, PAIRS]), more, 0.0,
                                              ALU.mult, ALU.add))
                    link(V.tensor_copy(meta[:, 1, 0:PAIRS], flag))
                    for r in (2, 3):
                        link(V.tensor_scalar(meta[:, 2 + r, 0:PAIRS], flag, 1.0 - r, None, ALU.add))
                for a in range(TT):
                    link(V.scalar_tensor_tensor(out=rank[:, a, 0:E], in0=B[7][:, (2 + a) * E:(3 + a) * E], scalar=1.0,
                                                in1=msk[:, a, 0:E], op0=ALU.add, op1=ALU.mult))
                    ins = V.tensor_scalar(rank[:, a, 0:E], rank[:, a, 0:E], -1.0, None, ALU.add)
                    link(ins) if a == 0 else done(ins, "meta_ready", l + 1)

            def add_ffn(name, value, nth, v):
                dve.wait_ge(sem(name), value)
                for d in range(KD):
                    ins = V.scalar_tensor_tensor(out=xT[:, d, :], in0=B[d // 2][:, (d % 2) * T:(d % 2 + 1) * T],
                                                 scalar=modc[:, v, 40 + d:41 + d], in1=xT[:, d, :], op0=ALU.mult, op1=ALU.add)
                done(ins, "x_ready", nth)

            def add_mix(name, nth, banks, v):
                for j in range(4):
                    dve.wait_ge(sem("plain_used"), plain_at[name] + j + 1)
                    for m in range(2):
                        d = 2 * j + m
                        ins = V.scalar_tensor_tensor(out=xT[:, d, :], in0=B[banks[j % len(banks)]][:, m * T:(m + 1) * T],
                                                     scalar=modc[:, v, 16 + d:17 + d], in1=xT[:, d, :], op0=ALU.mult, op1=ALU.add)
                    ins.then_inc(sem("x_part"), 1)
                dve.wait_ge(sem("x_part"), 4 * nth + 4)

            def mixer1(l):
                link(V.memset(upad[:, :, 0:3], 0.0))
                link(V.memset(sT[:, :, :], 0.0))
                dve.wait_ge(sem("lsig_ready"), l + 1)
                for m in range(2):
                    link(V.tensor_scalar(d1[:, m * T:(m + 1) * T], B[5][:, m * T:(m + 1) * T],
                                         VT[:, l, V_BG + m:V_BG + m + 1], 0.0, ALU.add, ALU.min))
                done(V.tensor_tensor(d1, d1, tmp1, ALU.subtract), "lf_done", l + 1)
                for m in range(2):
                    link(V.tensor_tensor_scan(lfs[:, m * T:(m + 1) * T], C[:, C_SCAN:C_SCAN + T], d1[:, m * T:(m + 1) * T],
                                              0.0, ALU.mult, ALU.add))
                b3 = lfs.rearrange("p (n t) -> p n t", t=CH)
                link(V.tensor_tensor(d1.rearrange("p (n t) -> p n t", t=CH), b3, b3[:, :, CH // 2 - 1:CH // 2].to_broadcast([P, 8, CH]), ALU.subtract))
                link(V.tensor_copy(blast.unsqueeze(2), b3[:, :, CH - 1:CH]))
                link(V.tensor_tensor(d2.rearrange("p (n t) -> p n t", t=CH), b3[:, :, CH - 1:CH].to_broadcast([P, 8, CH]), b3, ALU.subtract))
                V.tensor_copy(small[:, 22:23], small[:, 20:21]).then_inc(sem("bdiff_ready"), 1)
                dve.wait_ge(sem("z_in"), 10 * l + 4)
                for c in range(4):
                    o = uc[:, c * T:(c + 1) * T]
                    link(V.tensor_scalar(o, upad[:, c, 0:T], VT[:, l, V_CONVW + c:V_CONVW + c + 1],
                                         VT[:, l, V_CONVB + c:V_CONVB + c + 1], ALU.mult, ALU.add))
                    for tap in range(1, 4):
                        w = V_CONVW + 4 * tap + c
                        ins = V.scalar_tensor_tensor(out=o, in0=upad[:, c, tap:tap + T], scalar=VT[:, l, w:w + 1], in1=o,
                                                     op0=ALU.mult, op1=ALU.add)
                        link(ins) if (c, tap) != (3, 3) else done(ins, "conv_ready", l + 1)
                dve.wait_ge(sem("gla_e_ready"), l + 1)
                for o, z in ((qloc, qT), (kloc, kT), (kend, kT), (qin, qT)):
                    ins = V.tensor_tensor(o, o, z, ALU.mult)
                ins.then_inc(sem("gla_in"), 1)
                dve.wait_ge(sem("rtanh_ready"), l + 1)
                link(V.tensor_scalar(rr, rm, 1.0, None, ALU.add))
                recip(rr)
                V.scalar_tensor_tensor(out=rm, in0=rm, scalar=2.0, in1=rr, op0=ALU.mult, op1=ALU.mult).then_inc(sem("rm2_ready"), 1)
                dve.wait_ge(sem("rmult_ready"), l + 1)
                link(V.memset(rm.rearrange("p (c t) -> p c t", c=4)[:, :, 0:1], 1.0))
                link(V.tensor_tensor(rm, rm, ri, ALU.mult))
                link(V.tensor_tensor(rm, rm, uc, ALU.mult))
                for c in range(4):
                    s = slice(c * T, (c + 1) * T)
                    link(V.tensor_tensor_scan(rr[:, s], ra[:, s], rm[:, s], 0.0, ALU.mult, ALU.add))
                dve.wait_ge(sem("z_in"), 10 * l + 10)
                link(V.tensor_tensor(mixT[:, 0:4, :].rearrange("p k t -> p (k t)"), rr, gate, ALU.mult))
                mask = C[:, C_CAUS:C_CAUS + P].bitcast(U32).unsqueeze(1).to_broadcast([P, 2, P])
                s5 = sT[:, :, :].rearrange("p a (h r t) -> p r h a t", h=2, r=2)
                for par in range(2):
                    dve.wait_ge(sem("gla_s_ready"), 2 * l + par + 1)
                    for h2 in range(2):
                        ins = V.copy_predicated(s5[:, par, h2], mask,
                                                B[par][:, h2 * T:(h2 + 1) * T].rearrange("p (a t) -> p a t", a=TT))
                    ins.then_inc(sem("gla_sT_done"), 1)
                dve.wait_ge(sem("gla_u_ready"), l + 1)
                for n in range(NCH - 1):
                    src = B[5 + n % 2][:, (n // 2) * T:(n // 2 + 1) * T].rearrange("p (a v) -> p a v", a=2)
                    if n == 0:
                        ins = V.tensor_copy(St[:, 0, :, :], src)
                    else:
                        for pr in range(2):
                            ins = V.scalar_tensor_tensor(out=St[:, n, pr, :], in0=St[:, n - 1, pr, :],
                                                         scalar=small[:, 128 + pr * 4 + n:129 + pr * 4 + n],
                                                         in1=src[:, pr, :], op0=ALU.mult, op1=ALU.add)
                    done(ins, "state_ready", 3 * l + n + 1)
                for b in range(2):
                    dve.wait_ge(sem("gla_rms"), 2 * l + b + 1)
                    s = slice(b * 512, (b + 1) * 512)
                    recip(sc_sig[:, s])
                    g2 = gT.rearrange("p (h r t) -> p r h t", h=2, r=2)[:, b]
                    link(V.scalar_tensor_tensor(out=g2, in0=g2, scalar=VT[:, l, V_GLAG:V_GLAG + 1],
                                                in1=sc_sig[:, s].rearrange("p (h t) -> p h t", h=2), op0=ALU.mult, op1=ALU.mult))
                    ins = V.tensor_tensor(mixT[:, 4:8, :].rearrange("p (h r) t -> p r h t", r=2)[:, b],
                                          B[2 + b][:, :].rearrange("p (h t) -> p h t", h=2), g2, ALU.mult)
                done(ins, "mix_ready", l + 1)
                add_mix(f"wout{l}", l, [4, 5, 6], l)

            def softplus():
                x, y, s, s2, p = (small[:, 0:16], small[:, 384:400], small[:, 400:416], small[:, 416:432],
                                  small[:, 432:448])
                dve.wait_ge(sem("sp_exp"), 1)
                link(V.tensor_scalar(s2, y, 2.0, None, ALU.add))
                recip(s2)
                link(V.tensor_tensor(s, y, s2, ALU.mult))
                link(V.tensor_tensor(s2, s, s, ALU.mult))
                link(V.tensor_scalar(p, s2, 1.0 / 17, None, ALU.mult))
                for n in (15, 13, 11, 9, 7, 5, 3):
                    link(V.scalar_tensor_tensor(out=p, in0=p, scalar=1.0 / n, in1=s2, op0=ALU.add, op1=ALU.mult))
                link(V.scalar_tensor_tensor(out=p, in0=p, scalar=1.0, in1=s, op0=ALU.add, op1=ALU.mult))
                link(V.tensor_scalar(y, x, -1.0, 0.0, ALU.mult, ALU.max))
                link(V.scalar_tensor_tensor(out=p, in0=p, scalar=2.0, in1=y, op0=ALU.mult, op1=ALU.add))
                link(V.tensor_scalar(small[:, 48:56], p[:, 0:8], 8.0, None, ALU.mult))
                link(V.tensor_scalar(small[:, 64:72], p[:, 0:8], -8.0, None, ALU.mult))
                link(V.tensor_scalar(small[:, 72:80], p[:, 8:16], -1.0, None, ALU.mult))
                for dr in range(2):
                    for pr in range(2):
                        for hh in range(2):
                            r = slice(64 * hh, 64 * hh + 64)
                            h = 2 * pr + hh
                            link(V.tensor_copy(small[r, 80 + 2 * dr + pr:81 + 2 * dr + pr], small[r, 72 + 4 * dr + h:73 + 4 * dr + h]))
                V.tensor_copy(small[:, 22:23], small[:, 20:21]).then_inc(sem("lg_ready"), 1)

            def scalars():
                dve.wait_ge(sem("scalars_in"), NSCALARS)
                for k in range(2):
                    v = small[:, 256 + 128 * k:256 + 128 * k + 64]
                    w = small[:, 320 + 128 * k:320 + 128 * k + 64]
                    link(V.tensor_tensor(v, v, w, ALU.mult))
                    link(V.tensor_reduce(small[:, 184 + k:185 + k], v, AX, ALU.add))
                V.tensor_copy(small[:, 22:23], small[:, 20:21]).then_inc(sem("lam_dot"), 1)
                softplus()
                dve.wait_ge(sem("lam_exp"), 1)
                link(V.tensor_tensor(small[:, 188:189], small[:, 186:187], small[:, 187:188], ALU.subtract))
                link(V.tensor_scalar(small[:, 188:189], small[:, 188:189], LAM_INIT, None, ALU.add))
                link(V.tensor_scalar(small[:, 189:190], VT[:, 2, W_DG:W_DG + 1], 1.0 - LAM_INIT, None, ALU.mult))

            def decays(h):
                dve.wait_ge(sem("Dexp_ready"), h + 1)
                ef, eb = TMP[:, 4096:4608], TMP[:, 4608:5120]
                link(V.tensor_tensor(ef, ef, mixT[:, 4:6, :].rearrange("p k t -> p (k t)"), ALU.mult))
                link(V.tensor_tensor(eb, eb, mixT[:, 6:8, :].rearrange("p k t -> p (k t)"), ALU.mult))
                done(V.tensor_tensor(Dret[:, h, :], ef, eb, ALU.add), "D_ready", h + 1)

            def top2_gates():
                dve.wait_ge(sem("logits_ready"), 1)
                lg, top, idx, idf = (RT[:, 16 * n:16 * n + 16].rearrange("p (a e) -> p a e", a=2) for n in range(4))
                idx = RT[:, 32:48].bitcast(U32).rearrange("p (a e) -> p a e", a=2)
                link(V.tensor_copy(lg, B[7][:, 0:16].rearrange("p (a e) -> p a e", a=2)))
                for a in range(TT):
                    link(V.max(top[:, a, :], lg[:, a, :]))
                    link(V.max_index(idx[:, a, :], top[:, a, :], lg[:, a, :]))
                    link(V.tensor_copy(idf[:, a, :], idx[:, a, :]))
                    link(V.tensor_tensor(small[:, 402 + a:403 + a], top[:, a, 1:2], top[:, a, 0:1], ALU.subtract))
                V.tensor_copy(small[:, 22:23], small[:, 20:21]).then_inc(sem("top_diff"), 1)
                dve.wait_ge(sem("top_exp"), 1)
                link(V.tensor_scalar(small[:, 404:406], small[:, 400:402], 1.0, None, ALU.add))
                recip(small[:, 404:406])
                link(V.tensor_tensor(small[:, 406:408], small[:, 404:406], small[:, 400:402], ALU.mult))
                for a in range(TT):
                    g = gts[:, a, 0:8]
                    t8, u8 = RT[:, 64:72], RT[:, 72:80]
                    io = C[:, C_IOTA:C_IOTA + 8]
                    link(V.tensor_scalar(t8, io, idf[:, a, 0:1], None, ALU.is_equal))
                    link(V.tensor_scalar(u8, io, idf[:, a, 1:2], None, ALU.is_equal))
                    link(V.tensor_tensor(msk[:, a, 0:8], t8, u8, ALU.add))
                    link(V.tensor_scalar(t8, t8, small[:, 404 + a:405 + a], None, ALU.mult))
                    link(V.scalar_tensor_tensor(out=g, in0=u8, scalar=small[:, 406 + a:407 + a], in1=t8,
                                                op0=ALU.mult, op1=ALU.add))

            def one_hot_sum(dst, idf, n, width):
                io = C[:, C_IOTA:C_IOTA + width]
                link(V.tensor_scalar(dst, io, idf[:, 0:1], None, ALU.is_equal))
                for j in range(1, n):
                    link(V.scalar_tensor_tensor(out=dst, in0=io, scalar=idf[:, j:j + 1], in1=dst, op0=ALU.is_equal, op1=ALU.add))

            def group_gates():
                dve.wait_ge(sem("top_exp"), 2)
                for a in range(TT):
                    sc = RT[:, 64 * a:64 * a + 64]
                    sel = RT[:, 128:192]
                    t8 = RT[:, 192:256].rearrange("p (g e) -> p g e", g=8)
                    gs, tg, gm = RT[:, 256:264], RT[:, 264:272], RT[:, 272:280]
                    ix = RT[:, 280:288].bitcast(U32)
                    idf = RT[:, 288:296]
                    link(V.tensor_tensor(sel, sc, small[:, 192:256], ALU.add))
                    for g in range(8):
                        link(V.max(t8[:, g, :], sel[:, 8 * g:8 * g + 8]))
                    link(V.tensor_tensor(gs.unsqueeze(2), t8[:, :, 0:1], t8[:, :, 1:2], ALU.add))
                    link(V.max(tg, gs))
                    link(V.max_index(ix, tg, gs))
                    link(V.tensor_copy(idf, ix))
                    one_hot_sum(gm, idf, 4, 8)
                    s3 = sel.rearrange("p (g e) -> p g e", g=8)
                    link(V.tensor_tensor(s3, s3, gm.unsqueeze(2).to_broadcast([P, 8, 8]), ALU.mult))
                    link(V.tensor_scalar(gm, gm, -1.0, 3e38, ALU.add, ALU.mult))
                    link(V.tensor_tensor(s3, s3, gm.unsqueeze(2).to_broadcast([P, 8, 8]), ALU.add))
                    link(V.max(tg, sel))
                    link(V.max_index(ix, tg, sel))
                    link(V.tensor_copy(idf, ix))
                    one_hot_sum(msk[:, a, :], idf, 8, 64)
                    g = small[:, 512 + 64 * a:576 + 64 * a]
                    link(V.tensor_tensor(g, sc, msk[:, a, :], ALU.mult))
                    link(V.tensor_reduce(gs[:, 0:1], g, AX, ALU.add))
                    recip(gs[:, 0:1])
                    link(V.tensor_scalar(g, g, gs[:, 0:1], 2.5, ALU.mult, ALU.mult))

            def mixer2():
                dve.wait_ge(sem("z2_in"), 12)
                cos = C[:, C_COS:C_COS + T].unsqueeze(1).to_broadcast([P, 2, T])
                sin = C[:, C_SIN:C_SIN + T].unsqueeze(1).to_broadcast([P, 2, T])
                rt = rope_t.rearrange("p (h t) -> p h t", h=2)
                for g in range(6):
                    z = [rq[:, :, :], rk[:, :, :], k2[:, 0:2, T:], k2[:, 2:4, T:], q2[:, 0:2, :], q2[:, 2:4, :]][g]
                    dve.wait_ge(sem("rot_ready"), g + 1)
                    link(V.tensor_tensor(rt, B[4 + g % 2][:, :].rearrange("p (h t) -> p h t", h=2), sin, ALU.mult))
                    link(V.tensor_tensor(z, z, cos, ALU.mult))
                    done(V.tensor_tensor(z, z, rt, ALU.add), "rope_done", g + 1)
                    if g == 0:
                        dve.wait_ge(sem("qdec_exp"), 1)
                        for dr in range(2):
                            link(V.tensor_tensor(qdec[:, dr, :, :], qdec[:, dr, :, :], rq[:, :, :], ALU.mult))
                        V.tensor_copy(small[:, 22:23], small[:, 20:21]).then_inc(sem("qdec_ready"), 1)
                        dve.wait_ge(sem("kw_ready"), 1)
                        for dr in range(2):
                            w = small[:, 96 + 8 * dr:104 + 8 * dr].rearrange("p (a h) -> p a h", a=2)
                            for a in range(2):
                                ins = V.tensor_tensor(kdec[:, dr, a, :].rearrange("p (h d) -> p h d", h=HEADS),
                                                      rkn[:, a, :].rearrange("p (h d) -> p h d", h=HEADS),
                                                      w[:, a, :].unsqueeze(2).to_broadcast([P, HEADS, 64]), ALU.mult)
                        ins.then_inc(sem("kdec_ready"), 1)
                for h in range(HEADS):
                    dve.wait_ge(sem("ret_s"), h + 1)
                    if h >= 2:
                        dve.wait_ge(sem("ret_o"), h - 1)
                    V.tensor_tensor(sD[:, h % 2, :], B[h % 2][:, :], Dret[:, h, :], ALU.mult).then_inc(sem("sD_ready"), 1)
                for b in range(2):
                    dve.wait_ge(sem("ret_rms"), b + 1)
                    s = slice(b * 512, (b + 1) * 512)
                    recip(hflat[:, s])
                    r2 = rg[:, :, :].rearrange("p (h r) t -> p r h t", r=2)[:, b]
                    link(V.scalar_tensor_tensor(out=r2, in0=r2, scalar=VT[:, 2, W_RG:W_RG + 1],
                                                in1=hflat[:, s].rearrange("p (h t) -> p h t", h=2), op0=ALU.mult, op1=ALU.mult))
                    done(V.tensor_tensor(mixT[:, 4:8, :].rearrange("p (h r) t -> p r h t", r=2)[:, b],
                                         B[2 + b][:, :].rearrange("p (h t) -> p h t", h=2), r2, ALU.mult),
                         "ret_done", 2 * b + 1)
                    done(V.tensor_copy(small[:, 23:24], small[:, 20:21]), "ret_done", 2 * b + 2)
                for g in range(8):
                    for m in range(2):
                        dve.wait_ge(sem("att_s"), 2 * g + m + 1)
                        V.tensor_reduce(small[:, 144 + 2 * g + m:145 + 2 * g + m], B[2 * (g % 2) + m][:, :], AX, ALU.max,
                                        negate=True).then_inc(sem("nmax_ready"), 1)
                    if g >= 1:
                        combine(g - 1)
                    if g == 6:
                        att_norm(0)
                combine(7)
                att_norm(1)
                add_mix("wout2", 2, [0, 1, 2, 3], 2)

            def combine(g):
                dve.wait_ge(sem("p_ready"), 2 * g + 2)
                rs = small[:, 176:178]
                link(V.reciprocal(rs, small[:, 160 + 2 * g:162 + 2 * g]))
                link(V.tensor_tensor(rs[:, 1:2], rs[:, 1:2], small[:, 188:189], ALU.mult))
                link(V.tensor_scalar(pex[:, g % 2, 1, :], pex[:, g % 2, 1, :], rs[:, 1:2], None, ALU.mult))
                done(V.scalar_tensor_tensor(out=pex[:, g % 2, 0, :], in0=pex[:, g % 2, 0, :], scalar=rs[:, 0:1],
                                            in1=pex[:, g % 2, 1, :], op0=ALU.mult, op1=ALU.subtract), "a2_ready", g + 1)

            def att_norm(b):
                dve.wait_ge(sem("att_rms"), b + 1)
                s = sqf[:, 1024 + b * 512:1024 + (b + 1) * 512]
                recip(s)
                ins = V.scalar_tensor_tensor(out=mixT[:, 2 * b:2 * b + 2, :].rearrange("p k t -> p (k t)"), in0=B[5 + b][:, :],
                                             scalar=small[:, 189:190], in1=s, op0=ALU.mult, op1=ALU.mult)
                if b:
                    done(ins, "mix_ready", 3)
                else:
                    link(ins)

            link(V.memset(small[:, 16:24], EPS))
            link(V.memset(small[:, 21:22], 1.0))
            dve.wait_ge(sem("vec_ready"), 1)
            link(V.tensor_copy(VT[:, 0:2, 0:V_ROWS], B[6][:, 0:2 * P].rearrange("p (l r) -> p l r", l=2)[:, :, 0:V_ROWS]))
            done(V.tensor_copy(VT[:, 2, 0:W_ROWS], B[6][:, 2 * P:2 * P + W_ROWS]), "vec_done", 1)
            link(V.tensor_copy(small[:, 0:4], VT[:, 0, V_LAM:V_LAM + 4]))
            link(V.tensor_copy(small[:, 4:8], VT[:, 1, V_LAM:V_LAM + 4]))
            V.tensor_copy(small[:, 22:23], small[:, 20:21]).then_inc(sem("small_set"), 1)
            dve.wait_ge(sem("c_act"), 1)
            for n in range(ADA_UNITS):
                ada_unit(n)
                if n == 3:
                    scalars()
                elif 4 <= n < 4 + HEADS:
                    decays(n - 4)
            modulation(0, 1, 0, ADA_UNITS)
            for l in range(LAYERS):
                scale_cols(V_G1, l, l, 8, gcol)
                scale_cols(V_G2, l, l, 32, gcol_f)
                norm(2 * l, xT[:, :, :], lambda k: hT1[:, k, :], gcol, modc[:, l, 0:8])
                mixer1(l)
                norm(2 * l + 1, xT[:, :, :], lambda k: hT1[:, k, :], gcol_f, modc[:, l, 24:32])
                if l == 0:
                    dense("f0")
                    add_ffn("down_done", base["f0"] + 22, 1, 0)
                    modulation(1, 1, 0, ADA_UNITS + F0_UNITS)
                    modulation(2, 2, 64, ADA_UNITS + F0_UNITS)
                else:
                    top2_gates()
                    places(0, E1)
                    experts1()
                    combine_slots(0, A1 // P)
                    add_ffn("block_done", A1 // P, 2, 1)
            norm(4, xT[:, :, :], lambda k: xT[:, k, :], VT[:, 1, V_EXTRA:V_EXTRA + 8])
            V.tensor_copy(small[:, 22:23], small[:, 20:21]).then_inc(sem("x_ready"), 1)
            scale_cols(V_G1, 2, 2, 8, gcol)
            norm(5, xT[:, :, :], lambda k: hcat[:, k, 0:T], gcol, modc[:, 2, 0:8])
            V.tensor_copy(small[:, 22:23], small[:, 20:21]).then_inc(sem("ctx_go"), 1)
            scale_cols(V_G1, 2, 3, 8, gcol)
            norm(6, mixT[:, :, :], lambda k: hcat[:, k, T:2 * T], gcol, modc[:, 3, 0:8])
            scale_cols(V_G2, 2, 2, 32, gcol_f)
            mixer2()
            norm(7, xT[:, :, :], lambda k: hT1[:, k, :], gcol_f, modc[:, 2, 24:32])
            group_gates()
            dense("sh")
            places(1, E2)
            experts2()
            add_ffn("sum_done", 1, 4, 2)
            norm(8, xT[:, :, :], lambda k: xT[:, k, :], VT[:, 2, W_FG:W_FG + 8])
            for a in range(TT):
                dve.wait_ge(sem("outT_ready"), a + 1)
                for half in range(2):
                    ins = V.tensor_copy(hflat[:, a * D + half * 512:a * D + (half + 1) * 512], B[2 * a + half][:, :])
                ins.then_inc(sem("out_tile"), 1)


_INS = [
    "x", "c", "ada_w", "ada_b", "norm_mix_g", "norm_ffn_g", "w_in", "rg_conv_w", "rg_conv_b", "rg_wa", "rg_ba", "rg_wx",
    "rg_bx", "rg_lambda", "gla_wg2", "gla_bg", "gla_norm_g", "w_out", "ffn_w1", "ffn_w3", "ffn_w2", "router_w",
    "moe_w1", "moe_w3", "moe_w2", "final_g", "c_2", "ctx_2", "c_ctx_2", "ada_w_2", "ada_b_2", "norm1_g_2", "w_in_2",
    "lambda_q1_2", "lambda_k1_2", "lambda_q2_2", "lambda_k2_2", "dattn_norm_g_2", "ret_decay_fwd_2",
    "ret_decay_bwd_2", "ret_norm_g_2", "w_out_2", "norm2_g_2", "router_w_2", "router_bias_2", "exp_w1_2",
    "exp_w3_2", "exp_w2_2", "shared_w1_2", "shared_w3_2", "shared_w2_2", "final_norm_g_2",
]


def kernel(**inputs):
    import numpy as _np
    import concourse.bacc as _bacc
    from concourse import mybir as _mybir
    from concourse.bass_utils import run_bass_kernel_spmd as _run

    nc = _bacc.Bacc("TRN2", target_bir_lowering=False, num_devices=1)
    arrays, A = {}, {}
    for name in _INS:
        a = _np.ascontiguousarray(inputs[name])
        if a.ndim == 1 and name == "c_ctx_2":
            a = a.reshape(1, -1)
        arrays[f"in_{name}"] = a
        A[name] = nc.dram_tensor(f"in_{name}", a.shape, F32, kind="ExternalInput").ap()
    A["c_ctx_2"] = A["c_ctx_2"][0]
    extra = {}
    for name, a in zip(("constants", "relative"), constants()):
        arrays[name] = a
        extra[name] = nc.dram_tensor(name, a.shape, F32, kind="ExternalInput").ap()
    out = nc.dram_tensor("out", (1, T, D), F32, kind="ExternalOutput").ap()
    build(nc, A, extra["constants"], extra["relative"], out)
    r = _run(nc, [arrays], core_ids=[0])
    return r.results[0]["out"]
```
